# Optimizing a Trainium2 kernel written in Bass

```python
import jax
import jax.numpy as jnp
from jax import lax
import numpy as np
import math
import jax, jax.numpy as jnp

D_MODEL = 1024
BATCH = 1
SEQ = 512
DEPTH = 1

SB_HEADS = 16
SB_HEAD_DIM = 64
SB_WIDTH = SB_HEADS * SB_HEAD_DIM
RET_HEADS = 4
RET_QK_DIM = 256
RET_V_DIM = 2 * RET_QK_DIM
RET_QK_WIDTH = RET_HEADS * RET_QK_DIM
RET_V_WIDTH = RET_HEADS * RET_V_DIM
N_BRANCH = 2
BLOCK = 128
D_FF = -(-8 * D_MODEL // (3 * 256)) * 256
ROPE_BASE = 10000.0
EPS = 1e-6
N_MOD = 6
IN_SPLITS = (SB_WIDTH, 2 * SB_WIDTH, 3 * SB_WIDTH,
             3 * SB_WIDTH + RET_QK_WIDTH,
             3 * SB_WIDTH + 2 * RET_QK_WIDTH,
             3 * SB_WIDTH + 2 * RET_QK_WIDTH + RET_V_WIDTH,
             3 * SB_WIDTH + 2 * RET_QK_WIDTH + 2 * RET_V_WIDTH)
IN_WIDTH = 3 * SB_WIDTH + 2 * RET_QK_WIDTH + 2 * RET_V_WIDTH + N_BRANCH * D_MODEL


def rmsnorm(t, g):
    tf = t.astype(jnp.float32)
    y = tf * lax.rsqrt(jnp.mean(tf * tf, axis=-1, keepdims=True) + EPS)
    return (y * g.astype(jnp.float32)).astype(t.dtype)

def head_rmsnorm(t):
    tf = t.astype(jnp.float32)
    return (tf * lax.rsqrt(jnp.mean(tf * tf, axis=-1, keepdims=True) + EPS)).astype(t.dtype)

def modulate(h, shift, scale):
    return h * (1.0 + scale[:, None, :]) + shift[:, None, :]

def rotary(t):
    s, d = t.shape[1], t.shape[-1]
    inv_freq = ROPE_BASE ** (-jnp.arange(0, d, 2, dtype=jnp.float32) / d)
    ang = jnp.arange(s, dtype=jnp.float32)[:, None] * inv_freq[None, :]
    cos = jnp.cos(ang)[None, :, None, :]
    sin = jnp.sin(ang)[None, :, None, :]
    t1, t2 = jnp.split(t.astype(jnp.float32), 2, axis=-1)
    return jnp.concatenate([t1 * cos - t2 * sin, t1 * sin + t2 * cos], axis=-1).astype(t.dtype)

def stick_breaking_attention(q, k, v):
    s_len = q.shape[2]
    scale = SB_HEAD_DIM ** -0.5
    outs = []
    for i in range(s_len // BLOCK):
        end = (i + 1) * BLOCK
        qb = q[:, :, i * BLOCK:end]
        kb = k[:, :, :end]
        vb = v[:, :, :end]
        z = jnp.einsum('bhtd,bhsd->bhts', qb, kb).astype(jnp.float32) * scale
        t_pos = i * BLOCK + jnp.arange(BLOCK)
        s_pos = jnp.arange(end)
        mask = s_pos[None, :] < t_pos[:, None]
        log_1m_beta = jnp.where(mask, jax.nn.log_sigmoid(-z), 0.0)
        after = lax.cumsum(log_1m_beta, axis=3, reverse=True) - log_1m_beta
        log_a = jax.nn.log_sigmoid(z) + after
        a = jnp.where(mask, jnp.exp(log_a), 0.0)
        outs.append(jnp.einsum('bhts,bhsd->bhtd', a.astype(v.dtype), vb))
    return jnp.concatenate(outs, axis=2)

def retention(q, k, v):
    out_dtype = v.dtype
    q = q.astype(jnp.float32)
    k = k.astype(jnp.float32)
    v = v.astype(jnp.float32)
    b, h, s_len, dk = q.shape
    dv = v.shape[-1]
    n_chunks = s_len // BLOCK
    log_gamma = jnp.log(1.0 - 2.0 ** (-5.0 - jnp.arange(h, dtype=jnp.float32)))
    idx = jnp.arange(BLOCK, dtype=jnp.float32)
    diff = idx[:, None] - idx[None, :]
    decay_mask = jnp.where(diff >= 0, jnp.exp(jnp.maximum(diff, 0.0) * log_gamma[:, None, None]), 0.0)
    query_decay = jnp.exp((idx + 1.0) * log_gamma[:, None])
    key_decay = jnp.exp((BLOCK - 1.0 - idx) * log_gamma[:, None])
    chunk_decay = jnp.exp(BLOCK * log_gamma)
    qc = q.reshape(b, h, n_chunks, BLOCK, dk)
    kc = k.reshape(b, h, n_chunks, BLOCK, dk)
    vc = v.reshape(b, h, n_chunks, BLOCK, dv)
    scores = jnp.einsum('bhncd,bhnmd->bhncm', qc, kc) * decay_mask[None, :, None]
    intra = jnp.einsum('bhncm,bhnme->bhnce', scores, vc)
    k_dec = kc * key_decay[None, :, None, :, None]

    def step(state, xs):
        q_i, k_i, v_i = xs
        cross = jnp.einsum('bhcd,bhde->bhce', q_i, state) * query_decay[None, :, :, None]
        state = state * chunk_decay[None, :, None, None] + jnp.einsum('bhcd,bhce->bhde', k_i, v_i)
        return state, cross

    xs = (jnp.moveaxis(qc, 2, 0), jnp.moveaxis(k_dec, 2, 0), jnp.moveaxis(vc, 2, 0))
    init = jnp.zeros((b, h, dk, dv), jnp.float32)
    _, cross = lax.scan(step, init, xs)
    out = intra + jnp.moveaxis(cross, 0, 2)
    return out.reshape(b, h, s_len, dv).astype(out_dtype)

def first_inputs(seed: int = 0) -> dict:
    key = jax.random.key(seed)
    ks = jax.random.split(key, 14)

    def nrm(k, shape, fan_in):
        return jax.random.normal(k, shape, jnp.float32) * (fan_in ** -0.5)

    x = jax.random.normal(ks[0], (BATCH, SEQ, D_MODEL), jnp.float32)
    c = jax.random.normal(ks[1], (BATCH, D_MODEL), jnp.float32)
    w_ada = nrm(ks[2], (DEPTH, D_MODEL, N_MOD * D_MODEL), D_MODEL)
    b_ada = 0.02 * jax.random.normal(ks[3], (DEPTH, N_MOD * D_MODEL), jnp.float32)
    g_norm1 = 1.0 + 0.02 * jax.random.normal(ks[4], (DEPTH, D_MODEL), jnp.float32)
    w_in = nrm(ks[5], (DEPTH, D_MODEL, IN_WIDTH), D_MODEL)
    b_branch = 0.02 * jax.random.normal(ks[6], (DEPTH, N_BRANCH * D_MODEL), jnp.float32)
    w_proj_sb = nrm(ks[7], (DEPTH, SB_WIDTH, D_MODEL), SB_WIDTH)
    w_proj_ret = nrm(ks[8], (DEPTH, RET_V_WIDTH, D_MODEL), RET_V_WIDTH)
    w_out = nrm(ks[9], (DEPTH, D_MODEL, D_MODEL), D_MODEL)
    g_norm2 = 1.0 + 0.02 * jax.random.normal(ks[10], (DEPTH, D_MODEL), jnp.float32)
    w_ffn_in = nrm(ks[11], (DEPTH, D_MODEL, 2 * D_FF), D_MODEL)
    w_ffn_out = nrm(ks[12], (DEPTH, D_FF, D_MODEL), D_FF)
    g_final = 1.0 + 0.02 * jax.random.normal(ks[13], (D_MODEL,), jnp.float32)
    return {'x': x, 'c': c, 'w_ada': w_ada, 'b_ada': b_ada, 'g_norm1': g_norm1,
            'w_in': w_in, 'b_branch': b_branch, 'w_proj_sb': w_proj_sb,
            'w_proj_ret': w_proj_ret, 'w_out': w_out, 'g_norm2': g_norm2,
            'w_ffn_in': w_ffn_in, 'w_ffn_out': w_ffn_out, 'g_final': g_final}

def first_block(x, c, w_ada, b_ada, g_norm1, w_in, b_branch, w_proj_sb, w_proj_ret,
              w_out, g_norm2, w_ffn_in, w_ffn_out, g_final):
    b, s_len, _ = x.shape
    c_act = jax.nn.silu(c)
    for l in range(DEPTH):
        mod = jnp.einsum('bd,de->be', c_act, w_ada[l]) + b_ada[l]
        shift1, scale1, gate1, shift2, scale2, gate2 = jnp.split(mod, N_MOD, axis=-1)

        hmix = modulate(rmsnorm(x, g_norm1[l]), shift1, scale1)
        proj = jnp.einsum('bsd,de->bse', hmix, w_in[l])
        sb_q, sb_k, sb_v, r_q, r_k, r_v, r_g, br = jnp.split(proj, IN_SPLITS, axis=-1)

        def sb_heads(t):
            return t.reshape(b, s_len, SB_HEADS, SB_HEAD_DIM).transpose(0, 2, 1, 3)
        o_sb = stick_breaking_attention(sb_heads(sb_q), sb_heads(sb_k), sb_heads(sb_v))
        o_sb = o_sb.transpose(0, 2, 1, 3).reshape(b, s_len, SB_WIDTH)

        rq = rotary(r_q.reshape(b, s_len, RET_HEADS, RET_QK_DIM))
        rk = rotary(r_k.reshape(b, s_len, RET_HEADS, RET_QK_DIM)) * (RET_QK_DIM ** -0.5)
        rv = r_v.reshape(b, s_len, RET_HEADS, RET_V_DIM)
        o_ret = retention(rq.transpose(0, 2, 1, 3), rk.transpose(0, 2, 1, 3), rv.transpose(0, 2, 1, 3))
        o_ret = head_rmsnorm(o_ret.transpose(0, 2, 1, 3)).reshape(b, s_len, RET_V_WIDTH)
        o_ret = jax.nn.silu(r_g) * o_ret

        g_sb, g_ret = jnp.split(jax.nn.sigmoid(br + b_branch[l]), N_BRANCH, axis=-1)
        merged = (g_sb * jnp.einsum('bse,ed->bsd', o_sb, w_proj_sb[l])
                  + g_ret * jnp.einsum('bse,ed->bsd', o_ret, w_proj_ret[l]))
        x = x + gate1[:, None, :] * jnp.einsum('bsd,de->bse', merged, w_out[l])

        hffn = modulate(rmsnorm(x, g_norm2[l]), shift2, scale2)
        a, u = jnp.split(jnp.einsum('bsd,df->bsf', hffn, w_ffn_in[l]), 2, axis=-1)
        x = x + gate2[:, None, :] * jnp.einsum('bsf,fd->bsd', jax.nn.silu(a) * u, w_ffn_out[l])

    return rmsnorm(x, g_final)


MEM_LEN = 256
MIX_WIDTH = D_MODEL
GDN_HEADS = 4
GDN_HEAD_DIM = 128
GDN_WIDTH = GDN_HEADS * GDN_HEAD_DIM
CFM_WIDTH = MIX_WIDTH - GDN_WIDTH
GDN_SHORT_CONV = 4
CHUNK = 64
CFM_KERNEL = 31
XATTN_HEADS = 4
XATTN_HEAD_DIM = D_MODEL // XATTN_HEADS
D_FF_2 = 2816
FFN_CONV = 3
IN_COLS = 4 * GDN_WIDTH + 2 * GDN_HEADS + 2 * CFM_WIDTH


def rmsnorm_2(x, g):
    xf = x.astype(jnp.float32)
    y = xf * lax.rsqrt(jnp.mean(xf * xf, axis=-1, keepdims=True) + EPS)
    return (y * g.astype(jnp.float32)).astype(x.dtype)

def layernorm(x, g, b):
    xf = x.astype(jnp.float32)
    mu = jnp.mean(xf, axis=-1, keepdims=True)
    xc = xf - mu
    var = jnp.mean(xc * xc, axis=-1, keepdims=True)
    return (xc * lax.rsqrt(var + EPS) * g.astype(jnp.float32) + b.astype(jnp.float32)).astype(x.dtype)

def l2norm(x):
    return x * lax.rsqrt(jnp.sum(x * x, axis=-1, keepdims=True) + EPS)

def causal_dwconv(x, w):
    K, C = w.shape
    return lax.conv_general_dilated(
        x, w[:, None, :].astype(x.dtype), window_strides=(1,), padding=[(K - 1, 0)],
        dimension_numbers=("NWC", "WIO", "NWC"), feature_group_count=C)

def gated_delta_rule_chunked(q, k, v, g, beta):
    B, T, H, Dk = q.shape
    Dv = v.shape[-1]
    N = T // CHUNK

    def to_chunks(a):
        a = a.reshape((B, N, CHUNK, H) + a.shape[3:])
        return jnp.moveaxis(a, (1, 3), (0, 2))

    qc = to_chunks(q * (Dk ** -0.5))
    kc = to_chunks(k)
    vc = to_chunks(v)
    bc = to_chunks(beta)
    gc = jnp.cumsum(to_chunks(g), axis=-1)

    idx = jnp.arange(CHUNK)
    causal = idx[:, None] >= idx[None, :]
    strict = idx[:, None] > idx[None, :]
    diff = gc[..., :, None] - gc[..., None, :]
    decay = jnp.where(causal, jnp.exp(jnp.where(causal, diff, 0.0)), 0.0)

    kb = kc * bc[..., None]
    L = jnp.where(strict, jnp.einsum('nbhid,nbhjd->nbhij', kb, kc) * decay, 0.0)
    eye = jnp.eye(CHUNK, dtype=jnp.float32)
    rhs = jnp.concatenate([vc * bc[..., None], kb * jnp.exp(gc)[..., None]], axis=-1)
    sol = lax.linalg.triangular_solve(eye + L, rhs, left_side=True, lower=True, unit_diagonal=True)
    u = sol[..., :Dv]
    w = sol[..., Dv:]
    attn_intra = jnp.einsum('nbhid,nbhjd->nbhij', qc, kc) * decay

    def step(S, inp):
        q_i, k_i, u_i, w_i, g_i, a_i = inp
        v_new = u_i - jnp.einsum('bhcd,bhde->bhce', w_i, S)
        o = (jnp.einsum('bhcd,bhde->bhce', q_i * jnp.exp(g_i)[..., None], S)
             + jnp.einsum('bhij,bhje->bhie', a_i, v_new))
        g_last = g_i[..., -1]
        k_dec = k_i * jnp.exp(g_last[..., None] - g_i)[..., None]
        S = S * jnp.exp(g_last)[..., None, None] + jnp.einsum('bhcd,bhce->bhde', k_dec, v_new)
        return S, o

    S0 = jnp.zeros((B, H, Dk, Dv), jnp.float32)
    _, o = lax.scan(step, S0, (qc, kc, u, w, gc, attn_intra))
    return jnp.moveaxis(o, (0, 2), (1, 3)).reshape(B, T, H, Dv)

def hybrid_mixer(h, w_in, gdn_conv_w, a_log, dt_bias, gdn_norm_g,
                 cfm_dw_w, cfm_dw_b, cfm_ln_g, cfm_ln_b, w_out):
    B, T, _ = h.shape
    z = h @ w_in
    s1 = 3 * GDN_WIDTH
    s2 = 4 * GDN_WIDTH
    s3 = s2 + GDN_HEADS
    s4 = s3 + GDN_HEADS
    qkv, gate, a_logit, b_logit, cfm_in = jnp.split(z, [s1, s2, s3, s4], axis=-1)

    qkv = jax.nn.silu(causal_dwconv(qkv, gdn_conv_w)).astype(jnp.float32)
    q, k, v = jnp.split(qkv, 3, axis=-1)
    shp = (B, T, GDN_HEADS, GDN_HEAD_DIM)
    q = l2norm(q.reshape(shp))
    k = l2norm(k.reshape(shp))
    v = v.reshape(shp)
    g = -jnp.exp(a_log.astype(jnp.float32)) * jax.nn.softplus(
        a_logit.astype(jnp.float32) + dt_bias.astype(jnp.float32))
    beta = jax.nn.sigmoid(b_logit.astype(jnp.float32))
    o = gated_delta_rule_chunked(q, k, v, g, beta)
    o = rmsnorm_2(o, gdn_norm_g) * jax.nn.silu(gate.astype(jnp.float32).reshape(shp))
    o_gdn = o.reshape(B, T, GDN_WIDTH).astype(h.dtype)

    c = jax.nn.glu(cfm_in, axis=-1)
    c = causal_dwconv(c, cfm_dw_w) + cfm_dw_b
    c = jax.nn.silu(layernorm(c, cfm_ln_g, cfm_ln_b))

    return jnp.concatenate([o_gdn, c], axis=-1) @ w_out

def memory_cross_attention(h, mem_n, w_q, w_kv, w_o):
    B, T, _ = h.shape
    M = mem_n.shape[1]
    q = (h @ w_q).reshape(B, T, XATTN_HEADS, XATTN_HEAD_DIM)
    k, v = jnp.split(mem_n @ w_kv, 2, axis=-1)
    k = k.reshape(B, M, XATTN_HEADS, XATTN_HEAD_DIM)
    v = v.reshape(B, M, XATTN_HEADS, XATTN_HEAD_DIM)
    s = jnp.einsum('bthd,bmhd->bhtm', q, k).astype(jnp.float32) * (XATTN_HEAD_DIM ** -0.5)
    p = jax.nn.softmax(s, axis=-1).astype(h.dtype)
    o = jnp.einsum('bhtm,bmhd->bthd', p, v).reshape(B, T, D_MODEL)
    return o @ w_o

def conv_glu_ffn(h, w_up, conv_w, conv_b, w_down):
    u = causal_dwconv(h @ w_up, conv_w) + conv_b
    a, b = jnp.split(u, 2, axis=-1)
    return (jax.nn.silu(a) * b) @ w_down

def second_inputs(seed: int = 0) -> dict:
    key = jax.random.key(seed)
    ks = jax.random.split(key, 24)
    f32 = jnp.float32

    def nrm(k, shape, scale):
        return jax.random.normal(k, shape, f32) * scale

    x = nrm(ks[0], (BATCH, SEQ, D_MODEL), 1.0)
    mem = nrm(ks[1], (BATCH, MEM_LEN, D_MODEL), 1.0)
    norm_g = 1.0 + nrm(ks[2], (DEPTH, 6, D_MODEL), 0.05)
    w_in = nrm(ks[3], (DEPTH, D_MODEL, IN_COLS), D_MODEL ** -0.5)
    gdn_conv_w = nrm(ks[4], (DEPTH, GDN_SHORT_CONV, 3 * GDN_WIDTH), GDN_SHORT_CONV ** -0.5)
    gdn_a_log = jnp.log(jax.random.uniform(ks[5], (DEPTH, GDN_HEADS), f32, 1.0, 16.0))
    dt = jnp.exp(jax.random.uniform(ks[6], (DEPTH, GDN_HEADS), f32,
                                    math.log(1e-3), math.log(1e-1)))
    gdn_dt_bias = dt + jnp.log(-jnp.expm1(-dt))
    gdn_norm_g = 1.0 + nrm(ks[7], (DEPTH, GDN_HEAD_DIM), 0.05)
    cfm_dw_w = nrm(ks[8], (DEPTH, CFM_KERNEL, CFM_WIDTH), CFM_KERNEL ** -0.5)
    cfm_dw_b = nrm(ks[9], (DEPTH, CFM_WIDTH), 0.02)
    cfm_ln_g = 1.0 + nrm(ks[10], (DEPTH, CFM_WIDTH), 0.05)
    cfm_ln_b = nrm(ks[11], (DEPTH, CFM_WIDTH), 0.02)
    w_out = nrm(ks[12], (DEPTH, MIX_WIDTH, D_MODEL), MIX_WIDTH ** -0.5)
    mem_norm_g = 1.0 + nrm(ks[13], (DEPTH, D_MODEL), 0.05)
    xa_w_q = nrm(ks[14], (DEPTH, D_MODEL, D_MODEL), D_MODEL ** -0.5)
    xa_w_kv = nrm(ks[15], (DEPTH, D_MODEL, 2 * D_MODEL), D_MODEL ** -0.5)
    xa_w_o = nrm(ks[16], (DEPTH, D_MODEL, D_MODEL), D_MODEL ** -0.5)
    ffn_w_up = nrm(ks[17], (DEPTH, D_MODEL, 2 * D_FF_2), D_MODEL ** -0.5)
    ffn_conv_w = nrm(ks[18], (DEPTH, FFN_CONV, 2 * D_FF_2), FFN_CONV ** -0.5)
    ffn_conv_b = nrm(ks[19], (DEPTH, 2 * D_FF_2), 0.02)
    ffn_w_down = nrm(ks[20], (DEPTH, D_FF_2, D_MODEL), D_FF_2 ** -0.5)
    return {"x": x, "mem": mem, "norm_g": norm_g, "w_in": w_in, "gdn_conv_w": gdn_conv_w,
            "gdn_a_log": gdn_a_log, "gdn_dt_bias": gdn_dt_bias, "gdn_norm_g": gdn_norm_g,
            "cfm_dw_w": cfm_dw_w, "cfm_dw_b": cfm_dw_b, "cfm_ln_g": cfm_ln_g, "cfm_ln_b": cfm_ln_b,
            "w_out": w_out, "mem_norm_g": mem_norm_g, "xa_w_q": xa_w_q, "xa_w_kv": xa_w_kv,
            "xa_w_o": xa_w_o, "ffn_w_up": ffn_w_up, "ffn_conv_w": ffn_conv_w,
            "ffn_conv_b": ffn_conv_b, "ffn_w_down": ffn_w_down}

def second_block(x, mem, norm_g, w_in, gdn_conv_w, gdn_a_log, gdn_dt_bias, gdn_norm_g,
              cfm_dw_w, cfm_dw_b, cfm_ln_g, cfm_ln_b, w_out, mem_norm_g,
              xa_w_q, xa_w_kv, xa_w_o, ffn_w_up, ffn_conv_w, ffn_conv_b, ffn_w_down):
    h = x
    for l in range(DEPTH):
        g = norm_g[l]
        y = hybrid_mixer(rmsnorm_2(h, g[0]), w_in[l], gdn_conv_w[l], gdn_a_log[l], gdn_dt_bias[l],
                         gdn_norm_g[l], cfm_dw_w[l], cfm_dw_b[l], cfm_ln_g[l], cfm_ln_b[l], w_out[l])
        h = h + rmsnorm_2(y, g[1])
        y = memory_cross_attention(rmsnorm_2(h, g[2]), rmsnorm_2(mem, mem_norm_g[l]),
                                   xa_w_q[l], xa_w_kv[l], xa_w_o[l])
        h = h + rmsnorm_2(y, g[3])
        y = conv_glu_ffn(rmsnorm_2(h, g[4]), ffn_w_up[l], ffn_conv_w[l], ffn_conv_b[l], ffn_w_down[l])
        h = h + rmsnorm_2(y, g[5])
    return h


def setup_inputs(seed=0):
    out = dict(first_inputs(seed))
    for name, value in second_inputs(seed + 1).items():
        if name != "x":
            out[name + "_2"] = value
    return out


def reference(
    x, c, w_ada, b_ada, g_norm1, w_in, b_branch, w_proj_sb, w_proj_ret, w_out, g_norm2,
    w_ffn_in, w_ffn_out, g_final, mem_2, norm_g_2, w_in_2, gdn_conv_w_2, gdn_a_log_2,
    gdn_dt_bias_2, gdn_norm_g_2, cfm_dw_w_2, cfm_dw_b_2, cfm_ln_g_2, cfm_ln_b_2, w_out_2,
    mem_norm_g_2, xa_w_q_2, xa_w_kv_2, xa_w_o_2, ffn_w_up_2, ffn_conv_w_2, ffn_conv_b_2,
    ffn_w_down_2,
):
    x = first_block(
        x, c, w_ada, b_ada, g_norm1, w_in, b_branch, w_proj_sb, w_proj_ret, w_out, g_norm2,
        w_ffn_in, w_ffn_out, g_final,
    )
    return second_block(
        x, mem_2, norm_g_2, w_in_2, gdn_conv_w_2, gdn_a_log_2, gdn_dt_bias_2, gdn_norm_g_2,
        cfm_dw_w_2, cfm_dw_b_2, cfm_ln_g_2, cfm_ln_b_2, w_out_2, mem_norm_g_2, xa_w_q_2,
        xa_w_kv_2, xa_w_o_2, ffn_w_up_2, ffn_conv_w_2, ffn_conv_b_2, ffn_w_down_2,
    )


_drawn_inputs = setup_inputs


def setup_inputs(seed=0):
    import zlib

    import numpy as np

    out = dict(_drawn_inputs(seed))
    spreads = {}
    factors = {'g_norm1': 3.233,
     'b_branch': 8.0,
     'g_norm2': 3.221,
     'cfm_ln_b_2': 4.643,
     'ffn_conv_b_2': 3.966,
     'cfm_dw_b_2': 2.728}
    for name, (base, spread) in spreads.items():
        noise = np.random.default_rng([zlib.crc32(name.encode()), seed]).standard_normal(out[name].shape)
        drawn = base * np.exp(spread * noise) if base else spread * noise
        out[name] = jnp.asarray(drawn.astype(out[name].dtype))
    for name, factor in factors.items():
        out[name] = (out[name] * factor).astype(out[name].dtype)
    return out
```

```python
from contextlib import ExitStack, contextmanager

import numpy as np

import concourse.bass as bass
from concourse import mybir

F32 = mybir.dt.float32
F32R = mybir.dt.float32r
BF16 = mybir.dt.bfloat16
ALU = mybir.AluOpType
ACT = mybir.ActivationFunctionType
AX = mybir.AxisListType

P = 128
D = 1024
KT = D // P
T = 512
NB = T // P
EPS = 1e-6
UNIT = 1024
RING = 4
AHEAD = RING - 1

SB_DIM = 64
PAIRS = 8
RET_H = 4
RET_QT = 2
RET_VT = 4
D_FF = 2816
FT = D_FF // P
N_MOD = 6
NEG = -1e30

MEM = 256
GDN_H = 4
CONV_G = 4
CONV_C = 31
CONV_F = 3
XH = 4
CFM_T = 4
CFM_DVE = 2
X_MIX = 32

TRI_AT = (0, 512, 1024, 896)
TRI_W = tuple(T - P * j for j in range(NB))
TRI = sum(TRI_W)
TRI_ORDER = (0, 1, 3, 2)


class At:

    def __init__(self, c, i=None, m=0):
        self.c, self.i, self.m = c, i, m

    def __add__(self, k):
        return At(self.c + k, self.i, self.m)

    def val(self):
        return self.c if self.i is None else self.i * self.m + self.c

    def slot(self, n):
        assert self.m % n == 0
        return self.c % n

    def div(self, n):
        assert self.m % n == 0
        return At(self.c // n, self.i, self.m // n)


class Count:

    def __init__(self, eng, sem):
        self.eng, self.sem, self.at = eng, sem, At(0)

    def own(self, ins):
        ins.then_inc(self.sem, 1)
        self.at = self.at + 1
        self.eng.wait_ge(self.sem, self.at.val())

    def next(self, n=1):
        self.at = self.at + n
        self.eng.wait_ge(self.sem, self.at.val())

    def skip(self, n=1):
        self.at = self.at + n


@contextmanager
def loop(eng, n, counts):
    start = [c.at.c for c, _ in counts]
    with eng.Fori(0, n) as i:
        for (c, per), s in zip(counts, start):
            c.at = At(s, i, per)
        yield i
        for (c, per), s in zip(counts, start):
            assert c.at.c == s + per, (str(c.sem), c.at.c - s, per)
    for (c, per), s in zip(counts, start):
        c.at = At(s + n * per)


PHASES = [
    ("sb_v", 8), ("sb_qk", 16), ("sb_out", 16), ("ret", 64), ("merge", 8), ("out", 8),
    ("ff_in", 44), ("ff_out", 24),
    ("gdn_in", 28), ("mix_out", 8), ("kv", 16), ("xq", 8), ("xo", 8), ("up", 44), ("down", 24),
]
TILES = [
    ("first", 188), ("gdn_in", 25), ("turn", 4), ("mix_out", 8), ("kv", 8), ("xq", 8), ("x_val", 8), ("xo", 8),
    ("up", 44), ("down", 8),
]
AB, KVQ, GATE, CFM = 0, 1, 13, 17
LEVELS = 7
COLS = [
    ("c", 8), ("b_ada", 48), ("g_norm1", 8), ("b_branch", 16), ("g_norm2", 8), ("g_final", 8),
    ("norm_g", 48), ("mem_g", 8), ("gdn_conv", 3 * GDN_H * CONV_G), ("cfm_conv", CFM_T * CONV_C), ("cfm_b", CFM_T),
    ("ln_g", CFM_T), ("ln_b", CFM_T), ("gdn_g", 1), ("a_log", 1), ("dt_bias", 1),
    ("ff_conv", 2 * FT * CONV_F), ("ff_conv_b", 2 * FT),
]


def starts(table):
    out, at = {}, 0
    for name, n in table:
        out[name] = at
        at += n
    return out, at


U0, N_UNITS = starts(PHASES)
T0, _ = starts(TILES)
C0, N_COLS = starts(COLS)
TABLES = [("angles", 2 * T), ("decay", RET_H * T)]
SMALL = [("ones", P), ("ident", P), ("neg_tri", P), ("keep", P), ("tri", P)]
TB0, N_TABLE = starts(TABLES)
SM0, N_SMALL = starts(SMALL)


def shape_tables():
    f = np.float32
    qk = RET_QT * P
    inv = (f(10000.0) ** (-np.arange(0, qk, 2, dtype=f) / f(qk))).astype(f)
    ang = inv[:, None] * np.arange(T, dtype=f)[None, :]
    gamma = np.log(f(1.0) - f(2.0) ** (f(-5.0) - np.arange(RET_H, dtype=f))).astype(f)
    diff = (np.arange(T)[None, :] - np.arange(P)[:, None]).astype(f)
    decay = [np.where(diff >= 0, np.exp(np.maximum(diff, 0) * g), 0) * f(qk ** -0.5) for g in gamma]
    big = np.concatenate([np.cos(ang), np.sin(ang)] + decay, axis=1).astype(f)
    s, t = np.arange(P)[:, None], np.arange(P)[None, :]
    small = np.concatenate([
        np.ones((P, P)), s == t,
        -(s >= t).astype(f),
        (s < t).astype(f),
        (s <= t).astype(f),
    ], axis=1).astype(f)
    b = [s >> l for l in range(LEVELS)], [t >> l for l in range(LEVELS)]
    halves = np.concatenate([(ti % 2 == 1) & (si == ti - 1) for si, ti in zip(*b)], axis=1)
    return big, small, halves.astype(mybir.dt.np(BF16))


def build_program(nc, dram):
    ctx = ExitStack()
    with ctx:
        kib = 1024
        base = nc.sbuf_base
        at = [(base + 31) // 32 * 32]

        def put(name, shape, dt=F32, where=None):
            size = int(np.prod(shape[1:])) * (2 if dt == BF16 else 4)
            size = (size + 31) // 32 * 32
            offset = at[0] if where is None else where
            if where is None:
                at[0] += size
            return nc.alloc_sbuf_tensor_at(name, list(shape), dt, offset=offset), offset + size

        def fixed(name, shape, dt=F32):
            return put(name, shape, dt)[0]

        raw = [fixed(f"raw{s}", (P, UNIT)) for s in range(RING)]
        w_hi = [fixed(f"w_hi{s}", (P, UNIT), F32R) for s in range(RING)]
        w_lo = [fixed(f"w_lo{s}", (P, UNIT), F32R) for s in range(RING)]
        resid = fixed("resid", (P, KT, T))
        over_x = [at[0]]
        x_hi = fixed("x_hi", (P, KT, T), F32R)
        x_lo = fixed("x_lo", (P, KT, T), F32R)
        cols = fixed("cols", (P, N_COLS))
        small = fixed("small", (P, N_SMALL))
        mod = fixed("mod", (P, N_MOD * KT))
        gain1 = fixed("gain1", (P, KT))
        gain2 = fixed("gain2", (P, KT))
        c_act = fixed("c_act", (P, KT))
        eps = fixed("eps", (P, 1))
        negtri_r = fixed("negtri_r", (P, P), F32R)
        negone_r = fixed("negone_r", (P, P), F32R)
        ident_b = fixed("ident_b", (P, P), BF16)
        causal_b = fixed("causal_b", (P, P), BF16)
        halves = fixed("halves", (P, LEVELS, P), BF16)
        mask_b = fixed("mask_b", (P, P), BF16)
        rs = fixed("rs", (P, T))
        sqacc = fixed("sqacc", (P, T))
        sqt = fixed("sqt", (P, T))
        tn = fixed("tn", (P, 2, T))
        over = at[0]

        def overlay(start, *specs):
            out, o = [], start
            for name, shape, dt in specs:
                t, o = put(name, shape, dt, where=o)
                out.append(t)
            assert o <= nc.sbuf_usable_end, (specs, o - nc.sbuf_usable_end)
            return out, o

        gate_t = tn
        (ada0, adac0), _ = overlay(over, ("ada0", (P, 4, UNIT), F32), ("adac0", (P, UNIT), F32))
        qt, kt_ = sqacc, sqt
        vp = rs[:].rearrange("p (b n) -> p b n", b=NB)
        (osb_hi, osb_lo, v_sb, *pairbufs), _ = overlay(
            over, ("osb_hi", (P, PAIRS, T), F32R), ("osb_lo", (P, PAIRS, T), F32R),
            ("v_sb", (P, NB, D), F32),
            *[(f"{n}{h}", (P, TRI), d) for h in range(2)
              for n, d in (("sp", F32), ("sp_hi", F32R), ("sp_lo", F32R), ("prob", F32))])
        sp, sp_hi, sp_lo, prob = [pairbufs[n::4] for n in range(4)]
        o1 = over + 2 * PAIRS * T * 4
        (rq, rk, rv, rsc, oraw, decay), o2 = overlay(
            over, ("rq", (P, RET_QT, T), F32), ("rk", (P, RET_QT, T), F32), ("rv", (P, NB, T), F32),
            ("rsc", (P, TRI), F32), ("oraw", (P, RET_VT, T), F32),
            ("decay", (P, T), F32))
        assert o2 <= o1
        (msb, pret), o2 = overlay(o1, ("msb", (P, KT, T), F32), ("pret", (P, KT, T), F32))
        (orh, orl, angles, adac, ada1), _ = overlay(
            o2, ("orh", (P, RET_VT, T), F32R), ("orl", (P, RET_VT, T), F32R),
            ("angles", (P, 2 * T), F32), ("adac", (P, UNIT), F32), ("ada1", (P, UNIT), F32))
        cos, sin = angles[:, 0:T], angles[:, T:2 * T]
        (m_hi,), _ = overlay(over, ("m_hi", (P, KT, T), F32R))
        (m_lo, mt), _ = overlay(o2, ("m_lo", (P, KT, T), F32R), ("mt", (P, 2, T), F32))
        (ht, h_hi, h_lo), _ = overlay(
            over, ("ht", (P, 2, T), F32), ("h_hi", (P, FT, T), F32R), ("h_lo", (P, FT, T), F32R))

        (qkvf, sgate, cfin, cfy, gb, gbt, egr, kb, kdec, vb), o3 = overlay(
            over, ("qkvf", (P, 12, T), F32), ("sgate", (P, GDN_H, T), F32), ("cfin", (P, CFM_T, T + CONV_C - 1), F32),
            ("cfy", (P, CFM_T, T), F32), ("gb", (P, T), F32), ("gbt", (P, NB, 64), F32), ("egr", (P, GDN_H, T), F32),
            ("kb", (P, GDN_H * T), F32), ("kdec", (P, GDN_H * T), F32), ("vb", (P, GDN_H * T), F32))
        (solve, gcols), _ = overlay(o3, ("solve", (P, 4, T), F32), ("gcols", (P, 5, 16), F32))
        kf, vf, qf = qkvf[:, 0:4, :], qkvf[:, 4:8, :], qkvf[:, 8:12, :]
        (cin, abx), _ = overlay(o3, ("cin", (P, 2, T + CONV_G - 1), F32), ("abx", (P, T), F32))
        ngc, egc, bg, nega, egl = [gcols[:, n, :] for n in range(5)]
        abt = sgate[:, 0, :]
        cftmp = tn[:, 0, :]
        x_at = over_x[0]
        (bt, xm, xt, dect), _ = overlay(x_at, *[(n, (P, NB, T), F32) for n in ("bt", "xm", "xt", "dect")])
        (memf, mem_hi, mem_lo, yv, kmt, vm, qx, px, pxt, xcols), _ = overlay(
            over, ("memf", (P, KT, MEM), F32), ("mem_hi", (P, KT, MEM), F32R), ("mem_lo", (P, KT, MEM), F32R),
            ("yv", (P, KT, T), F32), ("kmt", (P, KT, MEM), F32), ("vm", (P, 2, D), F32), ("qx", (P, KT, T), F32),
            ("px", (P, 2, NB, MEM), F32), ("pxt", (P, 2, 2 * T), F32), ("xcols", (P, 2, 3, NB), F32))
        (xo_hi, xo_lo, yv_o), _ = overlay(over, ("xo_hi", (P, KT, T), F32R), ("xo_lo", (P, KT, T), F32R),
                                          ("yv_o", (P, KT, T), F32))
        msq = qx[:, 0:4, :].rearrange("p k n -> p (k n)")
        mroot = px[:, 0, 0, :]
        ht2 = sqt
        (g_hi, g_lo, fin), _ = overlay(
            over, ("g_hi", (P, FT, T), F32R), ("g_lo", (P, FT, T), F32R),
            ("fin", (P, 2, T + CONV_F - 1), F32))
        (yv2,), _ = overlay(x_at, ("yv2", (P, KT, T), F32))

        acc = ctx.enter_context(nc.psum_tensor("acc", [P, 2 * T], F32))
        aux = ctx.enter_context(nc.psum_tensor("aux", [P, 6 * T], F32))

        def bank(t):
            b = t.slot(2)
            return acc[:, b * T:(b + 1) * T]

        def sem(name):
            return ctx.enter_context(nc.semaphore(name))

        raw_loaded = [sem(f"raw_loaded{s}") for s in range(RING)]
        hi_ready, lo_ready, unit_used = sem("hi_ready"), sem("lo_ready"), sem("unit_used")
        acc_free = [sem("acc_free0"), sem("acc_free1")]
        S = {n: sem(n) for n in (
            "dve_step", "act_step", "pool_step",
            "decay_free", "decay_loaded", "consts_loaded", "x_loaded", "tables_loaded", "consts_ready", "stored",
            "ada0_loaded0", "ada0_loaded1", "ada0_loaded2", "ada0_loaded3", "ada1_loaded", "ada_used",
            "ada_ready", "mod_ready", "c_ready_act",
            "sq_ready", "stat_ready", "root_ready", "normed", "norm_hi", "x_ready",
            "v_ready", "z_ready", "log_ready", "sp_ready", "sp_hi_ready", "sp_split",
            "log_a_ready", "prob_ready", "qk_ready", "vp_ready", "tile_done", "osb_hi_ready", "osb_ready",
            "gate_ready", "msb_ready", "qk_rot", "rv_ready", "rsc_done", "rsc_ready", "oraw_ready",
            "oprod_ready", "orh_ready", "or_ready", "merged_f", "merged_hi", "merged",
            "resid_ready", "hidden_f", "hidden_hi", "hidden",
            "mem_loaded", "nega_ready", "ab_ready", "gb_ready", "gb_turned", "gbt_ready", "gc_done", "egc_ready", "gc_seen",
            "cin_ready", "conv_ready", "kvq_ready", "gsq_ready", "gstat_done", "groot_ready", "k_normed", "q_normed",
            "sgate_ready", "cfin_ready", "gc_row", "egr_ready", "gc_masked", "dec_ready", "beta_row", "kb_ready",
            "kk_done", "xt_ready", "x_turned", "x_first", "kv_turned", "kv_token", "bm_ready", "zz_done", "zs_ready",
            "xz_done", "x_upd", "qk_done", "at_ready", "wt_done", "nwt_ready", "vnew_done", "vnew_ready", "o_done",
            "o_ready", "s_done", "s_ready", "qe_ready", "cf_pool", "cf_dve", "cfsum_done", "cfc_ready", "cfsq_ready",
            "cfvar_done", "cfn_ready", "osq_ready", "ostat_done", "on_ready", "gdn_over",
            "memsq_ready", "memstat_done", "memroot_ready", "memn_ready", "mem_hi_ready", "mem_ready",
            "km_ready", "vm_ready", "qx_ready", "xs_done", "xmax_ready", "px_ready", "pxn_ready", "px_turned",
            "pxt_ready", "xo_hi_ready", "xo_ready", "fin_ready", "conv2_ready", "silu2_ready", "down_hi",
        )}

        NU = N_UNITS
        block = ctx.enter_context(nc.Block())

        @block.sync
        def _(sp_):
            def load(u):
                s = u.slot(RING)
                if u.i is not None or u.c >= RING:
                    sp_.wait_ge(lo_ready, (u + (1 - RING)).val())
                if u.i is None:
                    src = dram["weights"][u.c]
                else:
                    src = dram["weights"][bass.ds(u.val(), 1), :, :].rearrange("a p n -> (a p) n")
                sp_.dma_start(raw[s][:], src).then_inc(raw_loaded[s], 16)

            sp_.dma_start(cols[:], dram["cols"]).then_inc(S["consts_loaded"], 16)
            sp_.dma_start(small[:], dram["small"]).then_inc(S["consts_loaded"], 16)
            sp_.dma_start(halves[:], dram["halves"]).then_inc(S["consts_loaded"], 16)
            for n in range(16):
                if n >= 4:
                    sp_.wait_ge(S["ada_used"], n - 3)
                sp_.dma_start(ada0[:, n % 4, :], dram["ada"][n]).then_inc(S[f"ada0_loaded{n % 4}"], 16)
                if n == 1:
                    sp_.dma_start(resid[:], dram["x"]).then_inc(S["x_loaded"], 16)
            for u in range(RING):
                load(At(u))
            def load_units(first, end):
                with sp_.Fori(0, (end - first) // 4) as i:
                    for j in range(4):
                        load(At(first + j, i, 4))

            load_units(RING, U0["sb_out"] + 4)
            sp_.wait_ge(S["osb_ready"], PAIRS)
            sp_.dma_start(angles[:], dram["tables"][:, 0:2 * T]).then_inc(S["tables_loaded"], 16)
            load_units(U0["sb_out"] + 4, U0["ret"])
            with sp_.Fori(0, RET_H) as i:
                for j in range(16):
                    if j % 2 == 0:
                        n = At(16 + j // 2, i, 8)
                        sp_.wait_ge(S["ada_used"], n.val())
                        sp_.dma_start(ada1[:], dram["ada"][bass.ds(n.val(), 1), :, :]
                                      .rearrange("a p n -> (a p) n")).then_inc(S["ada1_loaded"], 16)
                    load(At(U0["ret"] + j, i, 16))
                    if j == 3:
                        sp_.wait_ge(S["decay_free"], i + 1)
                        sp_.dma_start(decay[:], dram["tables"][:, bass.ds(i * T + 2 * T, T)]
                                      ).then_inc(S["decay_loaded"], 16)
            rest = U0["ret"] + 64
            load_units(rest, U0["mix_out"] + 4)
            sp_.wait_ge(S["gdn_over"], 1)
            sp_.wait_ge(S["x_ready"], X_MIX)
            sp_.dma_start(memf[:], dram["mem"]).then_inc(S["mem_loaded"], 16)
            load_units(U0["mix_out"] + 4, NU)
            for k in range(KT):
                sp_.wait_ge(S["resid_ready"], k + 1)
                sp_.dma_start(dram["out"][:, k, :], resid[:, k, :]).then_inc(S["stored"], 16)
            sp_.wait_ge(S["stored"], 16 * KT)

        @block.gpsimd
        def _(pool):
            step = Count(pool, S["pool_step"])
            pool.wait_ge(S["x_loaded"], 16)
            step.own(nc.gpsimd.tensor_tensor(sqacc[:], resid[:, 0, :], resid[:, 0, :], ALU.mult))
            for k in range(1, KT):
                step.own(nc.gpsimd.tensor_tensor(sqt[:], resid[:, k, :], resid[:, k, :], ALU.mult))
                if k < KT - 1:
                    step.own(nc.gpsimd.tensor_tensor(sqacc[:], sqacc[:], sqt[:], ALU.add))
            nc.gpsimd.tensor_tensor(sqacc[:], sqacc[:], sqt[:], ALU.add).then_inc(S["sq_ready"], 1)

            def split_lo(u):
                s = u.slot(RING)
                pool.wait_ge(hi_ready, (u + 1).val())
                nc.gpsimd.tensor_tensor(w_lo[s][:], raw[s][:], w_hi[s][:].bitcast(F32),
                                        ALU.subtract).then_inc(lo_ready, 1)

            def split_units(first, end):
                with pool.Fori(0, (end - first) // RING) as i:
                    for j in range(RING):
                        split_lo(At(first + j, i, RING))

            split_units(0, U0["mix_out"])
            for n in range(CFM_DVE, CFM_T):
                pool.wait_ge(S["cfin_ready"], n + 1)
                for j in range(CONV_C):
                    w = cols[:, C0["cfm_conv"] + n * CONV_C + j:C0["cfm_conv"] + n * CONV_C + j + 1]
                    b = cols[:, C0["cfm_b"] + n:C0["cfm_b"] + n + 1]
                    if j == 0:
                        step.own(nc.gpsimd.tensor_scalar(cfy[:, n, :], cfin[:, n, j:j + T], w, b, ALU.mult, ALU.add))
                        continue
                    step.own(nc.gpsimd.tensor_scalar(cftmp, cfin[:, n, j:j + T], w, None, ALU.mult))
                    step.own(nc.gpsimd.tensor_tensor(cfy[:, n, :], cfy[:, n, :], cftmp, ALU.add))
            pool.sem_inc(S["cf_pool"], 1)
            split_units(U0["mix_out"], NU)

        @block.scalar
        def _(act):
            step = Count(act, S["act_step"])
            own = {n: Count(act, S[n]) for n in S}

            def f(out, in_, func=ACT.Copy, **kw):
                return nc.scalar.activation(out, in_, func, **kw)

            def split_hi(u):
                if u.i is None and u.c >= NU:
                    return
                s = u.slot(RING)
                act.wait_ge(raw_loaded[s], (u.div(RING).val() + 1) * 16)
                if u.i is not None or u.c >= RING:
                    act.wait_ge(unit_used, (u + (1 - RING)).val())
                f(w_hi[s][:], raw[s][:]).then_inc(hi_ready, 1)

            def root(scale):
                own["stat_ready"].next()
                own["root_ready"].own(f(rs[:], aux[:, 5 * T:6 * T], ACT.Sqrt, scale=scale, bias=eps[:, 0:1]))

            def norm_hi():
                for k in range(KT):
                    own["normed"].next()
                    own["norm_hi"].own(f(x_hi[:, k, :], tn[:, k % 2, :]))

            act.wait_ge(S["consts_loaded"], 48)
            own["c_ready_act"].own(f(c_act[:], cols[:, C0["c"]:C0["c"] + KT], ACT.Silu))
            own["consts_ready"].next(6)
            root(1.0 / D)
            for u in range(AHEAD):
                split_hi(At(u))
            norm_hi()

            for half in range(2):
                for j in range(4):
                    split_hi(At(4 * half + j + AHEAD))
                act.wait_ge(unit_used, 4 * half + 4)
                for b in range(NB):
                    bk = (4 * half + b) % 6
                    own["v_ready"].own(f(v_sb[:, b, half * T:(half + 1) * T], aux[:, bk * T:(bk + 1) * T]))

            nc.scalar.preload_act_table_set("natural_log_exp_and_others")
            u, t = At(U0["sb_qk"]), At(0)

            def qk_tile(u, t, dst, scale):
                split_hi(u + AHEAD)
                act.wait_ge(unit_used, (u + 1).val())
                own["qk_ready"].own(f(dst[:], bank(t), scale=scale))
                nc.scalar.sem_inc(acc_free[t.slot(2)], 1)

            SC = SB_DIM ** -0.5
            qk_tile(u, At(0), qt, SC)
            qk_tile(u + 1, At(1), kt_, 1.0)

            def pair(u, t, first, last, p):
                for h in range(2):
                    own["z_ready"].next()
                    step.own(f(sp[h][:], aux[:, 3 * T * h:3 * T * h + TRI], ACT.Abs))
                    step.own(f(sp[h][:], sp[h][:], ACT.Exp, scale=-1.0))
                    own["log_ready"].own(f(sp[h][:], sp[h][:], ACT.Ln, bias=1.0))
                for h in range(2):
                    own["sp_ready"].next()
                    own["sp_hi_ready"].own(f(sp_hi[h][:], sp[h][:]))
                if not first:
                    own["tile_done"].next()
                    own["osb_hi_ready"].own(f(osb_hi[:, p - 1, :] if t.i is None else
                                              osb_hi[:, bass.ds(p - 1, 1), :].rearrange("p a n -> p (a n)"), bank(t)))
                    t = t + 1
                if not last:
                    qk_tile(u, t, qt, SC)
                own["log_a_ready"].next()
                own["prob_ready"].own(f(prob[0][:], aux[:, 0:TRI], ACT.Exp))
                if not last:
                    qk_tile(u + 1, t + 1, kt_, 1.0)
                own["log_a_ready"].next()
                own["prob_ready"].own(f(prob[1][:], aux[:, 3 * T:3 * T + TRI], ACT.Exp))

            pair(u + 2, At(2), True, False, 0)
            with loop(act, 3, [(step, 8), (own["z_ready"], 4), (own["log_ready"], 4), (own["sp_ready"], 4),
                               (own["sp_hi_ready"], 4), (own["tile_done"], 2), (own["osb_hi_ready"], 2),
                               (own["log_a_ready"], 4), (own["prob_ready"], 4), (own["qk_ready"], 4)]) as i:
                for s in range(2):
                    pair(At(U0["sb_qk"] + 4 + 2 * s, i, 4), At(4 + 3 * s, i, 6), False, False, i * 2 + 1 + s)
            pair(None, At(22), False, True, 7)
            own["tile_done"].next()
            own["osb_hi_ready"].own(f(osb_hi[:, PAIRS - 1, :], bank(At(23))))

            with loop(act, 4, [(own["gate_ready"], 2)]) as i:
                for n in range(2):
                    u, t = At(U0["sb_out"] + 2 * n, i, 4), At(2 * n, i, 4)
                    split_hi(u + AHEAD)
                    act.wait_ge(unit_used, (u + 1).val())
                    own["gate_ready"].own(f(gate_t[:, n, :], bank(t), ACT.Sigmoid,
                                            bias=cols[:, bass.ds(i * 2 + (C0["b_branch"] + n), 1)]))
                    nc.scalar.sem_inc(acc_free[t.slot(2)], 1)
                    split_hi(u + 1 + AHEAD)

            with loop(act, RET_H, [(own["rv_ready"], 4), (own["tile_done"], 8), (own["oraw_ready"], 4),
                                   (own["stat_ready"], 1), (own["root_ready"], 1), (own["gate_ready"], 4),
                                   (own["oprod_ready"], 4), (own["orh_ready"], 4)]) as i:
                u0 = At(U0["ret"], i, 16)
                for j in range(8):
                    split_hi(u0 + j + AHEAD)
                act.wait_ge(unit_used, (u0 + 8).val())
                for b in range(NB):
                    own["rv_ready"].own(f(rv[:, b, :], aux[:, (2 + b) * T:(3 + b) * T]))
                for e in range(RET_VT):
                    own["tile_done"].next()
                    own["oraw_ready"].own(f(oraw[:, e, :], bank(At(e))))
                    nc.scalar.sem_inc(acc_free[e % 2], 1)
                root(1.0 / (RET_VT * P))
                for e in range(RET_VT):
                    u = u0 + 8 + e
                    split_hi(u + AHEAD)
                    act.wait_ge(unit_used, (u + 1).val())
                    own["gate_ready"].own(f(gate_t[:, e % 2, :], bank(At(e)), ACT.Silu))
                    nc.scalar.sem_inc(acc_free[e % 2], 1)
                    own["oprod_ready"].next()
                    own["orh_ready"].own(f(orh[:, e, :], oraw[:, e, :]))
                own["tile_done"].skip(4)
                for j in range(4):
                    split_hi(u0 + 12 + j + AHEAD)

            with loop(act, 2, [(own["gate_ready"], 4), (own["merged_f"], 4), (own["merged_hi"], 4)]) as i:
                for n in range(4):
                    u = At(U0["merge"] + n, i, 4)
                    split_hi(u + AHEAD)
                    act.wait_ge(unit_used, (u + 1).val())
                    own["gate_ready"].own(f(gate_t[:, n % 2, :], bank(At(n)), ACT.Sigmoid,
                                            bias=cols[:, bass.ds(i * 4 + (C0["b_branch"] + KT + n), 1)]))
                    nc.scalar.sem_inc(acc_free[n % 2], 1)
                    own["merged_f"].next()
                    own["merged_hi"].own(f(m_hi[:, bass.ds(i * 4 + n, 1), :].rearrange("p a n -> p (a n)"),
                                           mt[:, n % 2, :]))
            with act.Fori(0, 2) as i:
                for n in range(4):
                    split_hi(At(U0["out"] + n + AHEAD, i, 4))
            root(1.0 / D)
            norm_hi()

            with loop(act, FT // 2, [(own["gate_ready"], 2), (own["hidden_f"], 2), (own["hidden_hi"], 2)]) as i:
                for n in range(2):
                    u, t = At(U0["ff_in"] + 2 * n, i, 4), At(2 * n)
                    split_hi(u + AHEAD)
                    act.wait_ge(unit_used, (u + 1).val())
                    own["gate_ready"].own(f(gate_t[:, n, :], bank(t), ACT.Silu))
                    nc.scalar.sem_inc(acc_free[t.slot(2)], 1)
                    split_hi(u + 1 + AHEAD)
                    own["hidden_f"].next()
                    own["hidden_hi"].own(f(h_hi[:, bass.ds(i * 2 + n, 1), :].rearrange("p a n -> p (a n)"),
                                           ht[:, n, :]))
            for u in range(U0["ff_out"], U0["ff_out"] + 24):
                split_hi(At(u + AHEAD))
            root(1.0 / D)
            root(1.0 / D)
            own["nega_ready"].own(f(nega[0:GDN_H, 0:1], cols[0:GDN_H, C0["a_log"]:C0["a_log"] + 1], ACT.Exp))
            norm_hi()
            g0, t0 = At(U0["gdn_in"]), At(T0["gdn_in"])

            def free(t):
                nc.scalar.sem_inc(acc_free[t.slot(2)], 1)

            split_hi(g0 + AHEAD)
            act.wait_ge(unit_used, (g0 + 1).val())
            dt = cols[0:GDN_H, C0["dt_bias"]:C0["dt_bias"] + 1]
            step.own(f(gb[32:32 + GDN_H, :], bank(t0)[32:32 + GDN_H, :], ACT.Sigmoid))
            step.own(f(abx[0:GDN_H, :], bank(t0)[0:GDN_H, :], ACT.Identity, bias=dt))
            step.own(f(abt[0:GDN_H, :], bank(t0)[0:GDN_H, :], ACT.Abs, bias=dt))
            free(t0)
            step.own(f(abt[0:GDN_H, :], abt[0:GDN_H, :], ACT.Exp, scale=-1.0))
            own["ab_ready"].own(f(abt[0:GDN_H, :], abt[0:GDN_H, :], ACT.Ln, bias=1.0))

            with loop(act, 3, [(own["cin_ready"], 4), (own["conv_ready"], 4), (own["kvq_ready"], 4)]) as i:
                for n in range(4):
                    u, t = At(U0["gdn_in"] + KVQ + n, i, 4), At(T0["gdn_in"] + KVQ + n, i, 4)
                    split_hi(u + AHEAD)
                    act.wait_ge(unit_used, (u + 1).val())
                    own["cin_ready"].own(f(cin[:, n % 2, CONV_G - 1:], bank(t)))
                    free(t)
                    own["conv_ready"].next()
                    own["kvq_ready"].own(f(qkvf[:, bass.ds(i * 4 + n, 1), :].rearrange("p a n -> p (a n)"),
                                           tn[:, n % 2, :], ACT.Silu))

            def flat(x):
                return x.rearrange("p k n -> p (k n)")

            own["gsq_ready"].own(f(kdec[:], flat(kf), ACT.Square))
            own["gsq_ready"].own(f(vb[:], flat(qf), ACT.Square))
            for n in range(GDN_H):
                u, t = g0 + GATE + n, t0 + GATE + n
                split_hi(u + AHEAD)
                act.wait_ge(unit_used, (u + 1).val())
                own["sgate_ready"].own(f(sgate[:, n, :], bank(t), ACT.Silu))
                free(t)

            def l2_root(dst):
                own["gstat_done"].next()
                own["groot_ready"].own(f(dst[:], aux[:, 0:4 * T], ACT.Sqrt, bias=eps[:, 0:1]))

            def cfm_gate(n):
                u, t = g0 + CFM + 2 * n, t0 + CFM + 2 * n
                split_hi(u + AHEAD)
                act.wait_ge(unit_used, (u + 1).val())
                own["gate_ready"].own(f(gate_t[:, n % 2, :], bank(t), ACT.Sigmoid))
                free(t)
                split_hi(u + 1 + AHEAD)

            l2_root(kdec)
            cfm_gate(0)
            cfm_gate(1)
            l2_root(vb)
            own["gc_done"].next()
            own["egc_ready"].own(f(egc[:], aux[:, 5 * T:5 * T + 16], ACT.Exp))
            cfm_gate(2)
            cfm_gate(3)
            for j in range(25, 28):
                split_hi(g0 + j + AHEAD)

            def rows(c):
                b = 3 * (c % 2)
                own["gc_row"].next()
                own["egr_ready"].own(f(egr[:, :, c * P:(c + 1) * P],
                                       aux[:, b * T:(b + 1) * T].rearrange("p (h n) -> p h n", h=GDN_H), ACT.Exp))

            def decays(c):
                b = 3 * (c % 2)
                own["gc_masked"].next()
                for h in range(GDN_H):
                    ins = f(dect[:, c, h * P:(h + 1) * P], aux[:, b * T + h * P:b * T + (h + 1) * P], ACT.Exp,
                            bias=ngc[:, c * 4 + h:c * 4 + h + 1])
                    (step if h < 3 else own["dec_ready"]).own(ins)

            def first_inverse(c):
                own["x_turned"].next()
                own["x_first"].own(f(xm[:, c, :], bank(At(T0["turn"] + c))))
                free(At(T0["turn"] + c))

            own["gc_seen"].next()
            rows(0)
            rows(1)
            for c in range(NB):
                decays(c)
                if c + 2 < NB:
                    rows(c + 2)
                first_inverse(c)

            zs = [solve[:, n, :] for n in range(2)]
            for n in range((LEVELS - 1) * NB):
                own["zz_done"].next()
                own["zs_ready"].own(f(zs[n % 2], aux[:, (n % 2) * T:(n % 2 + 1) * T]))

            def w_turned(c):
                own["wt_done"].next()
                own["nwt_ready"].own(f(solve[:, c % 2, :], aux[:, 0:T], scale=-1.0))

            for c in range(NB):
                if c == 0:
                    w_turned(1)
                own["vnew_done"].next()
                own["vnew_ready"].own(f(solve[:, 2 + c % 2, :], aux[:, T:2 * T]))
                own["o_done"].next()
                own["o_ready"].own(f(vf[:, :, c * P:(c + 1) * P],
                                     aux[:, 3 * T:4 * T].rearrange("p (h n) -> p h n", h=GDN_H)))
                if 0 < c < NB - 1:
                    w_turned(c + 1)

            own["osq_ready"].own(f(kdec[:], flat(vf), ACT.Square))
            own["ostat_done"].next()
            own["groot_ready"].own(f(kdec[:], aux[:, 0:4 * T], ACT.Sqrt, bias=eps[:, 0:1], scale=1.0 / P))
            own["cfc_ready"].next()
            own["cfsq_ready"].own(f(kb[:], flat(cfy[:, :, :]), ACT.Square))
            for k in range(GDN_H):
                own["on_ready"].next()
                own["norm_hi"].own(f(x_hi[:, k, :], vf[:, k, :]))
            own["cfvar_done"].next()
            own["root_ready"].own(f(rs[:], aux[:, 5 * T:6 * T], ACT.Sqrt, scale=1.0 / (CFM_T * P), bias=eps[:, 0:1]))
            for k in range(CFM_T):
                own["cfn_ready"].next()
                step.own(f(cfy[:, k, :], cfy[:, k, :], ACT.Silu, bias=cols[:, C0["ln_b"] + k:C0["ln_b"] + k + 1]))
                own["norm_hi"].own(f(x_hi[:, GDN_H + k, :], cfy[:, k, :]))

            for n in range(4):
                split_hi(At(U0["mix_out"] + n + AHEAD))
            act.wait_ge(S["mem_loaded"], 16)
            own["memsq_ready"].own(f(msq, flat(memf[:, :, :]), ACT.Square))
            for n in range(4, 8):
                split_hi(At(U0["mix_out"] + n + AHEAD))
            own["memstat_done"].next()
            own["memroot_ready"].own(f(mroot, aux[:, 4 * T:4 * T + MEM], ACT.Sqrt, scale=1.0 / D, bias=eps[:, 0:1]))
            own["memn_ready"].next()
            own["mem_hi_ready"].own(f(mem_hi[:], memf[:]))
            root(1.0 / D)

            for n in range(KT):
                u, t = At(U0["kv"] + n), At(T0["kv"] + n)
                split_hi(u + AHEAD)
                act.wait_ge(unit_used, (u + 1).val())
                own["km_ready"].own(f(kmt[:, n, :], bank(t)[:, 0:MEM]))
                free(t)
            for half in range(2):
                for j in range(4):
                    split_hi(At(U0["kv"] + 8 + 4 * half + j + AHEAD))
                act.wait_ge(unit_used, U0["kv"] + 12 + 4 * half)
                for b in range(2):
                    bk = 2 * half + b
                    own["vm_ready"].own(f(vm[:, b, half * T:(half + 1) * T], aux[:, bk * T:(bk + 1) * T]))
            root(1.0 / D)
            norm_hi()
            with loop(act, 2, [(own["qx_ready"], 4)]) as i:
                for n in range(4):
                    u, t = At(U0["xq"] + n, i, 4), At(T0["xq"] + n, i, 4)
                    split_hi(u + AHEAD)
                    act.wait_ge(unit_used, (u + 1).val())
                    own["qx_ready"].own(f(qx[:, bass.ds(i * 4 + n, 1), :].rearrange("p a n -> p (a n)"), bank(t)))
                    free(t)

            XSC = (KT // XH * P) ** -0.5

            def exps(h):
                own["xmax_ready"].next()
                for t in range(NB):
                    ins = f(px[:, h % 2, t, :], aux[:, (h % 2) * 2 * T + t * MEM:(h % 2) * 2 * T + (t + 1) * MEM], ACT.Exp,
                            scale=XSC, bias=xcols[:, h % 2, 0, t:t + 1], accum_out=xcols[:, h % 2, 1, t:t + 1])
                    (step if t < NB - 1 else own["px_ready"]).own(ins)

            def turned(h):
                own["px_turned"].next()
                own["pxt_ready"].own(f(pxt[:, h % 2, :], aux[:, 4 * T:6 * T]))
                for d in range(2):
                    t = At(T0["x_val"] + 2 * h + d)
                    own["tile_done"].next()
                    own["xo_hi_ready"].own(f(xo_hi[:, 2 * h + d, :], bank(t)))

            own["tile_done"].skip(6)
            exps(0)
            for h in range(XH):
                if h + 1 < XH:
                    exps(h + 1)
                turned(h)
            for n in range(8):
                split_hi(At(U0["xo"] + n + AHEAD))
            root(1.0 / D)
            root(1.0 / D)
            norm_hi()

            with loop(act, FT // 2, [(own["fin_ready"], 4), (own["conv2_ready"], 4), (own["silu2_ready"], 2),
                                     (own["hidden_f"], 2), (own["hidden_hi"], 2)]) as i:
                for n in range(2):
                    u, t = At(U0["up"] + 2 * n, i, 4), At(T0["up"] + 2 * n, i, 4)
                    for m in range(2):
                        split_hi(u + m + AHEAD)
                        act.wait_ge(unit_used, (u + m + 1).val())
                        own["fin_ready"].own(f(fin[:, m, CONV_F - 1:], bank(t + m)))
                        free(t + m)
                    own["conv2_ready"].next()
                    own["silu2_ready"].own(f(tn[:, 0, :], tn[:, 0, :], ACT.Silu))
                    own["conv2_ready"].next()
                    own["hidden_f"].next()
                    own["hidden_hi"].own(f(g_hi[:, bass.ds(i * 2 + n, 1), :].rearrange("p a n -> p (a n)"), ht2[:]))
            for u in range(U0["down"], U0["down"] + 24):
                split_hi(At(u + AHEAD))
            root(1.0 / D)

        @block.vector
        def _(dve):
            own = {n: Count(dve, S[n]) for n in S}
            step = own["dve_step"]
            V = nc.vector

            def col(name, k):
                return cols[:, bass.ds(k + C0[name], 1)]

            def free(t):
                V.sem_inc(acc_free[t.slot(2)], 1)

            def at_tile(buf, k):
                return buf[:, bass.ds(k, 1), :].rearrange("p a n -> p (a n)")

            dve.wait_ge(S["consts_loaded"], 48)
            sm = {n: small[:, SM0[n]:SM0[n] + P] for n, _ in SMALL}
            ready = own["consts_ready"]
            ready.own(V.memset(eps[:], EPS))
            ready.own(V.tensor_copy(negtri_r[:], sm["neg_tri"]))
            ready.own(V.tensor_scalar(negone_r[:], sm["ones"], -1.0, None, ALU.mult))
            ready.own(V.tensor_copy(ident_b[:], sm["ident"]))
            ready.own(V.tensor_scalar(mask_b[:], sm["keep"], -NEG, NEG, ALU.mult, ALU.add))
            ready.own(V.tensor_scalar(causal_b[:], sm["tri"], -NEG, NEG, ALU.mult, ALU.add))

            def ada(w, dst, k):
                c = c_act[:, k:k + 1]
                if k == 0:
                    return V.tensor_scalar(dst[:], w, c, None, ALU.mult)
                return V.scalar_tensor_tensor(dst[:], w, c, dst[:], ALU.mult, ALU.add)

            own["c_ready_act"].next()
            for m in range(2):
                for k in range(KT):
                    n = m * KT + k
                    dve.wait_ge(S[f"ada0_loaded{n % 4}"], 16 * (n // 4 + 1))
                    own["ada_used"].own(ada(ada0[:, n % 4, :], adac0, k))
                own["ada_ready"].next()
                step.own(V.tensor_tensor(mod[:, m * KT:(m + 1) * KT], aux[:, 4 * T:4 * T + KT],
                                         cols[:, C0["b_ada"] + m * KT:C0["b_ada"] + (m + 1) * KT], ALU.add))
            step.own(V.scalar_tensor_tensor(gain1[:], mod[:, KT:2 * KT], 1.0,
                                            cols[:, C0["g_norm1"]:C0["g_norm1"] + KT], ALU.add, ALU.mult))

            def invert():
                own["root_ready"].next()
                step.own(V.reciprocal(rs[:], rs[:]))

            def norm(gain, shift):
                invert()

                def low(k):
                    own["norm_hi"].next()
                    own["x_ready"].own(V.tensor_tensor(x_lo[:, k, :], tn[:, k % 2, :], x_hi[:, k, :].bitcast(F32),
                                                       ALU.subtract))

                for k in range(KT):
                    t = tn[:, k % 2, :]
                    ins = V.scalar_tensor_tensor(t, resid[:, k, :], gain[:, k:k + 1], rs[:], ALU.mult, ALU.mult)
                    if shift is None:
                        own["normed"].own(ins)
                    else:
                        step.own(ins)
                        own["normed"].own(V.tensor_scalar(t, t, shift[:, k:k + 1], None, ALU.add))
                    if k:
                        low(k - 1)
                low(KT - 1)

            norm(gain1, mod[:, 0:KT])

            zp = [aux[:, 0:TRI], aux[:, 3 * T:3 * T + TRI]]

            def pair_values(p):
                own["vp_ready"].own(V.tensor_copy(vp, v_sb[:, :, bass.ds(p * P, P)]))

            def out_lo(t, p):
                own["osb_hi_ready"].next()
                own["osb_ready"].own(V.tensor_tensor(at_tile(osb_lo, p), bank(t), at_tile(osb_hi, p).bitcast(F32),
                                                     ALU.subtract))
                free(t)

            def pair(t, first, p):
                for h in range(2):
                    own["log_ready"].next()
                    step.own(V.scalar_tensor_tensor(sp[h][:], zp[h], 0.0, sp[h][:], ALU.max, ALU.add))
                    for j, a in enumerate(TRI_AT):
                        ins = V.tensor_tensor(sp[h][:, a:a + P], sp[h][:, a:a + P], sm["keep"], ALU.mult)
                        (step if j < NB - 1 else own["sp_ready"]).own(ins)
                for h in range(2):
                    own["sp_hi_ready"].next()
                    own["sp_split"].own(V.tensor_tensor(sp_lo[h][:], sp[h][:], sp_hi[h][:].bitcast(F32), ALU.subtract))
                if not first:
                    out_lo(t, p - 1)
                pair_values(p)

            own["v_ready"].next(8)
            pair(None, True, 0)
            with loop(dve, 3, [(step, 16), (own["log_ready"], 4),
                               (own["sp_ready"], 4), (own["sp_hi_ready"], 4), (own["sp_split"], 4),
                               (own["osb_hi_ready"], 2), (own["osb_ready"], 2), (own["vp_ready"], 2)]) as i:
                for s in range(2):
                    pair(At(4 + 3 * s, i, 6), False, i * 2 + (1 + s))
            pair(At(22), False, PAIRS - 1)
            out_lo(At(23), PAIRS - 1)

            with loop(dve, 4, [(own["gate_ready"], 2), (own["msb_ready"], 2)]) as i:
                for n in range(2):
                    u, t = At(U0["sb_out"] + 2 * n + 1, i, 4), At(2 * n + 1, i, 4)
                    own["gate_ready"].next()
                    dve.wait_ge(unit_used, (u + 1).val())
                    own["msb_ready"].own(V.tensor_tensor(at_tile(msb, i * 2 + n), bank(t), gate_t[:, n, :], ALU.mult))
                    free(t)
            own["decay_free"].own(V.memset(pret[:], 0.0))

            def rotate(u, dst):
                a, b = bank(At(0)), bank(At(1))
                dve.wait_ge(unit_used, (u + 1).val())
                step.own(V.tensor_tensor(dst[:, 0, :], a, cos, ALU.mult))
                step.own(V.tensor_tensor(dst[:, 1, :], a, sin, ALU.mult))
                free(At(0))
                dve.wait_ge(unit_used, (u + 2).val())
                step.own(V.tensor_tensor(sqt[:], b, sin, ALU.mult))
                step.own(V.tensor_tensor(dst[:, 0, :], dst[:, 0, :], sqt[:], ALU.subtract))
                step.own(V.tensor_tensor(sqt[:], b, cos, ALU.mult))
                free(At(1))
                own["qk_rot"].own(V.tensor_tensor(dst[:, 1, :], dst[:, 1, :], sqt[:], ALU.add))

            def ada_steps(n):
                for _ in range(n):
                    k = own["ada1_loaded"].at.c // 16 % KT
                    own["ada1_loaded"].next(16)
                    own["ada_used"].own(ada(ada1[:], adac, k))

            def square(src, first, last):
                end = own["sq_ready"] if last else step
                if first:
                    end.own(V.tensor_tensor(sqacc[:], src, src, ALU.mult))
                else:
                    step.own(V.tensor_tensor(sqt[:], src, src, ALU.mult))
                    end.own(V.tensor_tensor(sqacc[:], sqacc[:], sqt[:], ALU.add))

            dve.wait_ge(S["tables_loaded"], 16)
            own["tile_done"].skip(PAIRS)
            own["sq_ready"].skip(1)
            with loop(dve, RET_H, [(step, 10 + 3 + 6 + 1 + 4 + 1 + 8), (own["qk_rot"], 2), (own["ada_used"], 8), (own["ada1_loaded"], 16 * KT),
                                   (own["rsc_done"], 1), (own["rsc_ready"], 1), (own["decay_free"], 1),
                                   (own["oraw_ready"], 4), (own["sq_ready"], 1), (own["root_ready"], 1),
                                   (own["gate_ready"], 4), (own["oprod_ready"], 4), (own["orh_ready"], 4),
                                   (own["or_ready"], 4), (own["ada_ready"], 1), (own["tile_done"], 8)]) as i:
                u0 = At(U0["ret"], i, 16)
                rotate(u0, rq)
                ada_steps(3)
                rotate(u0 + 2, rk)
                ada_steps(3)
                own["rsc_done"].next()
                dve.wait_ge(S["decay_loaded"], i * 16 + 16)
                for j in range(NB):
                    a, w = TRI_AT[j], TRI_W[j]
                    ins = V.tensor_tensor(rsc[:, a:a + w], aux[:, a:a + w], decay[:, 0:w], ALU.mult)
                    (step if j < NB - 1 else own["rsc_ready"]).own(ins)
                V.sem_inc(S["decay_free"], 1)
                own["decay_free"].skip()
                for e in range(RET_VT):
                    own["oraw_ready"].next()
                    square(oraw[:, e, :], e == 0, e == RET_VT - 1)
                ada_steps(1)
                invert()
                for e in range(RET_VT):
                    step.own(V.tensor_tensor(oraw[:, e, :], oraw[:, e, :], rs[:], ALU.mult))
                for e in range(RET_VT):
                    own["gate_ready"].next()
                    own["oprod_ready"].own(V.tensor_tensor(oraw[:, e, :], oraw[:, e, :], gate_t[:, e % 2, :], ALU.mult))
                    if e == RET_VT - 1:
                        ada_steps(1)
                    own["orh_ready"].next()
                    own["or_ready"].own(V.tensor_tensor(orl[:, e, :], oraw[:, e, :], orh[:, e, :].bitcast(F32),
                                                        ALU.subtract))
                own["ada_ready"].next()
                step.own(V.tensor_tensor(mod[:, bass.ds(i * KT + 2 * KT, KT)], aux[:, 4 * T:4 * T + KT],
                                         cols[:, bass.ds(i * KT + (C0["b_ada"] + 2 * KT), KT)], ALU.add))
                own["tile_done"].skip(RET_VT)
                for n in range(KT):
                    if n % 2 == 0:
                        own["tile_done"].next()
                    else:
                        dve.wait_ge(unit_used, (u0 + 12 + n // 2 + 1).val())
                    step.own(V.tensor_tensor(pret[:, n, :], pret[:, n, :], bank(At(n)), ALU.add))
                    free(At(n))
            step.own(V.scalar_tensor_tensor(gain2[:], mod[:, 4 * KT:5 * KT], 1.0,
                                            cols[:, C0["g_norm2"]:C0["g_norm2"] + KT], ALU.add, ALU.mult))

            with loop(dve, 2, [(step, 4), (own["gate_ready"], 4), (own["merged_f"], 4), (own["merged_hi"], 4),
                               (own["merged"], 4)]) as i:
                for n in range(4):
                    own["gate_ready"].next()
                    m = mt[:, n % 2, :]
                    step.own(V.tensor_tensor(m, gate_t[:, n % 2, :], at_tile(pret, i * 4 + n), ALU.mult))
                    own["merged_f"].own(V.tensor_tensor(m, m, at_tile(msb, i * 4 + n), ALU.add))
                    own["merged_hi"].next()
                    own["merged"].own(V.tensor_tensor(at_tile(m_lo, i * 4 + n), m,
                                                      at_tile(m_hi, i * 4 + n).bitcast(F32), ALU.subtract))

            def residual(t, k, gate, last=None):
                r = at_tile(resid, k)
                step.own(V.scalar_tensor_tensor(r, bank(t), mod[:, bass.ds(k + gate * KT, 1)], r, ALU.mult, ALU.add))
                free(t)
                step.own(V.tensor_tensor(sqt[:], r, r, ALU.mult))
                step.own(V.tensor_tensor(sqacc[:], sqacc[:], sqt[:], ALU.add))

            step.own(V.memset(sqacc[:], 0.0))
            with loop(dve, 2, [(step, 12)]) as i:
                for n in range(4):
                    dve.wait_ge(unit_used, At(U0["out"] + n + 1, i, 4).val())
                    residual(At(n), i * 4 + n, 2)
            V.sem_inc(S["sq_ready"], 1)
            own["sq_ready"].skip()
            norm(gain2, mod[:, 3 * KT:4 * KT])

            with loop(dve, FT // 2, [(own["gate_ready"], 2), (own["hidden_f"], 2), (own["hidden_hi"], 2),
                                     (own["hidden"], 2)]) as i:
                for n in range(2):
                    u, t = At(U0["ff_in"] + 2 * n + 1, i, 4), At(2 * n + 1)
                    own["gate_ready"].next()
                    dve.wait_ge(unit_used, (u + 1).val())
                    own["hidden_f"].own(V.tensor_tensor(ht[:, n, :], bank(t), gate_t[:, n, :], ALU.mult))
                    free(t)
                    own["hidden_hi"].next()
                    own["hidden"].own(V.tensor_tensor(at_tile(h_lo, i * 2 + n), ht[:, n, :],
                                                      at_tile(h_hi, i * 2 + n).bitcast(F32), ALU.subtract))
            step.own(V.memset(sqacc[:], 0.0))
            with loop(dve, 2, [(step, 12), (own["tile_done"], 3)]) as i:
                for n in range(4):
                    if n < 3:
                        own["tile_done"].next()
                    else:
                        dve.wait_ge(unit_used, At(U0["ff_out"] + 12, i, 12).val())
                    residual(At(n), i * 4 + n, 5)
            V.sem_inc(S["sq_ready"], 1)
            own["sq_ready"].skip()
            invert()
            for k in range(KT):
                ins = V.scalar_tensor_tensor(resid[:, k, :], resid[:, k, :],
                                             cols[:, C0["g_final"] + k:C0["g_final"] + k + 1], rs[:], ALU.mult, ALU.mult)
                step.own(ins)
                square(resid[:, k, :], k == 0, k == KT - 1)
            def param(name, k=0, n=1):
                return cols[:, C0[name] + k:C0[name] + k + n]

            def heads(x):
                return x.rearrange("p (h n) -> p h n", h=GDN_H)

            def spread(x):
                return x.rearrange("p (h a) -> p h a", a=1).broadcast_to([P, GDN_H, P])

            def repeat(x):
                return x.rearrange("p (a n) -> p a n", a=1).broadcast_to([P, GDN_H, P])

            def flat(x):
                return x.rearrange("p k n -> p (k n)")

            step.own(V.memset(gb[:], 0.0))
            step.own(V.memset(cin[:, :, 0:CONV_G - 1], 0.0))
            step.own(V.memset(cfin[:, :, 0:CONV_C - 1], 0.0))
            norm_g = [param("norm_g", n * KT, KT) for n in range(6)]
            own["nega_ready"].skip()
            norm(norm_g[0], None)
            dve.wait_ge(S["nega_ready"], 1)
            step.own(V.tensor_scalar(nega[0:GDN_H, 0:1], nega[0:GDN_H, 0:1], -1.0, None, ALU.mult))
            g0, t0 = At(U0["gdn_in"]), At(T0["gdn_in"])
            own["ab_ready"].next()
            step.own(V.scalar_tensor_tensor(abx[0:GDN_H, :], abx[0:GDN_H, :], 0.0, abt[0:GDN_H, :], ALU.max, ALU.add))
            own["gb_ready"].own(V.tensor_scalar(gb[0:GDN_H, :], abx[0:GDN_H, :], nega[0:GDN_H, 0:1], None, ALU.mult))

            with loop(dve, 3, [(step, 12), (own["cin_ready"], 4), (own["conv_ready"], 4)]) as i:
                for n in range(4):
                    own["cin_ready"].next()
                    y = tn[:, n % 2, :]
                    for j in range(CONV_G):
                        w = cols[:, bass.ds(i * 16 + (C0["gdn_conv"] + n * CONV_G + j), 1)]
                        x = cin[:, n % 2, j:j + T]
                        if j == 0:
                            ins = V.tensor_scalar(y, x, w, None, ALU.mult)
                        else:
                            ins = V.scalar_tensor_tensor(y, x, w, y, ALU.mult, ALU.add)
                        (step if j < CONV_G - 1 else own["conv_ready"]).own(ins)

            def cfm_in(n):
                u, t = g0 + CFM + 2 * n + 1, t0 + CFM + 2 * n + 1
                own["gate_ready"].next()
                dve.wait_ge(unit_used, (u + 1).val() if n < 3 else U0["gdn_in"] + 28)
                own["cfin_ready"].own(V.tensor_tensor(cfin[:, n, CONV_C - 1:], bank(t), gate_t[:, n % 2, :], ALU.mult))
                free(t)

            own["groot_ready"].next()
            step.own(V.reciprocal(kdec[:], kdec[:]))
            own["k_normed"].own(V.tensor_tensor(flat(kf), flat(kf), kdec[:], ALU.mult))
            cfm_in(0)
            own["gb_turned"].next()
            own["gbt_ready"].own(V.tensor_copy(gbt[:], aux[:, 4 * T:5 * T].rearrange("p (c n) -> p c n", c=NB)[:, :, 0:64]))
            cfm_in(1)
            own["groot_ready"].next()
            step.own(V.reciprocal(vb[:], vb[:]))
            own["q_normed"].own(V.scalar_tensor_tensor(flat(qf), flat(qf), P ** -0.5, vb[:], ALU.mult, ALU.mult))
            own["egc_ready"].next()
            own["gc_seen"].own(V.tensor_scalar(ngc[:], aux[:, 5 * T:5 * T + 16], -1.0, None, ALU.mult))
            step.own(V.tensor_tensor(bg.rearrange("p (c h) -> p c h", c=NB), gbt[:, :, 32:36],
                                     egc.rearrange("p (c h) -> p c h", c=NB), ALU.mult))
            cfm_in(2)
            cfm_in(3)

            taps = [(n, j) for n in range(CFM_DVE) for j in range(CONV_C)]

            def cfm_taps(m):
                for _ in range(min(m, len(taps))):
                    n, j = taps.pop(0)
                    x, w, y = cfin[:, n, j:j + T], param("cfm_conv", n * CONV_C + j), cfy[:, n, :]
                    if j == 0:
                        step.own(V.tensor_scalar(y, x, w, param("cfm_b", n), ALU.mult, ALU.add))
                    else:
                        step.own(V.scalar_tensor_tensor(y, x, w, y, ALU.mult, ALU.add))

            def beta_k(c):
                b = 3 * (c % 2) + 1
                own["beta_row"].next()
                own["kb_ready"].own(V.tensor_tensor(kb[:].rearrange("p (h n) -> p h n", h=GDN_H)[:, :, c * P:(c + 1) * P],
                                                    kf[:, :, c * P:(c + 1) * P], heads(aux[:, b * T:(b + 1) * T]), ALU.mult))

            def lower(c):
                b = 3 * (c % 2) + 2
                own["kk_done"].next()
                own["dec_ready"].next()
                step.own(V.tensor_tensor(bt[:, c, :], aux[:, b * T:(b + 1) * T], dect[:, c, :], ALU.mult))
                step.own(V.tensor_tensor(heads(xt[:, c, :]), heads(bt[:, c, :]), repeat(halves[:, 0, :]), ALU.mult))
                own["xt_ready"].own(V.tensor_tensor(heads(xt[:, c, :]), repeat(sm["ident"]), heads(xt[:, c, :]),
                                                    ALU.subtract))

            beta_k(0)
            beta_k(1)
            for c in range(NB):
                lower(c)
                if c + 2 < NB:
                    beta_k(c + 2)
                cfm_taps(2)
            own["egr_ready"].next(NB)
            step.own(V.tensor_copy(egl.rearrange("p (c h) -> p h c", c=NB),
                                   egr[:, :, P - 1:T:P]))
            own["qe_ready"].own(V.tensor_tensor(flat(egr[:, :, :]), flat(egr[:, :, :]), flat(qf), ALU.mult))

            for c in range(NB):
                b = c % 2
                own["kv_turned"].next()
                cc = slice(c * T, (c + 1) * T)
                step.own(V.tensor_tensor(heads(vb[:, cc]), heads(aux[:, b * T:(b + 1) * T]),
                                         spread(gbt[:, c, 32:36]), ALU.mult))
                k = heads(aux[:, (2 + b) * T:(3 + b) * T])
                step.own(V.tensor_tensor(heads(kb[:, cc]), k, spread(bg[:, c * 4:c * 4 + 4]), ALU.mult))
                own["kv_token"].own(V.tensor_tensor(heads(kdec[:, cc]), k,
                                                    heads(dect[:, c, :])[:, :, P - 1:P].broadcast_to([P, GDN_H, P]),
                                                    ALU.mult))
                cfm_taps(1)

            def level_b(n):
                own["bm_ready"].own(V.tensor_tensor(heads(solve[:, 2 + n % 2, :]), heads(bt[:, n % NB, :]),
                                                    repeat(halves[:, 1 + n // NB, :]), ALU.mult))

            n_solve = (LEVELS - 1) * NB
            level_b(0)
            for n in range(n_solve):
                if n + 1 < n_solve:
                    level_b(n + 1)
                cfm_taps(2)
                own["xz_done"].next()
                c, b = n % NB, n % 2
                if n < n_solve - NB:
                    step.own(V.tensor_tensor(xm[:, c, :], xm[:, c, :], aux[:, (2 + b) * T:(3 + b) * T], ALU.subtract))
                own["x_upd"].own(V.tensor_tensor(xt[:, c, :], xt[:, c, :], aux[:, (4 + b) * T:(5 + b) * T], ALU.subtract))

            att = [sqt, rs]

            def within(c):
                own["qk_done"].next()
                own["at_ready"].own(V.tensor_tensor(att[c % 2][:], aux[:, 2 * T:3 * T], dect[:, c, :], ALU.mult))

            within(0)
            for c in range(NB):
                if c + 1 < NB:
                    own["s_done"].next()
                    if c == 0:
                        own["s_ready"].own(V.tensor_copy(sqacc[:], aux[:, 4 * T:5 * T]))
                    else:
                        step.own(V.tensor_tensor(heads(sqacc[:]), heads(sqacc[:]), spread(egl[:, c * 4:c * 4 + 4]), ALU.mult))
                        own["s_ready"].own(V.tensor_tensor(sqacc[:], sqacc[:], aux[:, 4 * T:5 * T], ALU.add))
                    within(c + 1)
                cfm_taps(2)
            cfm_taps(len(taps))
            own["cf_dve"].own(V.memset(egl[:, 0:1], 0.0))

            own["cfsum_done"].next()
            for k in range(CFM_T):
                ins = V.scalar_tensor_tensor(cfy[:, k, :], aux[:, 5 * T:6 * T], -1.0 / (CFM_T * P), cfy[:, k, :],
                                             ALU.mult, ALU.add)
                (step if k < CFM_T - 1 else own["cfc_ready"]).own(ins)

            def low(k, src):
                own["norm_hi"].next()
                own["x_ready"].own(V.tensor_tensor(x_lo[:, k, :], src, x_hi[:, k, :].bitcast(F32), ALU.subtract))

            own["groot_ready"].next()
            step.own(V.reciprocal(kdec[:], kdec[:]))
            own["sgate_ready"].next(GDN_H)
            for k in range(GDN_H):
                step.own(V.scalar_tensor_tensor(vf[:, k, :], vf[:, k, :], param("gdn_g"), kdec[:, k * T:(k + 1) * T],
                                                ALU.mult, ALU.mult))
                own["on_ready"].own(V.tensor_tensor(vf[:, k, :], vf[:, k, :], sgate[:, k, :], ALU.mult))
            for k in range(GDN_H):
                low(k, vf[:, k, :])
            invert()
            for k in range(CFM_T):
                own["cfn_ready"].own(V.scalar_tensor_tensor(cfy[:, k, :], cfy[:, k, :], param("ln_g", k), rs[:],
                                                            ALU.mult, ALU.mult))
            for k in range(CFM_T):
                low(GDN_H + k, cfy[:, k, :])
            V.sem_inc(S["gdn_over"], 1)

            def sublayer_tile(t, dst, last=False):
                step.own(V.tensor_copy(dst, bank(t)))
                free(t)
                step.own(V.tensor_tensor(sqt[:], dst, dst, ALU.mult))
                step.own(V.tensor_tensor(sqacc[:], sqacc[:], sqt[:], ALU.add))

            def add_sublayer(y, gain, last=False):
                invert()
                for k in range(KT):
                    step.own(V.scalar_tensor_tensor(y[:, k, :], y[:, k, :], gain[:, k:k + 1], rs[:], ALU.mult, ALU.mult))
                    ins = V.tensor_tensor(resid[:, k, :], resid[:, k, :], y[:, k, :], ALU.add)
                    if last:
                        own["resid_ready"].own(ins)
                    else:
                        step.own(ins)
                        square(resid[:, k, :], k == 0, k == KT - 1)

            def end_squares():
                V.sem_inc(S["sq_ready"], 1)
                own["sq_ready"].skip()

            step.own(V.memset(sqacc[:], 0.0))
            for n in range(KT):
                dve.wait_ge(unit_used, U0["mix_out"] + n + 1)
                sublayer_tile(At(T0["mix_out"] + n), yv[:, n, :])
            end_squares()
            own["memroot_ready"].next()
            step.own(V.reciprocal(mroot, mroot))
            for k in range(KT):
                ins = V.scalar_tensor_tensor(memf[:, k, :], memf[:, k, :], param("mem_g", k), mroot, ALU.mult, ALU.mult)
                (step if k < KT - 1 else own["memn_ready"]).own(ins)
            own["mem_hi_ready"].next()
            own["mem_ready"].own(V.tensor_tensor(mem_lo[:], memf[:], mem_hi[:].bitcast(F32), ALU.subtract))
            add_sublayer(yv, norm_g[1])
            norm(norm_g[2], None)

            def row_max(h):
                own["xs_done"].next()
                b = (h % 2) * 2 * T
                step.own(V.tensor_reduce(xcols[:, h % 2, 2, :], aux[:, b:b + 2 * T].rearrange("p (t m) -> p t m", t=NB),
                                         AX.X, ALU.max))
                own["xmax_ready"].own(V.tensor_scalar(xcols[:, h % 2, 0, :], xcols[:, h % 2, 2, :],
                                                      -((KT // XH * P) ** -0.5), None, ALU.mult))

            def normalize(h):
                own["px_ready"].next()
                step.own(V.reciprocal(xcols[:, h % 2, 1, :], xcols[:, h % 2, 1, :]))
                own["pxn_ready"].own(V.tensor_tensor(
                    px[:, h % 2, :, :], px[:, h % 2, :, :],
                    xcols[:, h % 2, 1, :].rearrange("p (t a) -> p t a", a=1).broadcast_to([P, NB, MEM]), ALU.mult))

            def out_low(h):
                for d in range(2):
                    t, k = At(T0["x_val"] + 2 * h + d), 2 * h + d
                    own["xo_hi_ready"].next()
                    own["xo_ready"].own(V.tensor_tensor(xo_lo[:, k, :], bank(t), xo_hi[:, k, :].bitcast(F32), ALU.subtract))
                    free(t)

            own["tile_done"].skip(KT)
            row_max(0)
            row_max(1)
            normalize(0)
            for h in range(XH):
                if h + 2 < XH:
                    row_max(h + 2)
                if h + 1 < XH:
                    normalize(h + 1)
                out_low(h)
            step.own(V.memset(sqacc[:], 0.0))
            for n in range(KT):
                dve.wait_ge(unit_used, U0["xo"] + n + 1)
                sublayer_tile(At(T0["xo"] + n), yv_o[:, n, :])
            end_squares()
            add_sublayer(yv_o, norm_g[3])
            step.own(V.memset(fin[:, :, 0:CONV_F - 1], 0.0))
            norm(norm_g[4], None)

            with loop(dve, FT // 2, [(step, 8), (own["fin_ready"], 4), (own["conv2_ready"], 4), (own["silu2_ready"], 2),
                                     (own["hidden_f"], 2), (own["hidden_hi"], 2), (own["hidden"], 2)]) as i:
                for n in range(2):
                    for m in range(2):
                        own["fin_ready"].next()
                        y = tn[:, m, :]
                        for j in range(CONV_F):
                            at_ = i * (4 * CONV_F) + (C0["ff_conv"] + (2 * n + m) * CONV_F + j)
                            w, x = cols[:, bass.ds(at_, 1)], fin[:, m, j:j + T]
                            if j == 0:
                                b = cols[:, bass.ds(i * 4 + (C0["ff_conv_b"] + 2 * n + m), 1)]
                                ins = V.tensor_scalar(y, x, w, b, ALU.mult, ALU.add)
                            else:
                                ins = V.scalar_tensor_tensor(y, x, w, y, ALU.mult, ALU.add)
                            (step if j < CONV_F - 1 else own["conv2_ready"]).own(ins)
                    own["silu2_ready"].next()
                    own["hidden_f"].own(V.tensor_tensor(ht2[:], tn[:, 0, :], tn[:, 1, :], ALU.mult))
                    own["hidden_hi"].next()
                    own["hidden"].own(V.tensor_tensor(at_tile(g_lo, i * 2 + n), ht2[:], at_tile(g_hi, i * 2 + n).bitcast(F32),
                                                      ALU.subtract))
            step.own(V.memset(sqacc[:], 0.0))
            with loop(dve, 2, [(step, 12), (own["tile_done"], 3)]) as i:
                for n in range(4):
                    if n < 3:
                        own["tile_done"].next()
                    else:
                        dve.wait_ge(unit_used, At(U0["down"] + 12, i, 12).val())
                    sublayer_tile(At(T0["down"] + n, i, 4), at_tile(yv2, i * 4 + n))
            end_squares()
            add_sublayer(yv2, norm_g[5], last=True)

        @block.tensor
        def _(pe):
            own = {n: Count(pe, S[n]) for n in S}
            M = nc.tensor.matmul
            ones = small[:, SM0["ones"]:SM0["ones"] + P]

            def wait_bank(t):
                if t.i is not None or t.c >= 2:
                    pe.wait_ge(acc_free[t.slot(2)], t.div(2).val())

            def weights(u):
                pe.wait_ge(lo_ready, (u + 1).val())
                return w_hi[u.slot(RING)], w_lo[u.slot(RING)]

            def three(out, a_hi, a_lo, b_hi, b_lo, first, last):
                M(out, a_hi, b_hi, start=first, stop=False)
                M(out, a_hi, b_lo, start=False, stop=False)
                return M(out, a_lo, b_hi, start=False, stop=last)

            def wt(w, k):
                return w[:, k * P:(k + 1) * P]

            def tile(u, t, hi, lo, width=T, extra=0):
                wait_bank(t)
                wh, wl = weights(u)
                if extra:
                    weights(u + extra)
                for k in range(KT):
                    m = three(bank(t)[:, 0:width], wt(wh, k), wt(wl, k), hi[:, k, :], lo[:, k, :], k == 0, k == KT - 1)
                m.then_inc(unit_used, 1 + extra)

            def token_tiles(u, banks, hi=x_hi, lo=x_lo):
                for j in range(4):
                    wh, wl = weights(u + j)
                    for kk in range(2):
                        k = 2 * j + kk
                        for b, bk in enumerate(banks):
                            m = three(aux[:, bk * T:(bk + 1) * T],
                                      hi[:, k, b * P:(b + 1) * P], lo[:, k, b * P:(b + 1) * P],
                                      wh[:, kk * T:(kk + 1) * T], wl[:, kk * T:(kk + 1) * T], k == 0, k == KT - 1)
                    m.then_inc(unit_used, 1)

            def stat():
                own["sq_ready"].next()
                M(aux[:, 5 * T:6 * T], ones, sqacc[:], start=True, stop=True).then_inc(S["stat_ready"], 1)

            def modulation(src):
                for n in range(KT):
                    m = M(aux[:, 4 * T + n:4 * T + n + 1], src[:, n * P:(n + 1) * P], ones[:, 0:1], start=True, stop=True)
                m.then_inc(S["ada_ready"], 1)

            pe.wait_ge(S["consts_loaded"], 48)
            stat()
            for m in range(2):
                own["ada_used"].next(KT)
                modulation(adac0)
            own["x_ready"].next(KT)
            token_tiles(At(0), (0, 1, 2, 3))
            own["v_ready"].next(2)
            token_tiles(At(4), (4, 5, 0, 1))

            tile(At(8), At(0), x_hi, x_lo)
            tile(At(9), At(1), x_hi, x_lo)
            own["v_ready"].next(6)
            own["consts_ready"].next(6)
            zp = [aux[:, 0:TRI], aux[:, 3 * T:3 * T + TRI]]

            def values(t):
                wait_bank(t)
                own["vp_ready"].next()
                for h in range(2):
                    r = slice(h * SB_DIM, (h + 1) * SB_DIM)
                    for j in range(NB):
                        a, w = TRI_AT[j], TRI_W[j]
                        m = M(bank(t)[r, j * P:T], vp[:, j, r], prob[h][:, a:a + w], start=j == 0, stop=j == NB - 1)
                m.then_inc(S["tile_done"], 1)

            def log_a(h):
                own["sp_split"].next()
                for j in TRI_ORDER:
                    a, w = TRI_AT[j], TRI_W[j]
                    for part in (sp_hi[h], sp_lo[h]):
                        M(zp[h][:, a:a + w], negtri_r[:], part[:, a:a + w], start=False, stop=False, skip_group_check=True)
                        for l in range(j + 1, NB):
                            b, v = TRI_AT[l], TRI_W[l]
                            M(zp[h][:, a + w - v:a + w], negone_r[:], part[:, b:b + v],
                              start=False, stop=False, skip_group_check=True)
                    m = M(zp[h][:, a:a + P], ident_b[:], mask_b[:], start=False, stop=True, skip_group_check=True)
                m.then_inc(S["log_a_ready"], 1)

            def pair(u, t, first, last):
                own["qk_ready"].next(2)
                for h in range(2):
                    if not first:
                        own["prob_ready"].next()
                    r = slice(h * SB_DIM, (h + 1) * SB_DIM)
                    for j in TRI_ORDER:
                        a, w = TRI_AT[j], TRI_W[j]
                        m = M(zp[h][:, a:a + w], kt_[r, j * P:(j + 1) * P], qt[r, j * P:T], start=j != 3, stop=True,
                              skip_group_check=True)
                    m.then_inc(S["z_ready"], 1)
                if not first:
                    values(t)
                    t = t + 1
                if not last:
                    tile(u, t, x_hi, x_lo)
                log_a(0)
                if not last:
                    tile(u + 1, t + 1, x_hi, x_lo)
                log_a(1)

            pair(At(10), At(2), True, False)
            with loop(pe, 3, [(own["qk_ready"], 4), (own["vp_ready"], 2), (own["prob_ready"], 4),
                              (own["sp_split"], 4)]) as i:
                for s in range(2):
                    pair(At(U0["sb_qk"] + 4 + 2 * s, i, 4), At(4 + 3 * s, i, 6), False, False)
            pair(None, At(22), False, True)
            own["prob_ready"].next(2)
            values(At(23))

            own["osb_ready"].next(PAIRS)
            with pe.Fori(0, 4) as i:
                for n in range(2):
                    u, t = At(U0["sb_out"] + 2 * n, i, 4), At(24 + 2 * n, i, 4)
                    tile(u, t, x_hi, x_lo)
                    tile(u + 1, t + 1, osb_hi, osb_lo)

            t_ret = 24 + 16
            pe.wait_ge(S["msb_ready"], KT)
            with loop(pe, RET_H, [(own["qk_rot"], 2), (own["rv_ready"], 4), (own["rsc_ready"], 1), (own["sq_ready"], 1),
                                  (own["ada_used"], 8), (own["or_ready"], 4)]) as i:
                u0, t0 = At(U0["ret"], i, 16), At(t_ret, i, 20)
                for n in range(4):
                    tile(u0 + n, t0 + n, x_hi, x_lo)
                token_tiles(u0 + 4, (2, 3, 4, 5))
                own["qk_rot"].next(2)
                own["rv_ready"].next(4)
                for j in TRI_ORDER:
                    a, w = TRI_AT[j], TRI_W[j]
                    for k in range(RET_QT):
                        m = M(aux[:, a:a + w], rk[:, k, j * P:(j + 1) * P], rq[:, k, j * P:T],
                              start=k == 0 and j != 3, stop=k == RET_QT - 1, skip_group_check=True)
                m.then_inc(S["rsc_done"], 1)
                own["rsc_ready"].next()
                for e in range(RET_VT):
                    t = t0 + 4 + e
                    wait_bank(t)
                    for j in range(NB):
                        a, w = TRI_AT[j], TRI_W[j]
                        m = M(bank(t)[:, j * P:T], rv[:, j, e * P:(e + 1) * P], rsc[:, a:a + w],
                              start=j == 0, stop=j == NB - 1)
                    m.then_inc(S["tile_done"], 1)
                for e in range(RET_VT):
                    tile(u0 + 8 + e, t0 + 8 + e, x_hi, x_lo)
                    if e == 0:
                        stat()
                own["ada_used"].next(KT)
                modulation(adac)
                own["or_ready"].next(RET_VT)
                for n in range(KT):
                    u, t = u0 + 12 + n // 2, t0 + 12 + n
                    wait_bank(t)
                    wh, wl = weights(u)
                    for e in range(RET_VT):
                        at_ = (n % 2) * RET_VT + e
                        m = three(bank(t), wt(wh, at_), wt(wl, at_), orh[:, e, :], orl[:, e, :], e == 0, e == RET_VT - 1)
                    m.then_inc(unit_used if n % 2 else S["tile_done"], 1)

            def tiles(phase, n, t0, hi, lo):
                with pe.Fori(0, n // 4) as i:
                    for k in range(4):
                        tile(At(U0[phase] + k, i, 4), At(t0 + k, i, 4), hi, lo)

            tiles("merge", KT, t_ret + 80, x_hi, x_lo)
            own["merged"].next(KT)
            tiles("out", KT, t_ret + 88, m_hi, m_lo)
            stat()
            own["x_ready"].next(KT)
            tiles("ff_in", 2 * FT, t_ret + 96, x_hi, x_lo)

            def down(phase, t0, hi, lo):
                own["hidden"].next(FT)
                with pe.Fori(0, 2) as i:
                    for n in range(4):
                        t = At(t0 + n, i, 4)
                        wait_bank(t)
                        for k in range(FT):
                            at_ = n * FT + k
                            u = At(U0[phase] + at_ // KT, i, 12)
                            if at_ % KT == 0 or k == 0:
                                wh, wl = weights(u)
                            m = three(bank(t), wt(wh, at_ % KT), wt(wl, at_ % KT), hi[:, k, :], lo[:, k, :],
                                      k == 0, k == FT - 1)
                            if at_ == 4 * FT - 1:
                                weights(u + 1)
                                m.then_inc(unit_used, 2)
                            elif at_ % KT == KT - 1:
                                m.then_inc(unit_used, 1)
                            elif k == FT - 1:
                                m.then_inc(S["tile_done"], 1)

            down("ff_out", t_ret + 96 + 2 * FT, h_hi, h_lo)
            stat()
            stat()
            own["x_ready"].next(KT)
            g0, t0 = At(U0["gdn_in"]), At(T0["gdn_in"])
            ident = small[:, SM0["ident"]:SM0["ident"] + P]
            tri = small[:, SM0["tri"]:SM0["tri"] + P]
            tile(g0, t0, x_hi, x_lo)
            with pe.Fori(0, 3) as i:
                for n in range(4):
                    tile(At(U0["gdn_in"] + KVQ + n, i, 4), At(T0["gdn_in"] + KVQ + n, i, 4), x_hi, x_lo)
            for n in range(GDN_H):
                tile(g0 + GATE + n, t0 + GATE + n, x_hi, x_lo)

            def head_stats(src, sem_):
                for h in range(GDN_H):
                    m = M(aux[:, h * T:(h + 1) * T], ones, src(h), start=True, stop=True)
                m.then_inc(S[sem_], 1)

            def cfm_pair(n):
                tile(g0 + CFM + 2 * n, t0 + CFM + 2 * n, x_hi, x_lo)
                if n < 3:
                    tile(g0 + CFM + 2 * n + 1, t0 + CFM + 2 * n + 1, x_hi, x_lo)
                else:
                    tile(g0 + CFM + 7, t0 + CFM + 7, x_hi, x_lo, extra=3)

            own["gsq_ready"].next()
            head_stats(lambda h: kdec[:, h * T:(h + 1) * T], "gstat_done")
            cfm_pair(0)
            own["gb_ready"].next()
            for c in range(NB):
                m = nc.tensor.transpose(aux[:, 4 * T + c * P:4 * T + (c + 1) * P], gb[:, c * P:(c + 1) * P], ident)
            m.then_inc(S["gb_turned"], 1)
            cfm_pair(1)
            own["gsq_ready"].next()
            own["groot_ready"].next()
            head_stats(lambda h: vb[:, h * T:(h + 1) * T], "gstat_done")
            own["gbt_ready"].next()
            M(aux[:, 5 * T:5 * T + 16], tri, gbt[:, :, 0:GDN_H], start=True, stop=True).then_inc(S["gc_done"], 1)
            cfm_pair(2)
            cfm_pair(3)

            def rows(c):
                b = 3 * (c % 2)
                for h in range(GDN_H):
                    m = M(aux[:, b * T + h * P:b * T + (h + 1) * P], gbt[:, c, h:h + 1].broadcast_to([P, P]), tri,
                          start=h == 0, stop=True, skip_group_check=True)
                m.then_inc(S["gc_row"], 1)
                for h in range(GDN_H):
                    m = M(aux[:, (b + 1) * T + h * P:(b + 1) * T + (h + 1) * P],
                          gbt[:, c, 32 + h:33 + h].broadcast_to([P, P]), ident, start=True, stop=True)
                m.then_inc(S["beta_row"], 1)

            own["groot_ready"].next()
            own["k_normed"].next()
            own["gc_seen"].next()
            rows(0)
            rows(1)
            for c in range(NB):
                b = 3 * (c % 2)
                own["egr_ready"].next()
                for h in range(GDN_H):
                    m = M(aux[:, b * T + h * P:b * T + (h + 1) * P], ident_b[:], causal_b[:], start=False, stop=True,
                          skip_group_check=True)
                m.then_inc(S["gc_masked"], 1)
                own["kb_ready"].next()
                for h in range(GDN_H):
                    at_ = slice(h * T + c * P, h * T + (c + 1) * P)
                    m = M(aux[:, (b + 2) * T + h * P:(b + 2) * T + (h + 1) * P], kf[:, h, c * P:(c + 1) * P], kb[:, at_],
                          start=True, stop=True)
                m.then_inc(S["kk_done"], 1)
                own["xt_ready"].next()
                if c + 2 < NB:
                    rows(c + 2)
                t = At(T0["turn"] + c)
                wait_bank(t)
                for h in range(GDN_H):
                    m = nc.tensor.transpose(bank(t)[:, h * P:(h + 1) * P], xt[:, c, h * P:(h + 1) * P], ident)
                m.then_inc(S["x_turned"], 1)

            for c in range(NB):
                b = c % 2
                if c >= 2:
                    own["kv_token"].next()
                for src, bk in ((vf, b), (kf, 2 + b)):
                    for h in range(GDN_H):
                        m = nc.tensor.transpose(aux[:, bk * T + h * P:bk * T + (h + 1) * P],
                                                src[:, h, c * P:(c + 1) * P], ident)
                m.then_inc(S["kv_turned"], 1)

            def each(bk, lhs, rhs):
                for h in range(GDN_H):
                    hh = slice(h * P, (h + 1) * P)
                    m = M(aux[:, bk * T + h * P:bk * T + (h + 1) * P], lhs[:, hh], rhs[:, hh], start=True, stop=True)
                return m

            n_solve = (LEVELS - 1) * NB
            own["kv_token"].next(2)

            def update(n):
                c, b = n % NB, n % 2
                own["zs_ready"].next()
                if n >= 2:
                    own["x_upd"].next()
                if n < n_solve - NB:
                    each(2 + b, xt[:, c, :], solve[:, b, :])
                each(4 + b, solve[:, b, :], xt[:, c, :]).then_inc(S["xz_done"], 1)

            for n in range(n_solve):
                if n < NB:
                    own["x_first"].next()
                else:
                    pe.wait_ge(S["x_upd"], n - NB + 1)
                own["bm_ready"].next()
                each(n % 2, solve[:, 2 + n % 2, :], xm[:, n % NB, :]).then_inc(S["zz_done"], 1)
                if n:
                    update(n - 1)
            update(n_solve - 1)
            own["x_upd"].next(2)
            own["qe_ready"].next()
            own["q_normed"].next()

            att = [sqt, rs]

            def within(c):
                if c:
                    own["at_ready"].next()
                for h in range(GDN_H):
                    m = M(aux[:, 2 * T + h * P:2 * T + (h + 1) * P], kf[:, h, c * P:(c + 1) * P],
                          qf[:, h, c * P:(c + 1) * P], start=True, stop=True)
                m.then_inc(S["qk_done"], 1)

            def w_turned(c):
                each(0, kb[:, c * T:(c + 1) * T], xt[:, c, :]).then_inc(S["wt_done"], 1)

            within(0)
            for c in range(NB):
                vn = solve[:, 2 + c % 2, :]
                if c == 0:
                    w_turned(1)
                if c:
                    own["nwt_ready"].next()
                    own["s_ready"].next()
                for h in range(GDN_H):
                    hh, out = slice(h * P, (h + 1) * P), aux[:, T + h * P:T + (h + 1) * P]
                    m = M(out, xt[:, c, hh], vb[:, c * T + h * P:c * T + (h + 1) * P], start=True, stop=c == 0)
                    if c:
                        m = M(out, solve[:, c % 2, hh], sqacc[:, hh], start=False, stop=True)
                m.then_inc(S["vnew_done"], 1)
                own["vnew_ready"].next()
                if c + 1 < NB:
                    pass
                if c == 0:
                    own["at_ready"].next()
                elif c < NB:
                    pe.wait_ge(S["at_ready"], c + 1)
                if c:
                    pe.wait_ge(S["o_ready"], c)
                for h in range(GDN_H):
                    hh, out = slice(h * P, (h + 1) * P), aux[:, 3 * T + h * P:3 * T + (h + 1) * P]
                    m = M(out, vn[:, hh], att[c % 2][:, hh], start=True, stop=c == 0)
                    if c:
                        m = M(out, sqacc[:, hh], egr[:, h, c * P:(c + 1) * P], start=False, stop=True)
                m.then_inc(S["o_done"], 1)
                if c + 1 < NB:
                    each(4, kdec[:, c * T:(c + 1) * T], vn).then_inc(S["s_done"], 1)
                    for h in range(GDN_H):
                        m = M(aux[:, 2 * T + h * P:2 * T + (h + 1) * P], kf[:, h, (c + 1) * P:(c + 2) * P],
                              qf[:, h, (c + 1) * P:(c + 2) * P], start=True, stop=True)
                    m.then_inc(S["qk_done"], 1)
                    if c:
                        w_turned(c + 1)

            own["osq_ready"].next()
            head_stats(lambda h: kdec[:, h * T:(h + 1) * T], "ostat_done")
            own["cf_dve"].next()
            own["cf_pool"].next()

            def long_stats(src, sem_):
                for k in range(CFM_T):
                    m = M(aux[:, 5 * T:6 * T], ones, src(k), start=k == 0, stop=k == CFM_T - 1)
                m.then_inc(S[sem_], 1)

            long_stats(lambda k: cfy[:, k, :], "cfsum_done")
            own["cfsq_ready"].next()
            long_stats(lambda k: kb[:, k * T:(k + 1) * T], "cfvar_done")
            own["x_ready"].next(KT)
            for n in range(4):
                tile(At(U0["mix_out"] + n), At(T0["mix_out"] + n), x_hi, x_lo)
            own["memsq_ready"].next()
            for k in range(KT):
                m = M(aux[:, 4 * T:4 * T + MEM], ones, msq[:, k * MEM:(k + 1) * MEM], start=k == 0, stop=k == KT - 1)
            m.then_inc(S["memstat_done"], 1)
            for n in range(4, 8):
                tile(At(U0["mix_out"] + n), At(T0["mix_out"] + n), x_hi, x_lo)
            stat()
            own["mem_ready"].next()
            for n in range(KT):
                tile(At(U0["kv"] + n), At(T0["kv"] + n), mem_hi, mem_lo, width=MEM)
            for half in range(2):
                token_tiles(At(U0["kv"] + 8 + 4 * half), (2 * half, 2 * half + 1), mem_hi, mem_lo)
            stat()
            own["x_ready"].next(KT)
            tiles("xq", KT, T0["xq"], x_hi, x_lo)

            own["km_ready"].next(KT)
            own["vm_ready"].next(4)
            own["qx_ready"].next(KT)

            def scores(h):
                if h >= 2:
                    own["px_ready"].next()
                b = (h % 2) * 2 * T
                for t in range(NB):
                    for k in range(2):
                        m = M(aux[:, b + t * MEM:b + (t + 1) * MEM], qx[:, 2 * h + k, t * P:(t + 1) * P],
                              kmt[:, 2 * h + k, :], start=k == 0, stop=k == 1)
                m.then_inc(S["xs_done"], 1)

            def attend(h):
                own["pxn_ready"].next()
                if h:
                    pe.wait_ge(S["pxt_ready"], h)
                for mt_ in range(2):
                    for t in range(NB):
                        m = nc.tensor.transpose(aux[:, (4 + mt_) * T + t * P:(4 + mt_) * T + (t + 1) * P],
                                                px[:, h % 2, t, mt_ * P:(mt_ + 1) * P], ident)
                m.then_inc(S["px_turned"], 1)
                own["pxt_ready"].next()
                for d in range(2):
                    t, k = At(T0["x_val"] + 2 * h + d), 2 * h + d
                    wait_bank(t)
                    for mt_ in range(2):
                        m = M(bank(t), vm[:, mt_, k * P:(k + 1) * P], pxt[:, h % 2, mt_ * T:(mt_ + 1) * T],
                              start=mt_ == 0, stop=mt_ == 1)
                    m.then_inc(S["tile_done"], 1)

            scores(0)
            scores(1)
            for h in range(XH):
                attend(h)
                if h + 2 < XH:
                    scores(h + 2)
            own["xo_ready"].next(KT)
            tiles("xo", KT, T0["xo"], xo_hi, xo_lo)
            stat()
            stat()
            own["x_ready"].next(KT)
            tiles("up", 2 * FT, T0["up"], x_hi, x_lo)
            down("down", T0["down"], g_hi, g_lo)
            stat()



def feature_units(w):
    k, n = w.shape
    return w.reshape(k // P, P, n // P, P).transpose(2, 1, 0, 3).reshape(n // P, P, k)


def token_units(w):
    k, n = w.shape
    return w.reshape(k // (2 * P), 2, P, n // T, T).transpose(3, 0, 2, 1, 4).reshape(-1, P, UNIT)


def zeros(n):
    return np.zeros((n, P, UNIT), np.float32)


def interleave(*parts):
    return np.stack(parts, 1).reshape(-1, P, UNIT)


def down_units(w):
    f = w.reshape(FT, P, KT, P).transpose(2, 0, 1, 3).reshape(2, 4 * FT // KT, KT, P, P).transpose(0, 1, 3, 2, 4)
    f = f.reshape(2, 4 * FT // KT, P, UNIT)
    return np.concatenate([f, np.zeros((2, 1, P, UNIT), np.float32)], 1).reshape(-1, P, UNIT)


def gdn_units(w):
    g = GDN_H * P
    q, k, v, gate = [w[:, n * g:(n + 1) * g] for n in range(4)]
    a, b, cfm = w[:, 4 * g:4 * g + 4], w[:, 4 * g + 4:4 * g + 8], w[:, 4 * g + 8:]
    ab = np.concatenate([a, np.zeros((D, 28), w.dtype), b, np.zeros((D, P - 36), w.dtype)], axis=1)
    half = CFM_T * P
    return np.concatenate([
        feature_units(ab), feature_units(k), feature_units(v), feature_units(q), feature_units(gate),
        interleave(feature_units(cfm[:, half:]), feature_units(cfm[:, :half])), zeros(3),
    ])


def tap_columns(w):
    return w.reshape(w.shape[0], -1, P).transpose(2, 1, 0).reshape(P, -1)


def few(v):
    return np.concatenate([v, np.zeros(P - len(v), v.dtype)])[:, None]


def halves_in_turn(v):
    return np.moveaxis(v.reshape(v.shape[:-1] + (2, FT, P)), -3, -2).reshape(v.shape)


def columns(v):
    return v.reshape(-1, P).T


def weight_stream(i):
    w_in = i["w_in"][0]
    sw, qw, vw = D, RET_H * RET_QT * P, RET_H * RET_VT * P
    cut = np.cumsum([0, sw, sw, sw, qw, qw, vw, vw, D, D])
    sq, sk, sv, rq, rk, rv, rg, b_sb, b_ret = [w_in[:, a:b] for a, b in zip(cut[:-1], cut[1:])]
    heads = []
    proj = i["w_proj_ret"][0].reshape(RET_H, RET_VT, P, KT // 2, 2, P).transpose(0, 3, 2, 4, 1, 5)
    for h in range(RET_H):
        q = slice(h * RET_QT * P, (h + 1) * RET_QT * P)
        v = slice(h * RET_VT * P, (h + 1) * RET_VT * P)
        heads += [feature_units(rq[:, q]), feature_units(rk[:, q]), token_units(rv[:, v]), feature_units(rg[:, v]),
                  proj[h].reshape(KT // 2, P, UNIT)]
    ff = i["w_ffn_in"][0]
    return {
        "sb_v": token_units(sv),
        "sb_qk": interleave(feature_units(sq), feature_units(sk)),
        "sb_out": interleave(feature_units(b_sb), feature_units(i["w_proj_sb"][0])),
        "ret": np.concatenate(heads),
        "merge": feature_units(b_ret),
        "out": feature_units(i["w_out"][0]),
        "ff_in": interleave(feature_units(ff[:, :D_FF]), feature_units(ff[:, D_FF:])),
        "ff_out": down_units(i["w_ffn_out"][0]),
        "gdn_in": gdn_units(i["w_in_2"][0]),
        "mix_out": feature_units(i["w_out_2"][0]),
        "kv": np.concatenate([feature_units(i["xa_w_kv_2"][0][:, :D]), token_units(i["xa_w_kv_2"][0][:, D:])]),
        "xq": feature_units(i["xa_w_q_2"][0]),
        "xo": feature_units(i["xa_w_o_2"][0]),
        "up": interleave(feature_units(i["ffn_w_up_2"][0][:, :D_FF]), feature_units(i["ffn_w_up_2"][0][:, D_FF:])),
        "down": down_units(i["ffn_w_down_2"][0]),
    }


def parameter_columns(i):
    return {
        "c": columns(i["c"][0]), "b_ada": columns(i["b_ada"][0]), "g_norm1": columns(i["g_norm1"][0]),
        "b_branch": columns(i["b_branch"][0]), "g_norm2": columns(i["g_norm2"][0]), "g_final": columns(i["g_final"]),
        "norm_g": columns(i["norm_g_2"][0].reshape(-1)), "mem_g": columns(i["mem_norm_g_2"][0]),
        "gdn_conv": tap_columns(np.concatenate(
            [i["gdn_conv_w_2"][0][:, n * GDN_H * P:(n + 1) * GDN_H * P] for n in (1, 2, 0)], axis=1)),
        "cfm_conv": tap_columns(i["cfm_dw_w_2"][0]), "cfm_b": columns(i["cfm_dw_b_2"][0]),
        "ln_g": columns(i["cfm_ln_g_2"][0]), "ln_b": columns(i["cfm_ln_b_2"][0]), "gdn_g": columns(i["gdn_norm_g_2"][0]),
        "a_log": few(i["gdn_a_log_2"][0]), "dt_bias": few(i["gdn_dt_bias_2"][0]),
        "ff_conv": tap_columns(halves_in_turn(i["ffn_conv_w_2"][0])),
        "ff_conv_b": columns(halves_in_turn(i["ffn_conv_b_2"][0])),
    }


def laid_out(i):
    stream, params = weight_stream(i), parameter_columns(i)
    assert [(n, len(stream[n])) for n, _ in PHASES] == PHASES
    assert [(n, params[n].shape[1]) for n, _ in COLS] == COLS
    tables, small, halves = shape_tables()
    ada = i["w_ada"][0].reshape(KT, P, N_MOD, D).transpose(2, 0, 1, 3).reshape(-1, P, UNIT)
    x = i["x"][0].T.reshape(KT, P, T).transpose(1, 0, 2)
    arrays = {
        "weights": np.concatenate([stream[n] for n, _ in PHASES]), "ada": ada,
        "cols": np.concatenate([params[n] for n, _ in COLS], 1), "small": small, "tables": tables, "x": x,
        "halves": halves.reshape(P, LEVELS, P), "mem": i["mem_2"][0].T.reshape(KT, P, MEM).transpose(1, 0, 2),
    }
    return {n: np.ascontiguousarray(a) for n, a in arrays.items()}


def kernel(**inputs):
    import concourse.bacc as bacc
    from concourse.bass_utils import run_bass_kernel_spmd as run

    nc = bacc.Bacc("TRN2", target_bir_lowering=False, num_devices=1)
    arrays = laid_out({n: np.asarray(a) for n, a in inputs.items()})
    dram = {n: nc.dram_tensor(f"in_{n}", a.shape, mybir.dt.from_np(a.dtype), kind="ExternalInput").ap()
            for n, a in arrays.items()}
    dram["out"] = nc.dram_tensor("out", (P, KT, T), F32, kind="ExternalOutput").ap()
    build_program(nc, dram)
    r = run(nc, [{f"in_{n}": a for n, a in arrays.items()}], core_ids=[0])
    out = r.results[0]["out"]
    return out.transpose(2, 1, 0).reshape(1, T, D)
```

```python
from contextlib import ExitStack, contextmanager

import numpy as np

import concourse.bass as bass
from concourse import mybir

F32 = mybir.dt.float32
F32R = mybir.dt.float32r
BF16 = mybir.dt.bfloat16
ALU = mybir.AluOpType
ACT = mybir.ActivationFunctionType
AX = mybir.AxisListType

P = 128
D = 1024
KT = D // P
T = 512
NB = T // P
EPS = 1e-6
UNIT = 1024
RING = 4
AHEAD = RING - 1

SB_DIM = 64
PAIRS = 8
RET_H = 4
RET_QT = 2
RET_VT = 4
D_FF = 2816
FT = D_FF // P
N_MOD = 6
NEG = -1e30

MEM = 256
GDN_H = 4
CONV_G = 4
CONV_C = 31
CONV_F = 3
XH = 4
CFM_T = 4
CFM_SHARED = 11
POOL_TAPS = [(n, j) for n in (CFM_T - 1, 1, 2) for j in range(CFM_SHARED if n == CFM_T - 1 else CONV_C)]
DVE_TAPS = [(n, j) for n in (0, CFM_T - 1) for j in range(CFM_SHARED if n else 0, CONV_C)]
X_MIX = 32

TRI_AT = (0, 512, 1024, 896)
TRI_W = tuple(T - P * j for j in range(NB))
TRI = sum(TRI_W)
TRI_ORDER = (0, 1, 3, 2)


class At:

    def __init__(self, c, i=None, m=0):
        self.c, self.i, self.m = c, i, m

    def __add__(self, k):
        return At(self.c + k, self.i, self.m)

    def val(self):
        return self.c if self.i is None else self.i * self.m + self.c

    def slot(self, n):
        assert self.m % n == 0
        return self.c % n

    def div(self, n):
        assert self.m % n == 0
        return At(self.c // n, self.i, self.m // n)


class Count:

    def __init__(self, eng, sem):
        self.eng, self.sem, self.at = eng, sem, At(0)

    def own(self, ins):
        ins.then_inc(self.sem, 1)
        self.at = self.at + 1
        self.eng.wait_ge(self.sem, self.at.val())

    def next(self, n=1):
        self.at = self.at + n
        self.eng.wait_ge(self.sem, self.at.val())

    def skip(self, n=1):
        self.at = self.at + n


@contextmanager
def loop(eng, n, counts):
    start = [c.at.c for c, _ in counts]
    with eng.Fori(0, n) as i:
        for (c, per), s in zip(counts, start):
            c.at = At(s, i, per)
        yield i
        for (c, per), s in zip(counts, start):
            assert c.at.c == s + per, (str(c.sem), c.at.c - s, per)
    for (c, per), s in zip(counts, start):
        c.at = At(s + n * per)


PHASES = [
    ("sb_v", 8), ("sb_qk", 16), ("sb_out", 16), ("ret", 64), ("merge", 8), ("out", 8),
    ("ff_in", 44), ("ff_out", 24),
    ("gdn_in", 28), ("mix_out", 8), ("kv", 16), ("xq", 8), ("xo", 8), ("up", 44), ("down", 24),
]
TILES = [
    ("first", 188), ("gdn_in", 25), ("turn", 4), ("mix_out", 8), ("kv", 8), ("xq", 8), ("x_val", 8), ("xo", 8),
    ("up", 44), ("down", 8),
]
AB, KVQ, GATE, CFM = 0, 1, 13, 17
LEVELS = 7
COLS = [
    ("c", 8), ("b_ada", 48), ("g_norm1", 8), ("b_branch", 16), ("g_norm2", 8), ("g_final", 8),
    ("norm_g", 48), ("mem_g", 8), ("gdn_conv", 3 * GDN_H * CONV_G), ("cfm_conv", CFM_T * CONV_C), ("cfm_b", CFM_T),
    ("ln_g", CFM_T), ("ln_b", CFM_T), ("gdn_g", 1), ("a_log", 1), ("dt_bias", 1),
    ("ff_conv", 2 * FT * CONV_F), ("ff_conv_b", 2 * FT),
]


def starts(table):
    out, at = {}, 0
    for name, n in table:
        out[name] = at
        at += n
    return out, at


U0, N_UNITS = starts(PHASES)
T0, _ = starts(TILES)
C0, N_COLS = starts(COLS)
SMALL = [("ones", P), ("ident", P), ("neg_tri", P), ("keep", P), ("tri", P)]
SM0, N_SMALL = starts(SMALL)


def shape_tables():
    f = np.float32
    qk = RET_QT * P
    inv = (f(10000.0) ** (-np.arange(0, qk, 2, dtype=f) / f(qk))).astype(f)
    ang = inv[:, None] * np.arange(T, dtype=f)[None, :]
    gamma = np.log(f(1.0) - f(2.0) ** (f(-5.0) - np.arange(RET_H, dtype=f))).astype(f)
    diff = (np.arange(T)[None, :] - np.arange(P)[:, None]).astype(f)
    decay = [np.where(diff >= 0, np.exp(np.maximum(diff, 0) * g), 0) * f(qk ** -0.5) for g in gamma]
    big = np.concatenate([np.cos(ang), np.sin(ang)] + decay, axis=1).astype(f)
    s, t = np.arange(P)[:, None], np.arange(P)[None, :]
    small = np.concatenate([
        np.ones((P, P)), s == t,
        -(s >= t).astype(f),
        (s < t).astype(f),
        (s <= t).astype(f),
    ], axis=1).astype(f)
    b = [s >> l for l in range(LEVELS)], [t >> l for l in range(LEVELS)]
    halves = np.concatenate([(ti % 2 == 1) & (si == ti - 1) for si, ti in zip(*b)], axis=1)
    return big, small, halves.astype(mybir.dt.np(BF16))


def build_program(nc, dram):
    ctx = ExitStack()
    with ctx:
        base = nc.sbuf_base
        at = [(base + 31) // 32 * 32]

        def put(name, shape, dt=F32, where=None):
            size = int(np.prod(shape[1:])) * (2 if dt == BF16 else 4)
            size = (size + 31) // 32 * 32
            offset = at[0] if where is None else where
            if where is None:
                at[0] += size
            return nc.alloc_sbuf_tensor_at(name, list(shape), dt, offset=offset), offset + size

        def fixed(name, shape, dt=F32):
            return put(name, shape, dt)[0]

        raw = [fixed(f"raw{s}", (P, UNIT)) for s in range(RING)]
        w_hi = [fixed(f"w_hi{s}", (P, UNIT), F32R) for s in range(RING)]
        w_lo = [fixed(f"w_lo{s}", (P, UNIT), F32R) for s in range(RING)]
        resid = fixed("resid", (P, KT, T))
        x_at = at[0]
        x_hi = fixed("x_hi", (P, KT, T), F32R)
        x_lo = fixed("x_lo", (P, KT, T), F32R)
        cols = fixed("cols", (P, N_COLS))
        small = fixed("small", (P, N_SMALL))
        mod = fixed("mod", (P, N_MOD * KT))
        gain1 = fixed("gain1", (P, KT))
        gain2 = fixed("gain2", (P, KT))
        c_act = fixed("c_act", (P, KT))
        eps = fixed("eps", (P, 1))
        negtri_r = fixed("negtri_r", (P, P), F32R)
        negone_r = fixed("negone_r", (P, P), F32R)
        ident_b = fixed("ident_b", (P, P), BF16)
        causal_b = fixed("causal_b", (P, P), BF16)
        halves = fixed("halves", (P, LEVELS, P), BF16)
        mask_b = fixed("mask_b", (P, P), BF16)
        rcol = fixed("rcol", (P, 32))
        spare = fixed("spare", (P, T))
        rs_sb = spare[:]
        norm_at = at[0]
        sqacc = fixed("sqacc", (P, T))
        sqt = fixed("sqt", (P, T))
        tn = fixed("tn", (P, 2, T))
        over = at[0]

        def overlay(start, *specs):
            out, o = [], start
            for name, shape, dt in specs:
                t, o = put(name, shape, dt, where=o)
                out.append(t)
            assert o <= nc.sbuf_usable_end, (specs, o - nc.sbuf_usable_end)
            return out, o

        gate_t = tn
        (ada0, adac0), _ = overlay(over, ("ada0", (P, 4, UNIT), F32), ("adac0", (P, 2, UNIT), F32))
        qk_at = [norm_at, norm_at + T * 4, norm_at + 2 * T * 4, norm_at + 3 * T * 4]
        qt_hi, qt_lo, kt_hi, kt_lo = [put(n, (P, T), F32R, where=o)[0]
                                      for n, o in zip(("qt_hi", "qt_lo", "kt_hi", "kt_lo"), qk_at)]
        vp = spare[:].rearrange("p (b n) -> p b n", b=NB)
        (osb_hi, osb_lo, v_sb, *pairbufs), _ = overlay(
            over, ("osb_hi", (P, PAIRS, T), F32R), ("osb_lo", (P, PAIRS, T), F32R),
            ("v_sb", (P, NB, D), F32),
            *[(f"{n}{h}", (P, TRI), d) for h in range(2)
              for n, d in (("sp", F32), ("sp_hi", F32R), ("sp_lo", F32R), ("prob", F32))])
        sp, sp_hi, sp_lo, prob = [pairbufs[n::4] for n in range(4)]
        o1 = over + 2 * PAIRS * T * 4
        (rq, rk, rv, rsc, oraw, decay), o2 = overlay(
            over, ("rq", (P, RET_QT, T), F32), ("rk", (P, RET_QT, T), F32), ("rv", (P, NB, T), F32),
            ("rsc", (P, TRI), F32), ("oraw", (P, RET_VT, T), F32),
            ("decay", (P, T), F32))
        assert o2 <= o1
        (msb, pret), o2 = overlay(o1, ("msb", (P, KT, T), F32), ("pret", (P, KT, T), F32))
        (orh, orl, angles, adac, ada1), _ = overlay(
            o2, ("orh", (P, RET_VT, T), F32R), ("orl", (P, RET_VT, T), F32R),
            ("angles", (P, 2 * T), F32), ("adac", (P, UNIT), F32), ("ada1", (P, UNIT), F32))
        cos, sin = angles[:, 0:T], angles[:, T:2 * T]
        (m_hi,), _ = overlay(over, ("m_hi", (P, KT, T), F32R))
        (m_lo, mt), _ = overlay(o2, ("m_lo", (P, KT, T), F32R), ("mt", (P, 2, T), F32))
        (ht, h_hi, h_lo), _ = overlay(
            over, ("ht", (P, 2, T), F32), ("h_hi", (P, FT, T), F32R), ("h_lo", (P, FT, T), F32R))

        (qkvf, sgate, cfin, cfy, gb, gbt, egr, kb, kdec, vb), o3 = overlay(
            over, ("qkvf", (P, 12, T), F32), ("sgate", (P, GDN_H, T), F32), ("cfin", (P, CFM_T, T + CONV_C - 1), F32),
            ("cfy", (P, CFM_T, T), F32), ("gb", (P, T), F32), ("gbt", (P, NB, 64), F32), ("egr", (P, GDN_H, T), F32),
            ("kb", (P, GDN_H * T), F32), ("kdec", (P, GDN_H * T), F32), ("vb", (P, GDN_H * T), F32))
        (solve, gcols), _ = overlay(o3, ("solve", (P, 4, T), F32), ("gcols", (P, 5, 16), F32))
        kf, vf, qf = qkvf[:, 0:4, :], qkvf[:, 4:8, :], qkvf[:, 8:12, :]
        (cin, abx), _ = overlay(o3, ("cin", (P, 2, T + CONV_G - 1), F32), ("abx", (P, T), F32))
        att = [sqt, spare]
        state = [sqacc[:], gb[:]]
        bm = [solve[:, 2, :], solve[:, 3, :], gb[:]]
        ngc, egc, bg, nega, egl = [gcols[:, n, :] for n in range(5)]
        abt = sgate[:, 0, :]
        (bt, xm, xt, dect), _ = overlay(x_at, *[(n, (P, NB, T), F32) for n in ("bt", "xm", "xt", "dect")])
        (memf, mem_hi, mem_lo, yv, kmt, vm, qx, px, pxt, xcols), _ = overlay(
            over, ("memf", (P, KT, MEM), F32), ("mem_hi", (P, KT, MEM), F32R), ("mem_lo", (P, KT, MEM), F32R),
            ("yv", (P, KT, T), F32), ("kmt", (P, KT, MEM), F32), ("vm", (P, 2, D), F32), ("qx", (P, KT, T), F32),
            ("px", (P, 2, NB, MEM), F32), ("pxt", (P, 2, 2 * T), F32), ("xcols", (P, 2, 3, NB), F32))
        (xo_hi, xo_lo, yv_o), _ = overlay(over, ("xo_hi", (P, KT, T), F32R), ("xo_lo", (P, KT, T), F32R),
                                          ("yv_o", (P, KT, T), F32))
        msq = qx[:, 0:4, :].rearrange("p k n -> p (k n)")
        ht2 = sqt
        (g_hi, g_lo, fin), _ = overlay(
            over, ("g_hi", (P, FT, T), F32R), ("g_lo", (P, FT, T), F32R),
            ("fin", (P, 2, T + CONV_F - 1), F32))
        (yv2,), _ = overlay(x_at, ("yv2", (P, KT, T), F32))

        acc = ctx.enter_context(nc.psum_tensor("acc", [P, 2 * T], F32))
        aux = ctx.enter_context(nc.psum_tensor("aux", [P, 6 * T], F32))
        rs = aux[:, 5 * T:6 * T]

        def bank(t):
            b = t.slot(2)
            return acc[:, b * T:(b + 1) * T]

        def sem(name):
            return ctx.enter_context(nc.semaphore(name))

        raw_loaded = [sem(f"raw_loaded{s}") for s in range(RING)]
        hi_ready, lo_ready, unit_used = sem("hi_ready"), sem("lo_ready"), sem("unit_used")
        acc_free = [sem("acc_free0"), sem("acc_free1")]
        S = {n: sem(n) for n in (
            "dve_step", "act_step", "pool_step",
            "decay_free", "decay_loaded", "consts_loaded", "x_loaded", "tables_loaded", "consts_ready", "stored",
            "ada0_loaded0", "ada0_loaded1", "ada0_loaded2", "ada0_loaded3", "ada1_loaded", "ada_used",
            "ada_ready", "c_ready_act",
            "sq_ready", "stat_ready", "root_ready", "recip_ready", "rs_ready", "res_ready", "rsq_ready", "rsq_used",
            "hs_ready", "hrecip_ready", "glogit_ready", "tap_ready", "tap_used", "normed", "norm_hi", "x_ready",
            "v_ready", "z_ready", "log_ready", "sp_ready", "sp_hi_ready", "sp_split",
            "log_a_ready", "prob_ready", "qk_hi_ready", "qk_ready", "vp_ready", "tile_done", "osb_hi_ready", "osb_ready",
            "gate_ready", "msb_ready", "qk_rot", "rv_ready", "rsc_done", "rsc_ready", "oraw_ready",
            "oprod_ready", "orh_ready", "or_ready", "merged_f", "merged_hi", "merged",
            "resid_ready", "hidden_f", "hidden_hi", "hidden",
            "mem_loaded", "nega_ready", "ab_ready", "gb_ready", "gb_turned", "gbt_ready", "gc_done", "egc_ready", "gc_seen",
            "conv_ready", "kvq_ready", "gsq_ready", "gstat_done", "groot_ready", "k_normed", "q_normed",
            "sgate_ready", "cfin_ready", "gc_row", "egr_ready", "gc_masked", "dec_ready", "beta_row", "kb_ready",
            "kk_done", "xt_ready", "x_turned", "x_first", "kv_turned", "kv_token", "bm_ready", "zz_done", "zs_ready",
            "xz_done", "x_upd", "qk_done", "at_ready", "wt_done", "nwt_ready", "vnew_done", "vnew_ready", "o_done",
            "o_ready", "s_done", "s_ready", "qe_ready", "cf_pool", "cf_dve", "cfsum_done", "cfc_ready", "cfsq_ready",
            "cfn_ready", "osq_ready", "ostat_done", "on_ready", "gdn_over",
            "memsq_ready", "memstat_done", "memroot_ready", "memn_ready", "mem_hi_ready", "mem_ready",
            "km_ready", "vm_ready", "qx_ready", "xs_done", "xmax_ready", "px_ready", "pxn_ready", "px_turned",
            "pxt_ready", "xo_hi_ready", "xo_ready", "conv2_ready", "silu2_ready",
        )}

        NU = N_UNITS
        SC = SB_DIM ** -0.5
        block = ctx.enter_context(nc.Block())

        @block.sync
        def _(sp_):
            def load(u):
                s = u.slot(RING)
                if u.i is not None or u.c >= RING:
                    sp_.wait_ge(lo_ready, (u + (1 - RING)).val())
                if u.i is None:
                    src = dram["weights"][u.c]
                else:
                    src = dram["weights"][bass.ds(u.val(), 1), :, :].rearrange("a p n -> (a p) n")
                sp_.dma_start(raw[s][:], src).then_inc(raw_loaded[s], 16)

            sp_.dma_start(cols[:], dram["cols"]).then_inc(S["consts_loaded"], 16)
            sp_.dma_start(small[:], dram["small"]).then_inc(S["consts_loaded"], 16)
            sp_.dma_start(halves[:], dram["halves"]).then_inc(S["consts_loaded"], 16)
            for n in range(16):
                if n >= 4:
                    sp_.wait_ge(S["ada_used"], n - 3)
                sp_.dma_start(ada0[:, n % 4, :], dram["ada"][n]).then_inc(S[f"ada0_loaded{n % 4}"], 16)
                if n == 3:
                    sp_.dma_start(resid[:], dram["x"]).then_inc(S["x_loaded"], 16)
            for u in range(RING):
                load(At(u))
            def load_units(first, end):
                with sp_.Fori(0, (end - first) // 4) as i:
                    for j in range(4):
                        load(At(first + j, i, 4))

            load_units(RING, U0["sb_out"] + 4)
            sp_.wait_ge(S["osb_ready"], PAIRS)
            sp_.dma_start(angles[:], dram["tables"][:, 0:2 * T]).then_inc(S["tables_loaded"], 16)
            load_units(U0["sb_out"] + 4, U0["ret"])
            with sp_.Fori(0, RET_H) as i:
                for j in range(16):
                    if 6 <= j < 14:
                        n = At(2 * KT + j - 6, i, 8)
                        sp_.wait_ge(S["ada_used"], n.val())
                        sp_.dma_start(ada1[:], dram["ada"][bass.ds(n.val(), 1), :, :]
                                      .rearrange("a p n -> (a p) n")).then_inc(S["ada1_loaded"], 16)
                    load(At(U0["ret"] + j, i, 16))
                    if j == 3:
                        sp_.wait_ge(S["decay_free"], i + 1)
                        sp_.dma_start(decay[:], dram["tables"][:, bass.ds(i * T + 2 * T, T)]
                                      ).then_inc(S["decay_loaded"], 16)
            rest = U0["ret"] + 64
            load_units(rest, U0["mix_out"] + 4)
            sp_.wait_ge(S["gdn_over"], 1)
            sp_.wait_ge(S["x_ready"], X_MIX)
            sp_.dma_start(memf[:], dram["mem"]).then_inc(S["mem_loaded"], 16)
            load_units(U0["mix_out"] + 4, NU)
            for k in range(KT):
                sp_.wait_ge(S["resid_ready"], k + 1)
                sp_.dma_start(dram["out"][:, k, :], resid[:, k, :]).then_inc(S["stored"], 16)
            sp_.wait_ge(S["stored"], 16 * KT)

        @block.gpsimd
        def _(pool):
            step = Count(pool, S["pool_step"])
            rsq, used = Count(pool, S["rsq_ready"]), Count(pool, S["rsq_used"])

            def add_square(k):
                rsq.next()
                if k:
                    used.own(nc.gpsimd.tensor_tensor(sqacc[:], sqacc[:], tn[:, k % 2, :], ALU.add))
                if k == KT - 1:
                    pool.sem_inc(S["sq_ready"], 1)

            def add_squares():
                for k in range(KT):
                    add_square(k)

            add_squares()

            def split_lo(u):
                s = u.slot(RING)
                pool.wait_ge(hi_ready, (u + 1).val())
                nc.gpsimd.tensor_tensor(w_lo[s][:], raw[s][:], w_hi[s][:].bitcast(F32),
                                        ALU.subtract).then_inc(lo_ready, 1)

            def split_units(first, end):
                with pool.Fori(0, (end - first) // RING) as i:
                    for j in range(RING):
                        split_lo(At(first + j, i, RING))

            split_units(0, U0["gdn_in"])

            def next_phase(first, end):
                for j in range(AHEAD):
                    split_lo(At(first + j))
                add_squares()
                split_lo(At(first + AHEAD))
                split_units(first + RING, end)

            next_phase(U0["gdn_in"], U0["mix_out"])
            tap_used = Count(pool, S["tap_used"])
            for m, (n, j) in enumerate(POOL_TAPS):
                if j:
                    pool.wait_ge(S["tap_ready"], m + 1)
                    tap_used.own(nc.gpsimd.tensor_tensor(cfy[:, n, :], cfy[:, n, :], tn[:, tap_used.at.c % 2, :],
                                                         ALU.add))
            pool.sem_inc(S["cf_pool"], 1)
            split_units(U0["mix_out"], U0["kv"])
            for j in range(AHEAD):
                split_lo(At(U0["kv"] + j))
            for k in range(KT):
                split_lo(At(U0["kv"] + AHEAD + k))
                if k:
                    add_square(k - 1)
            split_lo(At(U0["kv"] + AHEAD + KT))
            add_square(KT - 1)
            split_units(U0["kv"] + AHEAD + KT + 1, U0["up"])
            next_phase(U0["up"], NU)

        @block.scalar
        def _(act):
            step = Count(act, S["act_step"])
            own = {n: Count(act, S[n]) for n in S}

            def f(out, in_, func=ACT.Copy, **kw):
                return nc.scalar.activation(out, in_, func, **kw)

            def split_hi(u):
                if u.i is None and u.c >= NU:
                    return
                s = u.slot(RING)
                act.wait_ge(raw_loaded[s], (u.div(RING).val() + 1) * 16)
                if u.i is not None or u.c >= RING:
                    act.wait_ge(unit_used, (u + (1 - RING)).val())
                f(w_hi[s][:], raw[s][:]).then_inc(hi_ready, 1)

            def root(scale):
                own["stat_ready"].next()
                own["root_ready"].own(f(rcol[:, 0:NB], rs[:, 0:NB], ACT.Sqrt, scale=scale, bias=eps[:, 0:1]))

            def norm_hi(shift):
                for k in range(KT):
                    own["normed"].next()
                    own["norm_hi"].own(f(x_hi[:, k, :], tn[:, k % 2, :], ACT.Identity,
                                         bias=mod[:, shift * KT + k:shift * KT + k + 1]))

            def square_tile(k):
                if k >= 3:
                    own["rsq_used"].next()
                own["rsq_ready"].own(f(tn[:, k % 2, :] if k else sqacc[:], resid[:, k, :], ACT.Square))

            def scaled_tile(k, gain):
                own["res_ready"].next()
                own["norm_hi"].own(f(x_hi[:, k, :], resid[:, k, :], scale=gain[:, k:k + 1]))
                square_tile(k)
                if k == KT - 1:
                    own["rsq_used"].next(2)

            def scaled_hi(gain):
                for k in range(KT):
                    scaled_tile(k, gain)

            act.wait_ge(S["consts_loaded"], 48)
            own["c_ready_act"].own(f(c_act[:], cols[:, C0["c"]:C0["c"] + KT], ACT.Silu))
            act.wait_ge(S["x_loaded"], 16)
            for k in range(KT):
                square_tile(k)
            own["rsq_used"].next(2)
            own["consts_ready"].next(6)
            root(1.0 / D)
            for u in range(AHEAD):
                split_hi(At(u))
            norm_hi(0)

            for half in range(2):
                for j in range(4):
                    split_hi(At(4 * half + j + AHEAD))
                act.wait_ge(unit_used, 4 * half + 4)
                for b in range(NB):
                    bk = (4 * half + b) % 6
                    own["v_ready"].own(f(v_sb[:, b, half * T:(half + 1) * T], aux[:, bk * T:(bk + 1) * T]))

            nc.scalar.preload_act_table_set("natural_log_exp_and_others")
            u, t = At(U0["sb_qk"]), At(0)

            def qk_tile(u, t, dst, scale):
                split_hi(u + AHEAD)
                act.wait_ge(unit_used, (u + 1).val())
                own["qk_hi_ready"].own(f(dst[:], bank(t), scale=scale))

            qk_tile(u, At(0), qt_hi, SC)
            qk_tile(u + 1, At(1), kt_hi, 1.0)

            def pair(u, t, first, last, p):
                def exp(h):
                    own["z_ready"].next()
                    step.own(f(sp[h][:], aux[:, 3 * T * h:3 * T * h + TRI], ACT.Abs))
                    step.own(f(sp[h][:], sp[h][:], ACT.Exp, scale=-1.0))

                def log(h):
                    own["log_ready"].own(f(sp[h][:], sp[h][:], ACT.Ln, bias=1.0))

                def high(h):
                    own["sp_ready"].next()
                    own["sp_hi_ready"].own(f(sp_hi[h][:], sp[h][:]))

                exp(0)
                log(0)
                exp(1)
                if not first:
                    own["tile_done"].next()
                    own["osb_hi_ready"].own(f(osb_hi[:, p - 1, :] if t.i is None else
                                              osb_hi[:, bass.ds(p - 1, 1), :].rearrange("p a n -> p (a n)"), bank(t)))
                    t = t + 1
                high(0)
                log(1)
                high(1)
                if not last:
                    qk_tile(u, t, qt_hi, SC)
                own["log_a_ready"].next()
                own["prob_ready"].own(f(prob[0][:], aux[:, 0:TRI], ACT.Exp))
                if not last:
                    qk_tile(u + 1, t + 1, kt_hi, 1.0)
                own["log_a_ready"].next()
                own["prob_ready"].own(f(prob[1][:], aux[:, 3 * T:3 * T + TRI], ACT.Exp))

            pair(u + 2, At(2), True, False, 0)
            with loop(act, 3, [(step, 8), (own["z_ready"], 4), (own["log_ready"], 4), (own["sp_ready"], 4),
                               (own["sp_hi_ready"], 4), (own["tile_done"], 2), (own["osb_hi_ready"], 2),
                               (own["log_a_ready"], 4), (own["prob_ready"], 4), (own["qk_hi_ready"], 4)]) as i:
                for s in range(2):
                    pair(At(U0["sb_qk"] + 4 + 2 * s, i, 4), At(4 + 3 * s, i, 6), False, False, i * 2 + 1 + s)
            pair(None, At(22), False, True, 7)

            def sb_gate(u, t, n, k):
                split_hi(u + AHEAD)
                act.wait_ge(unit_used, (u + 1).val())
                own["gate_ready"].own(f(gate_t[:, n, :], bank(t), ACT.Sigmoid,
                                        bias=cols[:, bass.ds(k + C0["b_branch"], 1)]))
                nc.scalar.sem_inc(acc_free[t.slot(2)], 1)

            sb_gate(At(U0["sb_out"]), At(23), 0, 0)
            own["tile_done"].next()
            own["osb_hi_ready"].own(f(osb_hi[:, PAIRS - 1, :], bank(At(24))))
            sb_gate(At(U0["sb_out"] + 1), At(25), 1, 1)
            for n in range(2):
                split_hi(At(U0["sb_out"] + 2 + n + AHEAD))
            with loop(act, 3, [(own["gate_ready"], 2)]) as i:
                for n in range(2):
                    sb_gate(At(U0["sb_out"] + 4 + n, i, 4), At(28 + n, i, 4), n, i * 2 + (2 + n))
                for n in range(2):
                    split_hi(At(U0["sb_out"] + 6 + n + AHEAD, i, 4))

            with loop(act, RET_H, [(own["rv_ready"], 4), (own["tile_done"], 8), (own["oraw_ready"], 4),
                                   (own["stat_ready"], 1), (own["root_ready"], 1), (own["gate_ready"], 4),
                                   (own["oprod_ready"], 4), (own["orh_ready"], 4)]) as i:
                u0 = At(U0["ret"], i, 16)
                for j in range(8):
                    split_hi(u0 + j + AHEAD)
                act.wait_ge(unit_used, (u0 + 8).val())
                for b in range(NB):
                    own["rv_ready"].own(f(rv[:, b, :], aux[:, (2 + b) * T:(3 + b) * T]))

                def gate(e):
                    split_hi(u0 + 8 + e + AHEAD)
                    act.wait_ge(unit_used, (u0 + 8 + e + 1).val())
                    own["gate_ready"].own(f(gate_t[:, e % 2, :], bank(At(e)), ACT.Silu))
                    nc.scalar.sem_inc(acc_free[e % 2], 1)

                def product_hi(e):
                    own["oprod_ready"].next()
                    own["orh_ready"].own(f(orh[:, e, :], oraw[:, e, :]))

                gate(0)
                gate(1)
                for e in range(RET_VT):
                    own["tile_done"].next()
                    own["oraw_ready"].own(f(oraw[:, e, :], bank(At(e))))
                    nc.scalar.sem_inc(acc_free[e % 2], 1)
                product_hi(0)
                product_hi(1)
                gate(2)
                root(1.0 / (RET_VT * P))
                product_hi(2)
                gate(3)
                product_hi(3)
                own["tile_done"].skip(4)
                for j in range(4):
                    split_hi(u0 + 12 + j + AHEAD)

            with loop(act, 2, [(own["gate_ready"], 4), (own["merged_f"], 4), (own["merged_hi"], 4)]) as i:
                for n in range(4):
                    u = At(U0["merge"] + n, i, 4)
                    split_hi(u + AHEAD)
                    act.wait_ge(unit_used, (u + 1).val())
                    own["gate_ready"].own(f(gate_t[:, n % 2, :], bank(At(n)), ACT.Sigmoid,
                                            bias=cols[:, bass.ds(i * 4 + (C0["b_branch"] + KT + n), 1)]))
                    nc.scalar.sem_inc(acc_free[n % 2], 1)
                    own["merged_f"].next()
                    own["merged_hi"].own(f(m_hi[:, bass.ds(i * 4 + n, 1), :].rearrange("p a n -> p (a n)"),
                                           mt[:, n % 2, :]))
            with act.Fori(0, 2) as i:
                for n in range(4):
                    split_hi(At(U0["out"] + n + AHEAD, i, 4))
            root(1.0 / D)
            norm_hi(3)

            with loop(act, FT // 2, [(own["gate_ready"], 2), (own["hidden_f"], 2), (own["hidden_hi"], 2)]) as i:
                for n in range(2):
                    u, t = At(U0["ff_in"] + 2 * n, i, 4), At(2 * n)
                    split_hi(u + AHEAD)
                    act.wait_ge(unit_used, (u + 1).val())
                    own["gate_ready"].own(f(gate_t[:, n, :], bank(t), ACT.Silu))
                    nc.scalar.sem_inc(acc_free[t.slot(2)], 1)
                    split_hi(u + 1 + AHEAD)
                    own["hidden_f"].next()
                    own["hidden_hi"].own(f(h_hi[:, bass.ds(i * 2 + n, 1), :].rearrange("p a n -> p (a n)"),
                                           ht[:, n, :]))
            for u in range(U0["ff_out"], U0["ff_out"] + 24):
                split_hi(At(u + AHEAD))
            root(1.0 / D)
            own["nega_ready"].own(f(nega[0:GDN_H, 0:1], cols[0:GDN_H, C0["a_log"]:C0["a_log"] + 1], ACT.Exp))
            norm_g = [cols[:, C0["norm_g"] + n * KT:C0["norm_g"] + (n + 1) * KT] for n in range(6)]
            scaled_hi(norm_g[0])
            root(1.0 / D)
            g0, t0 = At(U0["gdn_in"]), At(T0["gdn_in"])

            def free(t):
                nc.scalar.sem_inc(acc_free[t.slot(2)], 1)

            for j in range(2):
                split_hi(g0 + j + AHEAD)
            own["glogit_ready"].next()
            dt = cols[0:GDN_H, C0["dt_bias"]:C0["dt_bias"] + 1]
            step.own(f(gb[32:32 + GDN_H, :], tn[32:32 + GDN_H, 1, :], ACT.Sigmoid))
            step.own(f(abx[0:GDN_H, :], tn[0:GDN_H, 1, :], ACT.Identity, bias=dt))
            step.own(f(abt[0:GDN_H, :], tn[0:GDN_H, 1, :], ACT.Abs, bias=dt))
            step.own(f(abt[0:GDN_H, :], abt[0:GDN_H, :], ACT.Exp, scale=-1.0))
            own["ab_ready"].own(f(abt[0:GDN_H, :], abt[0:GDN_H, :], ACT.Ln, bias=1.0))

            nc.scalar.sem_inc(S["kvq_ready"], 2)
            own["kvq_ready"].skip(2)
            with loop(act, 3, [(own["conv_ready"], 4), (own["kvq_ready"], 4)]) as i:
                for n in range(4):
                    split_hi(At(U0["gdn_in"] + 1 + KVQ + n + AHEAD, i, 4))
                    own["conv_ready"].next()
                    own["kvq_ready"].own(f(qkvf[:, bass.ds(i * 4 + n, 1), :].rearrange("p a n -> p (a n)"),
                                           tn[:, n % 2, :], ACT.Silu))

            def flat(x):
                return x.rearrange("p k n -> p (k n)")

            own["gsq_ready"].own(f(kdec[:], flat(kf), ACT.Square))
            own["gsq_ready"].own(f(vb[:], flat(qf), ACT.Square))
            for n in range(GDN_H):
                split_hi(g0 + GATE + n + 1 + AHEAD)
                own["glogit_ready"].next()
                own["sgate_ready"].own(f(sgate[:, n, :], tn[:, n % 2, :], ACT.Silu))
            own["gstat_done"].next()
            own["groot_ready"].own(f(rcol[:], aux[:, 4 * T:4 * T + 32], ACT.Sqrt, bias=eps[:, 0:1]))

            def cfm_gate(n):
                split_hi(g0 + CFM + 2 * n + 1 + AHEAD)
                own["glogit_ready"].next()
                own["gate_ready"].own(f(gate_t[:, n % 2, :], gate_t[:, n % 2, :], ACT.Sigmoid))
                if n < 3:
                    split_hi(g0 + CFM + 2 * n + 2 + AHEAD)

            for n in range(3):
                cfm_gate(n)
            own["gc_done"].next()
            own["egc_ready"].own(f(egc[:], aux[:, 4 * T + 32:4 * T + 48], ACT.Exp))
            cfm_gate(3)
            for j in range(25, 28):
                split_hi(g0 + j + AHEAD)

            def rows(c):
                b = 3 * (c % 2)
                own["gc_row"].next()
                own["egr_ready"].own(f(egr[:, :, c * P:(c + 1) * P],
                                       aux[:, b * T:(b + 1) * T].rearrange("p (h n) -> p h n", h=GDN_H), ACT.Exp))

            def decays(c):
                b = 3 * (c % 2)
                own["gc_masked"].next()
                for h in range(GDN_H):
                    ins = f(dect[:, c, h * P:(h + 1) * P], aux[:, b * T + h * P:b * T + (h + 1) * P], ACT.Exp,
                            bias=ngc[:, c * 4 + h:c * 4 + h + 1])
                    (step if h < 3 else own["dec_ready"]).own(ins)

            def first_inverse(c):
                own["x_turned"].next()
                own["x_first"].own(f(xm[:, c, :], bank(At(T0["turn"] + c))))
                free(At(T0["turn"] + c))

            taps, made = list(POOL_TAPS), [0]

            def cfm_taps(m):
                for _ in range(min(m, len(taps))):
                    n, j = taps.pop(0)
                    x, w = cfin[:, n, j:j + T], cols[:, C0["cfm_conv"] + n * CONV_C + j:C0["cfm_conv"] + n * CONV_C + j + 1]
                    if j == 0:
                        own["tap_ready"].own(f(cfy[:, n, :], x, ACT.Identity, scale=w,
                                               bias=cols[:, C0["cfm_b"] + n:C0["cfm_b"] + n + 1]))
                        continue
                    if made[0] >= 2:
                        act.wait_ge(S["tap_used"], made[0] - 1)
                    own["tap_ready"].own(f(tn[:, made[0] % 2, :], x, scale=w))
                    made[0] += 1

            own["gc_seen"].next()
            rows(0)
            rows(1)
            act.wait_ge(S["cfin_ready"], CFM_T)
            cfm_taps(2)
            for c in range(0, NB, 2):
                decays(c)
                decays(c + 1)
                cfm_taps(3)
                for d in range(2):
                    if c + d + 2 < NB:
                        rows(c + d + 2)
                    first_inverse(c + d)
            cfm_taps(8)

            zs = [solve[:, n, :] for n in range(2)]
            for n in range((LEVELS - 1) * NB):
                own["zz_done"].next()
                own["zs_ready"].own(f(zs[n % 2], aux[:, (n % 2) * T:(n % 2 + 1) * T]))
                cfm_taps(2)

            def w_turned(c):
                own["wt_done"].next()
                own["nwt_ready"].own(f(solve[:, c % 2, :], aux[:, 0:T], scale=-1.0))

            for c in range(NB):
                own["vnew_done"].next()
                own["vnew_ready"].own(f(solve[:, 2 + c % 2, :], aux[:, T:2 * T]))
                if c + 1 < NB:
                    w_turned(c + 1)
                cfm_taps(1)
                own["o_done"].next()
                own["o_ready"].own(f(vf[:, :, c * P:(c + 1) * P],
                                     aux[:, 3 * T:4 * T].rearrange("p (h n) -> p h n", h=GDN_H)))
                cfm_taps(2)

            own["osq_ready"].own(f(kdec[:], flat(vf), ACT.Square))
            cfm_taps(len(taps))
            own["ostat_done"].next()
            own["groot_ready"].own(f(rcol[:, 0:16], aux[:, 4 * T:4 * T + 16], ACT.Sqrt, bias=eps[:, 0:1], scale=1.0 / P))
            own["cfc_ready"].next()
            own["cfsq_ready"].own(f(kb[:], flat(cfy[:, :, :]), ACT.Square))
            for k in range(GDN_H):
                if k == 2:
                    root(1.0 / (CFM_T * P))
                own["on_ready"].next()
                own["norm_hi"].own(f(x_hi[:, k, :], vf[:, k, :]))
            for k in range(CFM_T):
                own["cfn_ready"].next()
                step.own(f(cfy[:, k, :], cfy[:, k, :], ACT.Silu, bias=cols[:, C0["ln_b"] + k:C0["ln_b"] + k + 1]))
                own["norm_hi"].own(f(x_hi[:, GDN_H + k, :], cfy[:, k, :]))

            split_hi(At(U0["mix_out"] + AHEAD))
            act.wait_ge(S["mem_loaded"], 16)
            own["memsq_ready"].own(f(msq, flat(memf[:, :, :]), ACT.Square))
            for n in range(1, 4):
                split_hi(At(U0["mix_out"] + n + AHEAD))
            own["memstat_done"].next()
            own["memroot_ready"].own(f(rcol[:, 0:2], aux[:, 4 * T:4 * T + 2], ACT.Sqrt, scale=1.0 / D, bias=eps[:, 0:1]))
            for n in range(4, 6):
                split_hi(At(U0["mix_out"] + n + AHEAD))
            own["memn_ready"].next()
            own["mem_hi_ready"].own(f(mem_hi[:], memf[:]))
            for n in range(6, 8):
                split_hi(At(U0["mix_out"] + n + AHEAD))
            root(1.0 / D)

            for n in range(KT):
                u, t = At(U0["kv"] + n), At(T0["kv"] + n)
                split_hi(u + AHEAD)
                act.wait_ge(unit_used, (u + 1).val())
                own["km_ready"].own(f(kmt[:, n, :], bank(t)[:, 0:MEM]))
                free(t)
                if n:
                    scaled_tile(n - 1, norm_g[2])
            for half in range(2):
                for j in range(4):
                    split_hi(At(U0["kv"] + 8 + 4 * half + j + AHEAD))
                    if half == 0 and j == 0:
                        scaled_tile(KT - 1, norm_g[2])
                if half:
                    root(1.0 / D)
                act.wait_ge(unit_used, U0["kv"] + 12 + 4 * half)
                for b in range(2):
                    bk = 2 * half + b
                    own["vm_ready"].own(f(vm[:, b, half * T:(half + 1) * T], aux[:, bk * T:(bk + 1) * T]))
            for n in range(KT):
                split_hi(At(U0["xq"] + n + AHEAD))

            XSC = (KT // XH * P) ** -0.5

            def exps(h):
                own["xmax_ready"].next()
                for t in range(NB):
                    ins = f(px[:, h % 2, t, :], aux[:, (h % 2) * 2 * T + t * MEM:(h % 2) * 2 * T + (t + 1) * MEM], ACT.Exp,
                            scale=XSC, bias=xcols[:, h % 2, 0, t:t + 1], accum_out=xcols[:, h % 2, 1, t:t + 1])
                    (step if t < NB - 1 else own["px_ready"]).own(ins)

            own["tile_done"].skip(6)
            exps(0)
            for h in range(XH):
                own["px_turned"].next()
                own["pxt_ready"].own(f(pxt[:, h % 2, :], aux[:, 4 * T:6 * T]))
                if h + 1 < XH:
                    exps(h + 1)
                for d in range(2):
                    t = At(T0["x_val"] + 2 * h + d)
                    own["tile_done"].next()
                    own["xo_hi_ready"].own(f(xo_hi[:, 2 * h + d, :], bank(t)))
            for n in range(8):
                split_hi(At(U0["xo"] + n + AHEAD))
            root(1.0 / D)
            scaled_hi(norm_g[4])
            root(1.0 / D)

            with loop(act, FT // 2, [(own["conv2_ready"], 4), (own["silu2_ready"], 2),
                                     (own["hidden_f"], 2), (own["hidden_hi"], 2)]) as i:
                for n in range(2):
                    for m in range(2):
                        split_hi(At(U0["up"] + 2 * n + m + AHEAD, i, 4))
                    own["conv2_ready"].next()
                    own["silu2_ready"].own(f(tn[:, 0, :], tn[:, 0, :], ACT.Silu))
                    own["conv2_ready"].next()
                    own["hidden_f"].next()
                    own["hidden_hi"].own(f(g_hi[:, bass.ds(i * 2 + n, 1), :].rearrange("p a n -> p (a n)"), ht2[:]))
            for u in range(U0["down"], U0["down"] + 24):
                split_hi(At(u + AHEAD))
            root(1.0 / D)

        @block.vector
        def _(dve):
            own = {n: Count(dve, S[n]) for n in S}
            step = own["dve_step"]
            V = nc.vector

            def col(name, k):
                return cols[:, bass.ds(k + C0[name], 1)]

            def free(t):
                V.sem_inc(acc_free[t.slot(2)], 1)

            def at_tile(buf, k):
                return buf[:, bass.ds(k, 1), :].rearrange("p a n -> p (a n)")

            def take_rs():
                own["rs_ready"].next()
                step.own(V.tensor_copy(rs_sb, rs))

            def evict(dst, t, end=None):
                (end or step).own(V.tensor_tensor(dst, bank(t), rs_sb, ALU.mult))
                free(t)

            dve.wait_ge(S["consts_loaded"], 48)
            sm = {n: small[:, SM0[n]:SM0[n] + P] for n, _ in SMALL}
            ready = own["consts_ready"]
            ready.own(V.memset(eps[:], EPS))
            ready.own(V.tensor_copy(negtri_r[:], sm["neg_tri"]))
            ready.own(V.tensor_scalar(negone_r[:], sm["ones"], -1.0, None, ALU.mult))
            ready.own(V.tensor_copy(ident_b[:], sm["ident"]))
            ready.own(V.tensor_scalar(mask_b[:], sm["keep"], -NEG, NEG, ALU.mult, ALU.add))
            ready.own(V.tensor_scalar(causal_b[:], sm["tri"], -NEG, NEG, ALU.mult, ALU.add))

            def ada(w, dst, k):
                c = c_act[:, k:k + 1]
                if k == 0:
                    return V.tensor_scalar(dst[:], w, c, None, ALU.mult)
                return V.scalar_tensor_tensor(dst[:], w, c, dst[:], ALU.mult, ALU.add)

            def invert():
                own["root_ready"].next()
                own["recip_ready"].own(V.reciprocal(rcol[:, 0:NB], rcol[:, 0:NB]))

            own["c_ready_act"].next()
            for m in range(2):
                for k in range(KT):
                    n = m * KT + k
                    dve.wait_ge(S[f"ada0_loaded{n % 4}"], 16 * (n // 4 + 1))
                    own["ada_used"].own(ada(ada0[:, n % 4, :], adac0[:, m, :], k))
                    if n == 2 * KT - 3:
                        invert()

            own["ada_ready"].next(2)
            step.own(V.tensor_tensor(mod[:, 0:2 * KT], aux[:, 4 * T:4 * T + 2 * KT],
                                     cols[:, C0["b_ada"]:C0["b_ada"] + 2 * KT], ALU.add))
            step.own(V.scalar_tensor_tensor(gain1[:], mod[:, KT:2 * KT], 1.0,
                                            cols[:, C0["g_norm1"]:C0["g_norm1"] + KT], ALU.add, ALU.mult))

            def norm(gain, shift):
                own["rs_ready"].next()

                def low(k):
                    own["norm_hi"].next()
                    own["x_ready"].own(V.scalar_tensor_tensor(x_lo[:, k, :], tn[:, k % 2, :], shift[:, k:k + 1],
                                                              x_hi[:, k, :].bitcast(F32), ALU.add, ALU.subtract))

                for k in range(KT):
                    own["normed"].own(V.scalar_tensor_tensor(tn[:, k % 2, :], resid[:, k, :], gain[:, k:k + 1], rs,
                                                             ALU.mult, ALU.mult))
                    if k:
                        low(k - 1)
                low(KT - 1)

            norm(gain1, mod[:, 0:KT])

            zp = [aux[:, 0:TRI], aux[:, 3 * T:3 * T + TRI]]

            def pair_values(p):
                own["vp_ready"].own(V.tensor_copy(vp, v_sb[:, :, bass.ds(p * P, P)]))

            def out_lo(t, p):
                own["osb_hi_ready"].next()
                own["osb_ready"].own(V.tensor_tensor(at_tile(osb_lo, p), bank(t), at_tile(osb_hi, p).bitcast(F32),
                                                     ALU.subtract))
                free(t)

            def qk_low(t, hi, lo, scale):
                own["qk_hi_ready"].next()
                own["qk_ready"].own(V.scalar_tensor_tensor(lo[:], bank(t), scale, hi[:].bitcast(F32), ALU.mult, ALU.subtract))
                free(t)

            def pair(t, first, p, last=False):
                def softplus(h):
                    own["log_ready"].next()
                    step.own(V.scalar_tensor_tensor(sp[h][:], zp[h], 0.0, sp[h][:], ALU.max, ALU.add))

                def keep(h):
                    for n, (part, width) in enumerate(((sp[h][:, 0:2 * T], T), (sp[h][:, TRI_AT[3]:TRI], P))):
                        x = part[:, 0:2 * width].rearrange("p (b n) -> p b n", b=2)[:, :, 0:P]
                        k = sm["keep"].rearrange("p (b n) -> p b n", b=1).broadcast_to([P, 2, P])
                        (own["sp_ready"] if n else step).own(V.tensor_tensor(x, x, k, ALU.mult))

                def low(h):
                    own["sp_hi_ready"].next()
                    own["sp_split"].own(V.tensor_tensor(sp_lo[h][:], sp[h][:], sp_hi[h][:].bitcast(F32), ALU.subtract))

                softplus(0)
                keep(0)
                if not first:
                    out_lo(t, p - 1)
                    t = t + 1
                low(0)
                softplus(1)
                keep(1)
                low(1)
                if last:
                    pair_values(p)
                else:
                    qk_low(t, qt_hi, qt_lo, SC)
                    pair_values(p)
                    qk_low(t + 1, kt_hi, kt_lo, 1.0)

            own["v_ready"].next(8)
            qk_low(At(0), qt_hi, qt_lo, SC)
            qk_low(At(1), kt_hi, kt_lo, 1.0)
            pair(At(2), True, 0)
            with loop(dve, 3, [(step, 8), (own["qk_hi_ready"], 4), (own["qk_ready"], 4), (own["log_ready"], 4),
                               (own["sp_ready"], 4), (own["sp_hi_ready"], 4), (own["sp_split"], 4),
                               (own["osb_hi_ready"], 2), (own["osb_ready"], 2), (own["vp_ready"], 2)]) as i:
                for s in range(2):
                    pair(At(4 + 3 * s, i, 6), False, i * 2 + (1 + s))
            pair(At(22), False, PAIRS - 1, last=True)
            out_lo(At(24), PAIRS - 1)

            with loop(dve, 4, [(own["gate_ready"], 2), (own["msb_ready"], 2)]) as i:
                for n in range(2):
                    u, t = At(U0["sb_out"] + 2 + n, i, 4), At(n, i, 4)
                    own["gate_ready"].next()
                    dve.wait_ge(unit_used, (u + 1).val())
                    own["msb_ready"].own(V.tensor_tensor(at_tile(msb, i * 2 + n), bank(t), gate_t[:, n, :], ALU.mult))
                    free(t)
            own["decay_free"].own(V.memset(pret[:], 0.0))

            def ada_steps(n):
                for _ in range(n):
                    k = own["ada1_loaded"].at.c // 16 % KT
                    own["ada1_loaded"].next(16)
                    own["ada_used"].own(ada(ada1[:], adac, k))

            def rotate(u, dst):
                a, b = bank(At(0)), bank(At(1))
                ada_steps(1)
                dve.wait_ge(unit_used, (u + 1).val())
                step.own(V.tensor_tensor(dst[:, 0, :], a, cos, ALU.mult))
                step.own(V.tensor_tensor(dst[:, 1, :], a, sin, ALU.mult))
                free(At(0))
                ada_steps(1)
                dve.wait_ge(unit_used, (u + 2).val())
                step.own(V.tensor_tensor(sqt[:], b, sin, ALU.mult))
                step.own(V.tensor_tensor(dst[:, 0, :], dst[:, 0, :], sqt[:], ALU.subtract))
                step.own(V.tensor_tensor(sqt[:], b, cos, ALU.mult))
                free(At(1))
                own["qk_rot"].own(V.tensor_tensor(dst[:, 1, :], dst[:, 1, :], sqt[:], ALU.add))

            def square(src, first, last):
                end = own["sq_ready"] if last else step
                if first:
                    end.own(V.tensor_tensor(sqacc[:], src, src, ALU.mult))
                else:
                    step.own(V.tensor_tensor(sqt[:], src, src, ALU.mult))
                    end.own(V.tensor_tensor(sqacc[:], sqacc[:], sqt[:], ALU.add))

            dve.wait_ge(S["tables_loaded"], 16)
            own["tile_done"].skip(PAIRS)
            own["sq_ready"].skip(1)
            with loop(dve, RET_H, [(own["recip_ready"], 1), (own["rs_ready"], 1), (step, 10 + 3 + 6 + 1 + 1 + 16), (own["qk_rot"], 2), (own["ada_used"], 8), (own["ada1_loaded"], 16 * KT),
                                   (own["rsc_done"], 1), (own["rsc_ready"], 1), (own["decay_free"], 1),
                                   (own["oraw_ready"], 4), (own["sq_ready"], 1), (own["root_ready"], 1),
                                   (own["gate_ready"], 4), (own["oprod_ready"], 4), (own["orh_ready"], 4),
                                   (own["or_ready"], 4), (own["ada_ready"], 1), (own["tile_done"], 8)]) as i:
                u0 = At(U0["ret"], i, 16)
                rotate(u0, rq)
                rotate(u0 + 2, rk)
                ada_steps(KT - 4)
                own["rsc_done"].next()
                dve.wait_ge(S["decay_loaded"], i * 16 + 16)
                for j in range(NB):
                    a, w = TRI_AT[j], TRI_W[j]
                    ins = V.tensor_tensor(rsc[:, a:a + w], aux[:, a:a + w], decay[:, 0:w], ALU.mult)
                    (step if j < NB - 1 else own["rsc_ready"]).own(ins)
                V.sem_inc(S["decay_free"], 1)
                own["decay_free"].skip()
                for e in range(RET_VT):
                    own["oraw_ready"].next()
                    square(oraw[:, e, :], e == 0, e == RET_VT - 1)
                for e in range(RET_VT):
                    own["gate_ready"].next()
                    own["oprod_ready"].own(V.tensor_tensor(oraw[:, e, :], oraw[:, e, :], gate_t[:, e % 2, :], ALU.mult))
                    own["orh_ready"].next()
                    own["or_ready"].own(V.tensor_tensor(orl[:, e, :], oraw[:, e, :], orh[:, e, :].bitcast(F32),
                                                        ALU.subtract))
                    if e == 2:
                        invert()
                own["ada_ready"].next()
                step.own(V.tensor_tensor(mod[:, bass.ds(i * KT + 2 * KT, KT)], aux[:, 4 * T:4 * T + KT],
                                         cols[:, bass.ds(i * KT + (C0["b_ada"] + 2 * KT), KT)], ALU.add))
                own["tile_done"].skip(RET_VT)
                take_rs()
                for n in range(KT):
                    if n % 2 == 0:
                        own["tile_done"].next()
                    else:
                        dve.wait_ge(unit_used, (u0 + 12 + n // 2 + 1).val())
                    evict(sqt[:], At(n))
                    step.own(V.tensor_tensor(pret[:, n, :], pret[:, n, :], sqt[:], ALU.add))
            step.own(V.scalar_tensor_tensor(gain2[:], mod[:, 4 * KT:5 * KT], 1.0,
                                            cols[:, C0["g_norm2"]:C0["g_norm2"] + KT], ALU.add, ALU.mult))

            with loop(dve, 2, [(step, 4), (own["gate_ready"], 4), (own["merged_f"], 4), (own["merged_hi"], 4),
                               (own["merged"], 4)]) as i:
                for n in range(4):
                    own["gate_ready"].next()
                    m = mt[:, n % 2, :]
                    step.own(V.tensor_tensor(m, gate_t[:, n % 2, :], at_tile(pret, i * 4 + n), ALU.mult))
                    own["merged_f"].own(V.tensor_tensor(m, m, at_tile(msb, i * 4 + n), ALU.add))
                    own["merged_hi"].next()
                    own["merged"].own(V.tensor_tensor(at_tile(m_lo, i * 4 + n), m,
                                                      at_tile(m_hi, i * 4 + n).bitcast(F32), ALU.subtract))

            def residual(t, k, gate, last=None):
                r = at_tile(resid, k)
                step.own(V.scalar_tensor_tensor(r, bank(t), mod[:, bass.ds(k + gate * KT, 1)], r, ALU.mult, ALU.add))
                free(t)
                step.own(V.tensor_tensor(sqt[:], r, r, ALU.mult))
                step.own(V.tensor_tensor(sqacc[:], sqacc[:], sqt[:], ALU.add))

            step.own(V.memset(sqacc[:], 0.0))
            with loop(dve, 2, [(step, 12)]) as i:
                for n in range(4):
                    dve.wait_ge(unit_used, At(U0["out"] + n + 1, i, 4).val())
                    residual(At(n), i * 4 + n, 2)
            V.sem_inc(S["sq_ready"], 1)
            own["sq_ready"].skip()
            invert()
            norm(gain2, mod[:, 3 * KT:4 * KT])

            with loop(dve, FT // 2, [(own["gate_ready"], 2), (own["hidden_f"], 2), (own["hidden_hi"], 2),
                                     (own["hidden"], 2)]) as i:
                for n in range(2):
                    u, t = At(U0["ff_in"] + 2 * n + 1, i, 4), At(2 * n + 1)
                    own["gate_ready"].next()
                    dve.wait_ge(unit_used, (u + 1).val())
                    own["hidden_f"].own(V.tensor_tensor(ht[:, n, :], bank(t), gate_t[:, n, :], ALU.mult))
                    free(t)
                    own["hidden_hi"].next()
                    own["hidden"].own(V.tensor_tensor(at_tile(h_lo, i * 2 + n), ht[:, n, :],
                                                      at_tile(h_hi, i * 2 + n).bitcast(F32), ALU.subtract))
            step.own(V.memset(sqacc[:], 0.0))
            with loop(dve, 2, [(step, 12), (own["tile_done"], 3)]) as i:
                for n in range(4):
                    if n < 3:
                        own["tile_done"].next()
                    else:
                        dve.wait_ge(unit_used, At(U0["ff_out"] + 12, i, 12).val())
                    residual(At(n), i * 4 + n, 5)
            V.sem_inc(S["sq_ready"], 1)
            own["sq_ready"].skip()
            invert()
            def param(name, k=0, n=1):
                return cols[:, C0[name] + k:C0[name] + k + n]

            def heads(x):
                return x.rearrange("p (h n) -> p h n", h=GDN_H)

            def spread(x):
                return x.rearrange("p (h a) -> p h a", a=1).broadcast_to([P, GDN_H, P])

            def repeat(x):
                return x.rearrange("p (a n) -> p a n", a=1).broadcast_to([P, GDN_H, P])

            def flat(x):
                return x.rearrange("p k n -> p (k n)")

            step.own(V.memset(gb[:], 0.0))
            step.own(V.memset(cin[:, :, 0:CONV_G - 1], 0.0))
            step.own(V.memset(cfin[:, :, 0:CONV_C - 1], 0.0))
            norm_g = [param("norm_g", n * KT, KT) for n in range(6)]

            def next_residual(y, gain, x_gain):
                own["rs_ready"].next()

                def low(k):
                    own["norm_hi"].next()
                    own["x_ready"].own(V.scalar_tensor_tensor(x_lo[:, k, :], resid[:, k, :], x_gain[:, k:k + 1],
                                                              x_hi[:, k, :].bitcast(F32), ALU.mult, ALU.subtract))

                for k in range(KT):
                    if y is None:
                        own["res_ready"].own(V.scalar_tensor_tensor(resid[:, k, :], resid[:, k, :], gain[:, k:k + 1], rs,
                                                                    ALU.mult, ALU.mult))
                    else:
                        step.own(V.scalar_tensor_tensor(y[:, k, :], y[:, k, :], gain[:, k:k + 1], rs, ALU.mult, ALU.mult))
                        own["res_ready"].own(V.tensor_tensor(resid[:, k, :], resid[:, k, :], y[:, k, :], ALU.add))
                    if k:
                        low(k - 1)
                low(KT - 1)
                own["sq_ready"].skip()
                invert()
                take_rs()

            next_residual(None, param("g_final", 0, KT), norm_g[0])
            own["nega_ready"].next()
            step.own(V.tensor_scalar(nega[0:GDN_H, 0:1], nega[0:GDN_H, 0:1], -1.0, None, ALU.mult))
            g0, t0 = At(U0["gdn_in"]), At(T0["gdn_in"])
            evict(tn[:, 1, :], t0, own["glogit_ready"])
            own["ab_ready"].next()
            step.own(V.scalar_tensor_tensor(abx[0:GDN_H, :], abx[0:GDN_H, :], 0.0, abt[0:GDN_H, :], ALU.max, ALU.add))
            own["gb_ready"].own(V.tensor_scalar(gb[0:GDN_H, :], abx[0:GDN_H, :], nega[0:GDN_H, 0:1], None, ALU.mult))

            with loop(dve, 3, [(step, 16), (own["conv_ready"], 4)]) as i:
                for n in range(4):
                    dve.wait_ge(unit_used, At(U0["gdn_in"] + KVQ + n + 1, i, 4).val())
                    evict(cin[:, n % 2, CONV_G - 1:], At(T0["gdn_in"] + KVQ + n, i, 4))
                    dve.wait_ge(S["kvq_ready"], At(n + 1, i, 4).val())
                    y = tn[:, n % 2, :]
                    for j in range(CONV_G):
                        w = cols[:, bass.ds(i * 16 + (C0["gdn_conv"] + n * CONV_G + j), 1)]
                        x = cin[:, n % 2, j:j + T]
                        if j == 0:
                            ins = V.tensor_scalar(y, x, w, None, ALU.mult)
                        else:
                            ins = V.scalar_tensor_tensor(y, x, w, y, ALU.mult, ALU.add)
                        (step if j < CONV_G - 1 else own["conv_ready"]).own(ins)

            dve.wait_ge(S["kvq_ready"], 2 + 12)
            for n in range(GDN_H):
                dve.wait_ge(unit_used, U0["gdn_in"] + GATE + n + 1)
                if n >= 2:
                    own["sgate_ready"].next()
                evict(tn[:, n % 2, :], t0 + GATE + n, own["glogit_ready"])
            own["sgate_ready"].next(2)

            def cfm_in(n):
                u, t = g0 + CFM + 2 * n, t0 + CFM + 2 * n
                dve.wait_ge(unit_used, (u + 1).val())
                evict(gate_t[:, n % 2, :], t, own["glogit_ready"])
                dve.wait_ge(unit_used, (u + 2).val() if n < 3 else U0["gdn_in"] + 28)
                y = cfin[:, n, CONV_C - 1:]
                evict(y, t + 1)
                own["gate_ready"].next()
                own["cfin_ready"].own(V.tensor_tensor(y, y, gate_t[:, n % 2, :], ALU.mult))

            own["groot_ready"].next()
            own["hrecip_ready"].own(V.reciprocal(rcol[:], rcol[:]))
            cfm_in(0)
            own["hs_ready"].next()
            own["k_normed"].own(V.tensor_tensor(flat(kf), flat(kf), aux[:, 0:4 * T], ALU.mult))
            own["gb_turned"].next()
            own["gbt_ready"].own(V.tensor_copy(gbt[:], aux[:, 4 * T:5 * T].rearrange("p (c n) -> p c n", c=NB)[:, :, 0:64]))
            cfm_in(1)
            own["hs_ready"].next()
            own["q_normed"].own(V.scalar_tensor_tensor(flat(qf), flat(qf), P ** -0.5, aux[:, 0:4 * T], ALU.mult, ALU.mult))
            cfm_in(2)
            own["egc_ready"].next()
            own["gc_seen"].own(V.tensor_scalar(ngc[:], aux[:, 4 * T + 32:4 * T + 48], -1.0, None, ALU.mult))
            step.own(V.tensor_tensor(bg.rearrange("p (c h) -> p c h", c=NB), gbt[:, :, 32:36],
                                     egc.rearrange("p (c h) -> p c h", c=NB), ALU.mult))
            cfm_in(3)

            taps = list(DVE_TAPS)

            def cfm_taps(m):
                for _ in range(min(m, len(taps))):
                    n, j = taps.pop(0)
                    if (n, j) == (CFM_T - 1, CFM_SHARED):
                        dve.wait_ge(S["tap_used"], CFM_SHARED - 1)
                    x, w, y = cfin[:, n, j:j + T], param("cfm_conv", n * CONV_C + j), cfy[:, n, :]
                    if j == 0:
                        step.own(V.tensor_scalar(y, x, w, param("cfm_b", n), ALU.mult, ALU.add))
                    else:
                        step.own(V.scalar_tensor_tensor(y, x, w, y, ALU.mult, ALU.add))

            def beta_k(c):
                b = 3 * (c % 2) + 1
                own["beta_row"].next()
                own["kb_ready"].own(V.tensor_tensor(kb[:].rearrange("p (h n) -> p h n", h=GDN_H)[:, :, c * P:(c + 1) * P],
                                                    kf[:, :, c * P:(c + 1) * P], heads(aux[:, b * T:(b + 1) * T]), ALU.mult))

            def lower(c):
                b = 3 * (c % 2) + 2
                own["kk_done"].next()
                own["dec_ready"].next()
                step.own(V.tensor_tensor(bt[:, c, :], aux[:, b * T:(b + 1) * T], dect[:, c, :], ALU.mult))
                step.own(V.tensor_tensor(heads(xt[:, c, :]), heads(bt[:, c, :]), repeat(halves[:, 0, :]), ALU.mult))
                own["xt_ready"].own(V.tensor_tensor(heads(xt[:, c, :]), repeat(sm["ident"]), heads(xt[:, c, :]),
                                                    ALU.subtract))

            beta_k(0)
            beta_k(1)
            for c in range(0, NB, 2):
                lower(c)
                lower(c + 1)
                for d in range(2):
                    if c + d + 2 < NB:
                        beta_k(c + d + 2)
                cfm_taps(2)
            for c in range(NB):
                b = c % 2
                own["kv_turned"].next()
                cc = slice(c * T, (c + 1) * T)
                step.own(V.tensor_tensor(heads(vb[:, cc]), heads(aux[:, b * T:(b + 1) * T]),
                                         spread(gbt[:, c, 32:36]), ALU.mult))
                k = heads(aux[:, (2 + b) * T:(3 + b) * T])
                step.own(V.tensor_tensor(heads(kb[:, cc]), k, spread(bg[:, c * 4:c * 4 + 4]), ALU.mult))
                own["kv_token"].own(V.tensor_tensor(heads(kdec[:, cc]), k,
                                                    heads(dect[:, c, :])[:, :, P - 1:P].broadcast_to([P, GDN_H, P]),
                                                    ALU.mult))

            def level_b(n):
                own["bm_ready"].own(V.tensor_tensor(heads(bm[n % 3]), heads(bt[:, n % NB, :]),
                                                    repeat(halves[:, 1 + n // NB, :]), ALU.mult))

            n_solve = (LEVELS - 1) * NB
            level_b(0)
            level_b(1)
            for n in range(n_solve):
                if n + 2 < n_solve:
                    level_b(n + 2)
                if n == 4:
                    own["egr_ready"].next(NB)
                    step.own(V.tensor_copy(egl.rearrange("p (c h) -> p h c", c=NB),
                                           egr[:, :, P - 1:T:P]))
                    own["qe_ready"].own(V.tensor_tensor(flat(egr[:, :, :]), flat(egr[:, :, :]), flat(qf), ALU.mult))
                cfm_taps(1)
                own["xz_done"].next()
                c, b = n % NB, n % 2
                if n < n_solve - NB:
                    step.own(V.tensor_tensor(xm[:, c, :], xm[:, c, :], aux[:, (2 + b) * T:(3 + b) * T], ALU.subtract))
                own["x_upd"].own(V.tensor_tensor(xt[:, c, :], xt[:, c, :], aux[:, (4 + b) * T:(5 + b) * T], ALU.subtract))

            def within(c):
                own["qk_done"].next()
                own["at_ready"].own(V.tensor_tensor(att[c % 2][:], aux[:, 2 * T:3 * T], dect[:, c, :], ALU.mult))

            within(0)
            for c in range(NB):
                if c + 1 < NB:
                    after, add = state[c % 2], aux[:, 4 * T:5 * T]
                    if c == 0:
                        own["s_done"].next()
                        own["s_ready"].own(V.tensor_copy(after, add))
                    else:
                        if c >= 2:
                            dve.wait_ge(S["o_done"], c)
                        step.own(V.tensor_tensor(heads(after), heads(state[(c + 1) % 2]), spread(egl[:, c * 4:c * 4 + 4]),
                                                 ALU.mult))
                        own["s_done"].next()
                        own["s_ready"].own(V.tensor_tensor(after, after, add, ALU.add))
                    within(c + 1)
                cfm_taps(5)
            cfm_taps(len(taps))
            own["cf_dve"].own(V.memset(egl[:, 0:1], 0.0))

            own["groot_ready"].next()
            own["hrecip_ready"].own(V.reciprocal(rcol[:, 0:16], rcol[:, 0:16]))
            own["cfsum_done"].next()
            for k in range(CFM_T):
                ins = V.scalar_tensor_tensor(cfy[:, k, :], aux[:, 5 * T:6 * T], -1.0 / (CFM_T * P), cfy[:, k, :],
                                             ALU.mult, ALU.add)
                (step if k < CFM_T - 1 else own["cfc_ready"]).own(ins)

            def low(k, src):
                own["norm_hi"].next()
                own["x_ready"].own(V.tensor_tensor(x_lo[:, k, :], src, x_hi[:, k, :].bitcast(F32), ALU.subtract))

            own["hs_ready"].next()
            for k in range(GDN_H):
                if k == 2:
                    invert()
                step.own(V.scalar_tensor_tensor(vf[:, k, :], vf[:, k, :], param("gdn_g"), aux[:, k * T:(k + 1) * T],
                                                ALU.mult, ALU.mult))
                own["on_ready"].own(V.tensor_tensor(vf[:, k, :], vf[:, k, :], sgate[:, k, :], ALU.mult))
                if k:
                    low(k - 1, vf[:, k - 1, :])
            low(GDN_H - 1, vf[:, GDN_H - 1, :])
            own["rs_ready"].next()
            for k in range(CFM_T):
                own["cfn_ready"].own(V.scalar_tensor_tensor(cfy[:, k, :], cfy[:, k, :], param("ln_g", k), rs,
                                                            ALU.mult, ALU.mult))
                if k:
                    low(GDN_H + k - 1, cfy[:, k - 1, :])
            low(KT - 1, cfy[:, CFM_T - 1, :])
            V.sem_inc(S["gdn_over"], 1)

            def sublayer_tile(t, dst):
                step.own(V.tensor_copy(dst, bank(t)))
                free(t)
                step.own(V.tensor_tensor(sqt[:], dst, dst, ALU.mult))
                step.own(V.tensor_tensor(sqacc[:], sqacc[:], sqt[:], ALU.add))

            def end_squares():
                V.sem_inc(S["sq_ready"], 1)
                own["sq_ready"].skip()

            step.own(V.memset(sqacc[:], 0.0))
            for n in range(KT):
                dve.wait_ge(unit_used, U0["mix_out"] + n + 1)
                sublayer_tile(At(T0["mix_out"] + n), yv[:, n, :])
                if n == 3:
                    own["memroot_ready"].next()
                    own["hrecip_ready"].own(V.reciprocal(rcol[:, 0:2], rcol[:, 0:2]))
                elif n == 4:
                    own["hs_ready"].next()
                    for k in range(KT):
                        ins = V.scalar_tensor_tensor(memf[:, k, :], memf[:, k, :], param("mem_g", k),
                                                     aux[:, 4 * T:4 * T + MEM], ALU.mult, ALU.mult)
                        (step if k < KT - 1 else own["memn_ready"]).own(ins)
                elif n == 6:
                    own["mem_hi_ready"].next()
                    own["mem_ready"].own(V.tensor_tensor(mem_lo[:], memf[:], mem_hi[:].bitcast(F32), ALU.subtract))
            end_squares()
            invert()
            next_residual(yv, norm_g[1], norm_g[2])
            for n in range(KT):
                dve.wait_ge(unit_used, U0["xq"] + n + 1)
                evict(qx[:, n, :], At(T0["xq"] + n), own["qx_ready"])

            def row_max(h):
                own["xs_done"].next()
                b = (h % 2) * 2 * T
                step.own(V.tensor_reduce(xcols[:, h % 2, 2, :], aux[:, b:b + 2 * T].rearrange("p (t m) -> p t m", t=NB),
                                         AX.X, ALU.max))
                own["xmax_ready"].own(V.tensor_scalar(xcols[:, h % 2, 0, :], xcols[:, h % 2, 2, :],
                                                      -((KT // XH * P) ** -0.5), None, ALU.mult))

            def normalize(h):
                own["px_ready"].next()
                step.own(V.reciprocal(xcols[:, h % 2, 1, :], xcols[:, h % 2, 1, :]))
                own["pxn_ready"].own(V.tensor_tensor(
                    px[:, h % 2, :, :], px[:, h % 2, :, :],
                    xcols[:, h % 2, 1, :].rearrange("p (t a) -> p t a", a=1).broadcast_to([P, NB, MEM]), ALU.mult))

            def out_low(h):
                for d in range(2):
                    t, k = At(T0["x_val"] + 2 * h + d), 2 * h + d
                    own["xo_hi_ready"].next()
                    own["xo_ready"].own(V.tensor_tensor(xo_lo[:, k, :], bank(t), xo_hi[:, k, :].bitcast(F32), ALU.subtract))
                    free(t)

            own["tile_done"].skip(KT)
            row_max(0)
            row_max(1)
            normalize(0)
            for h in range(XH):
                if h + 1 < XH:
                    normalize(h + 1)
                if h + 2 < XH:
                    row_max(h + 2)
                out_low(h)
            step.own(V.memset(sqacc[:], 0.0))
            for n in range(KT):
                dve.wait_ge(unit_used, U0["xo"] + n + 1)
                sublayer_tile(At(T0["xo"] + n), yv_o[:, n, :])
            end_squares()
            invert()
            step.own(V.memset(fin[:, :, 0:CONV_F - 1], 0.0))
            next_residual(yv_o, norm_g[3], norm_g[4])

            with loop(dve, FT // 2, [(step, 12), (own["conv2_ready"], 4), (own["silu2_ready"], 2),
                                     (own["hidden_f"], 2), (own["hidden_hi"], 2), (own["hidden"], 2)]) as i:
                for n in range(2):
                    for m in range(2):
                        dve.wait_ge(unit_used, At(U0["up"] + 2 * n + m + 1, i, 4).val())
                        evict(fin[:, m, CONV_F - 1:], At(T0["up"] + 2 * n + m, i, 4))
                        y = tn[:, m, :]
                        for j in range(CONV_F):
                            at_ = i * (4 * CONV_F) + (C0["ff_conv"] + (2 * n + m) * CONV_F + j)
                            w, x = cols[:, bass.ds(at_, 1)], fin[:, m, j:j + T]
                            if j == 0:
                                b = cols[:, bass.ds(i * 4 + (C0["ff_conv_b"] + 2 * n + m), 1)]
                                ins = V.tensor_scalar(y, x, w, b, ALU.mult, ALU.add)
                            else:
                                ins = V.scalar_tensor_tensor(y, x, w, y, ALU.mult, ALU.add)
                            (step if j < CONV_F - 1 else own["conv2_ready"]).own(ins)
                    own["silu2_ready"].next()
                    own["hidden_f"].own(V.tensor_tensor(ht2[:], tn[:, 0, :], tn[:, 1, :], ALU.mult))
                    own["hidden_hi"].next()
                    own["hidden"].own(V.tensor_tensor(at_tile(g_lo, i * 2 + n), ht2[:], at_tile(g_hi, i * 2 + n).bitcast(F32),
                                                      ALU.subtract))
            step.own(V.memset(sqacc[:], 0.0))
            with loop(dve, 2, [(step, 12), (own["tile_done"], 3)]) as i:
                for n in range(4):
                    if n < 3:
                        own["tile_done"].next()
                    else:
                        dve.wait_ge(unit_used, At(U0["down"] + 12, i, 12).val())
                    sublayer_tile(At(T0["down"] + n, i, 4), at_tile(yv2, i * 4 + n))
            end_squares()
            invert()
            own["rs_ready"].next()
            for k in range(KT):
                step.own(V.scalar_tensor_tensor(yv2[:, k, :], yv2[:, k, :], norm_g[5][:, k:k + 1], rs, ALU.mult, ALU.mult))
                own["resid_ready"].own(V.tensor_tensor(resid[:, k, :], resid[:, k, :], yv2[:, k, :], ALU.add))

        @block.tensor
        def _(pe):
            own = {n: Count(pe, S[n]) for n in S}
            M = nc.tensor.matmul
            ones = small[:, SM0["ones"]:SM0["ones"] + P]
            ident = small[:, SM0["ident"]:SM0["ident"] + P]

            def wait_bank(t):
                if t.i is not None or t.c >= 2:
                    pe.wait_ge(acc_free[t.slot(2)], t.div(2).val())

            def weights(u):
                pe.wait_ge(lo_ready, (u + 1).val())
                return w_hi[u.slot(RING)], w_lo[u.slot(RING)]

            def three(out, a_hi, a_lo, b_hi, b_lo, first, last):
                M(out, a_hi, b_hi, start=first, stop=False)
                M(out, a_hi, b_lo, start=False, stop=False)
                return M(out, a_lo, b_hi, start=False, stop=last)

            def wt(w, k):
                return w[:, k * P:(k + 1) * P]

            def pair_tiles(u, t, hi, lo, ready):
                wait_bank(t)
                wait_bank(t + 1)
                w = [weights(u), weights(u + 1)]
                for k in range(KT):
                    ready.next()
                    for j, (wh, wl) in enumerate(w):
                        m = three(bank(t + j), wt(wh, k), wt(wl, k), hi[:, k, :], lo[:, k, :], k == 0, k == KT - 1)
                        if k == KT - 1:
                            m.then_inc(unit_used, 1)

            def lead(phase, t0, hi, lo, ready, between=None):
                u, t = At(U0[phase]), At(t0)
                pair_tiles(u, t, hi, lo, ready)
                if between:
                    between()
                tile(u + 2, t + 2, hi, lo)
                tile(u + 3, t + 3, hi, lo)

            def tile(u, t, hi, lo, width=T, extra=0):
                wait_bank(t)
                wh, wl = weights(u)
                for k in range(KT):
                    if extra and k == KT - 1:
                        weights(u + extra)
                    m = three(bank(t)[:, 0:width], wt(wh, k), wt(wl, k), hi[:, k, :], lo[:, k, :], k == 0, k == KT - 1)
                m.then_inc(unit_used, 1 + extra)

            def token_tiles(u, banks, hi=x_hi, lo=x_lo, ready=None):
                for j in range(4):
                    wh, wl = weights(u + j)
                    for kk in range(2):
                        k = 2 * j + kk
                        if ready:
                            ready.next()
                        for b, bk in enumerate(banks):
                            m = three(aux[:, bk * T:(bk + 1) * T],
                                      hi[:, k, b * P:(b + 1) * P], lo[:, k, b * P:(b + 1) * P],
                                      wh[:, kk * T:(kk + 1) * T], wl[:, kk * T:(kk + 1) * T], k == 0, k == KT - 1)
                    m.then_inc(unit_used, 1)

            def column_sums(at_, sources, blocks=NB):
                for k, src in enumerate(sources):
                    for b in range(blocks):
                        m = M(aux[:, at_ + b:at_ + b + 1], src[:, b * P:(b + 1) * P], ones[:, 0:1],
                              start=k == 0 and b == 0, stop=k == len(sources) - 1, skip_group_check=True)
                return m

            def spread(at_, col, blocks=NB):
                for b in range(blocks):
                    m = M(aux[:, at_ + b * P:at_ + (b + 1) * P], rcol[:, col + b:col + b + 1].broadcast_to([P, P]), ident,
                          start=True, stop=True)
                return m

            def stat(sources=None):
                if sources is None:
                    own["sq_ready"].next()
                column_sums(5 * T, sources or [sqacc]).then_inc(S["stat_ready"], 1)

            def spread_rs():
                own["recip_ready"].next()
                spread(5 * T, 0).then_inc(S["rs_ready"], 1)

            def stat_spread():
                stat()
                spread_rs()

            def modulation(src, m=0):
                for n in range(KT):
                    at_ = 4 * T + m * KT + n
                    ins = M(aux[:, at_:at_ + 1], src[:, n * P:(n + 1) * P], ones[:, 0:1], start=True, stop=True)
                ins.then_inc(S["ada_ready"], 1)

            pe.wait_ge(S["consts_loaded"], 48)
            own["ada_used"].next(KT)
            modulation(adac0[:, 0, :])
            stat()
            spread_rs()
            own["ada_used"].next(KT)
            modulation(adac0[:, 1, :], 1)
            token_tiles(At(0), (0, 1, 2, 3), ready=own["x_ready"])
            own["v_ready"].next(2)
            token_tiles(At(4), (4, 5, 0, 1))

            tile(At(8), At(0), x_hi, x_lo)
            tile(At(9), At(1), x_hi, x_lo)
            own["v_ready"].next(6)
            own["consts_ready"].next(6)
            zp = [aux[:, 0:TRI], aux[:, 3 * T:3 * T + TRI]]

            def values(t):
                wait_bank(t)
                own["vp_ready"].next()
                for h in range(2):
                    r = slice(h * SB_DIM, (h + 1) * SB_DIM)
                    for j in range(NB):
                        a, w = TRI_AT[j], TRI_W[j]
                        m = M(bank(t)[r, j * P:T], vp[:, j, r], prob[h][:, a:a + w], start=j == 0, stop=j == NB - 1)
                m.then_inc(S["tile_done"], 1)

            def log_a(h):
                own["sp_split"].next()
                for j in TRI_ORDER:
                    a, w = TRI_AT[j], TRI_W[j]
                    for part in (sp_hi[h], sp_lo[h]):
                        M(zp[h][:, a:a + w], negtri_r[:], part[:, a:a + w], start=False, stop=False, skip_group_check=True)
                        for l in range(j + 1, NB):
                            b, v = TRI_AT[l], TRI_W[l]
                            M(zp[h][:, a + w - v:a + w], negone_r[:], part[:, b:b + v],
                              start=False, stop=False, skip_group_check=True)
                    m = M(zp[h][:, a:a + P], ident_b[:], mask_b[:], start=False, stop=True, skip_group_check=True)
                m.then_inc(S["log_a_ready"], 1)

            gate0 = At(U0["sb_out"])

            def pair(u, t, first, last):
                own["qk_ready"].next(2)
                for h in range(2):
                    if not first:
                        own["prob_ready"].next()
                    r = slice(h * SB_DIM, (h + 1) * SB_DIM)
                    for j in TRI_ORDER:
                        a, w = TRI_AT[j], TRI_W[j]
                        for n, (k, q) in enumerate(((kt_hi, qt_hi), (kt_hi, qt_lo), (kt_lo, qt_hi))):
                            m = M(zp[h][:, a:a + w], k[r, j * P:(j + 1) * P], q[r, j * P:T], start=n == 0 and j != 3,
                                  stop=n == 2, skip_group_check=True)
                    m.then_inc(S["z_ready"], 1)
                if not first:
                    values(t)
                    t = t + 1
                if last:
                    tile(gate0, t, x_hi, x_lo)
                else:
                    tile(u, t, x_hi, x_lo)
                log_a(0)
                if not last:
                    tile(u + 1, t + 1, x_hi, x_lo)
                log_a(1)

            pair(At(10), At(2), True, False)
            with loop(pe, 3, [(own["qk_ready"], 4), (own["vp_ready"], 2), (own["prob_ready"], 4),
                              (own["sp_split"], 4)]) as i:
                for s in range(2):
                    pair(At(U0["sb_qk"] + 4 + 2 * s, i, 4), At(4 + 3 * s, i, 6), False, False)
            pair(None, At(22), False, True)
            own["prob_ready"].next(2)
            values(At(24))

            tile(gate0 + 1, At(25), x_hi, x_lo)
            own["osb_ready"].next(PAIRS)
            for n in range(2, 4):
                tile(gate0 + n, At(24 + n), osb_hi, osb_lo)
            with pe.Fori(0, 3) as i:
                for n in range(4):
                    tile(At(U0["sb_out"] + 4 + n, i, 4), At(28 + n, i, 4), *((x_hi, x_lo) if n < 2 else (osb_hi, osb_lo)))

            t_ret = 24 + 16
            pe.wait_ge(S["msb_ready"], KT)
            with loop(pe, RET_H, [(own["qk_rot"], 2), (own["rv_ready"], 4), (own["rsc_ready"], 1), (own["sq_ready"], 1), (own["recip_ready"], 1),
                                  (own["ada_used"], 8), (own["or_ready"], 4)]) as i:
                u0, t0 = At(U0["ret"], i, 16), At(t_ret, i, 20)
                for n in range(4):
                    tile(u0 + n, t0 + n, x_hi, x_lo)
                token_tiles(u0 + 4, (2, 3, 4, 5))
                tile(u0 + 8, t0 + 4, x_hi, x_lo)
                own["qk_rot"].next(2)
                own["rv_ready"].next(4)
                for j in TRI_ORDER:
                    a, w = TRI_AT[j], TRI_W[j]
                    for k in range(RET_QT):
                        m = M(aux[:, a:a + w], rk[:, k, j * P:(j + 1) * P], rq[:, k, j * P:T],
                              start=k == 0 and j != 3, stop=k == RET_QT - 1, skip_group_check=True)
                m.then_inc(S["rsc_done"], 1)
                tile(u0 + 9, t0 + 5, x_hi, x_lo)
                own["rsc_ready"].next()
                for e in range(RET_VT):
                    t = t0 + 6 + e
                    wait_bank(t)
                    for j in range(NB):
                        a, w = TRI_AT[j], TRI_W[j]
                        m = M(bank(t)[:, j * P:T], rv[:, j, e * P:(e + 1) * P], rsc[:, a:a + w],
                              start=j == 0, stop=j == NB - 1)
                    m.then_inc(S["tile_done"], 1)
                tile(u0 + 10, t0 + 10, x_hi, x_lo)
                stat()
                tile(u0 + 11, t0 + 11, x_hi, x_lo)
                own["ada_used"].next(KT)
                modulation(adac)
                spread_rs()

                def project(n, e):
                    wh, wl = weights(u0 + 12 + n // 2)
                    at_, t = (n % 2) * RET_VT + e, t0 + 12 + n
                    m = three(bank(t), wt(wh, at_), wt(wl, at_), orh[:, e, :], orl[:, e, :], e == 0, e == RET_VT - 1)
                    if e == RET_VT - 1:
                        m.then_inc(unit_used if n % 2 else S["tile_done"], 1)

                wait_bank(t0 + 12)
                wait_bank(t0 + 13)
                for e in range(RET_VT):
                    own["or_ready"].next()
                    project(0, e)
                    project(1, e)
                for n in range(2, KT):
                    wait_bank(t0 + 12 + n)
                    for e in range(RET_VT):
                        project(n, e)

            def tiles(phase, n, t0, hi, lo, first=0):
                with pe.Fori(0, (n - first) // 4) as i:
                    for k in range(4):
                        tile(At(U0[phase] + first + k, i, 4), At(t0 + first + k, i, 4), hi, lo)

            tiles("merge", KT, t_ret + 80, x_hi, x_lo)
            lead("out", t_ret + 88, m_hi, m_lo, own["merged"])
            tiles("out", KT, t_ret + 88, m_hi, m_lo, first=4)
            stat_spread()
            lead("ff_in", t_ret + 96, x_hi, x_lo, own["x_ready"])
            tiles("ff_in", 2 * FT, t_ret + 96, x_hi, x_lo, first=4)

            def down(phase, t0, hi, lo):
                own["hidden"].next(FT - 2)
                done = own["hidden"].at
                own["hidden"].skip(2)
                with pe.Fori(0, 2) as i:
                    for n in range(4):
                        t = At(t0 + n, i, 4)
                        wait_bank(t)
                        for k in range(FT):
                            if n == 0 and k >= FT - 2:
                                pe.wait_ge(S["hidden"], (done + (k + 3 - FT)).val())
                            at_ = n * FT + k
                            u = At(U0[phase] + at_ // KT, i, 12)
                            if at_ % KT == 0 or k == 0:
                                wh, wl = weights(u)
                            m = three(bank(t), wt(wh, at_ % KT), wt(wl, at_ % KT), hi[:, k, :], lo[:, k, :],
                                      k == 0, k == FT - 1)
                            if at_ == 4 * FT - 1:
                                weights(u + 1)
                                m.then_inc(unit_used, 2)
                            elif at_ % KT == KT - 1:
                                m.then_inc(unit_used, 1)
                            elif k == FT - 1:
                                m.then_inc(S["tile_done"], 1)

            down("ff_out", t_ret + 96 + 2 * FT, h_hi, h_lo)
            stat_spread()
            g0, t0 = At(U0["gdn_in"]), At(T0["gdn_in"])
            tri = small[:, SM0["tri"]:SM0["tri"] + P]
            lead("gdn_in", T0["gdn_in"], x_hi, x_lo, own["x_ready"], stat_spread)
            tile(g0 + 4, t0 + 4, x_hi, x_lo)
            with pe.Fori(0, 2) as i:
                for n in range(4):
                    tile(At(U0["gdn_in"] + KVQ + 4 + n, i, 4), At(T0["gdn_in"] + KVQ + 4 + n, i, 4), x_hi, x_lo)
            for n in range(GDN_H):
                tile(g0 + GATE + n, t0 + GATE + n, x_hi, x_lo)

            def head_sums(at_, src):
                for h in range(GDN_H):
                    m = column_sums(at_ + h * NB, [src[:, h * T:(h + 1) * T]])
                return m

            def head_spread(col):
                for h in range(GDN_H):
                    m = spread(h * T, col + h * NB)
                m.then_inc(S["hs_ready"], 1)

            def cfm_pair(n):
                tile(g0 + CFM + 2 * n, t0 + CFM + 2 * n, x_hi, x_lo)
                if n < 3:
                    tile(g0 + CFM + 2 * n + 1, t0 + CFM + 2 * n + 1, x_hi, x_lo)
                else:
                    tile(g0 + CFM + 7, t0 + CFM + 7, x_hi, x_lo, extra=3)

            own["gsq_ready"].next(2)
            head_sums(4 * T, kdec)
            head_sums(4 * T + 16, vb).then_inc(S["gstat_done"], 1)
            cfm_pair(0)
            own["hrecip_ready"].next()
            head_spread(0)
            own["gb_ready"].next()
            for c in range(NB):
                m = nc.tensor.transpose(aux[:, 4 * T + c * P:4 * T + (c + 1) * P], gb[:, c * P:(c + 1) * P], ident)
            m.then_inc(S["gb_turned"], 1)
            cfm_pair(1)
            own["k_normed"].next()
            head_spread(16)
            own["gbt_ready"].next()
            M(aux[:, 4 * T + 32:4 * T + 48], tri, gbt[:, :, 0:GDN_H], start=True, stop=True).then_inc(S["gc_done"], 1)
            cfm_pair(2)
            cfm_pair(3)

            def rows(c):
                b = 3 * (c % 2)
                for h in range(GDN_H):
                    m = M(aux[:, b * T + h * P:b * T + (h + 1) * P], gbt[:, c, h:h + 1].broadcast_to([P, P]), tri,
                          start=h == 0, stop=True, skip_group_check=True)
                m.then_inc(S["gc_row"], 1)
                for h in range(GDN_H):
                    m = M(aux[:, (b + 1) * T + h * P:(b + 1) * T + (h + 1) * P],
                          gbt[:, c, 32 + h:33 + h].broadcast_to([P, P]), ident, start=True, stop=True)
                m.then_inc(S["beta_row"], 1)

            own["q_normed"].next()
            own["gc_seen"].next()
            rows(0)
            rows(1)
            def lower(c):
                b = 3 * (c % 2)
                own["egr_ready"].next()
                for h in range(GDN_H):
                    m = M(aux[:, b * T + h * P:b * T + (h + 1) * P], ident_b[:], causal_b[:], start=False, stop=True,
                          skip_group_check=True)
                m.then_inc(S["gc_masked"], 1)
                own["kb_ready"].next()
                for h in range(GDN_H):
                    at_ = slice(h * T + c * P, h * T + (c + 1) * P)
                    m = M(aux[:, (b + 2) * T + h * P:(b + 2) * T + (h + 1) * P], kf[:, h, c * P:(c + 1) * P], kb[:, at_],
                          start=True, stop=True)
                m.then_inc(S["kk_done"], 1)

            def turn(c):
                t = At(T0["turn"] + c)
                wait_bank(t)
                for h in range(GDN_H):
                    m = nc.tensor.transpose(bank(t)[:, h * P:(h + 1) * P], xt[:, c, h * P:(h + 1) * P], ident)
                m.then_inc(S["x_turned"], 1)

            for c in range(0, NB, 2):
                lower(c)
                lower(c + 1)
                for d in range(2):
                    own["xt_ready"].next()
                    if c + d + 2 < NB:
                        rows(c + d + 2)
                    turn(c + d)

            for c in range(NB):
                b = c % 2
                if c >= 2:
                    own["kv_token"].next()
                for src, bk in ((vf, b), (kf, 2 + b)):
                    for h in range(GDN_H):
                        m = nc.tensor.transpose(aux[:, bk * T + h * P:bk * T + (h + 1) * P],
                                                src[:, h, c * P:(c + 1) * P], ident)
                m.then_inc(S["kv_turned"], 1)

            def each(bk, lhs, rhs):
                for h in range(GDN_H):
                    hh = slice(h * P, (h + 1) * P)
                    m = M(aux[:, bk * T + h * P:bk * T + (h + 1) * P], lhs[:, hh], rhs[:, hh], start=True, stop=True)
                return m

            n_solve = (LEVELS - 1) * NB
            own["kv_token"].next(2)

            def update(n):
                c, b = n % NB, n % 2
                own["zs_ready"].next()
                if n >= 2:
                    own["x_upd"].next()
                if n < n_solve - NB:
                    each(2 + b, xt[:, c, :], solve[:, b, :])
                each(4 + b, solve[:, b, :], xt[:, c, :]).then_inc(S["xz_done"], 1)

            for n in range(n_solve):
                if n < NB:
                    own["x_first"].next()
                else:
                    pe.wait_ge(S["x_upd"], n - NB + 1)
                own["bm_ready"].next()
                each(n % 2, bm[n % 3], xm[:, n % NB, :]).then_inc(S["zz_done"], 1)
                if n:
                    update(n - 1)
            update(n_solve - 1)
            own["x_upd"].next(2)
            own["qe_ready"].next()

            def within(c):
                if c:
                    own["at_ready"].next()
                for h in range(GDN_H):
                    m = M(aux[:, 2 * T + h * P:2 * T + (h + 1) * P], kf[:, h, c * P:(c + 1) * P],
                          qf[:, h, c * P:(c + 1) * P], start=True, stop=True)
                m.then_inc(S["qk_done"], 1)

            def w_turned(c):
                each(0, kb[:, c * T:(c + 1) * T], xt[:, c, :]).then_inc(S["wt_done"], 1)

            within(0)
            for c in range(NB):
                vn, before = solve[:, 2 + c % 2, :], state[(c + 1) % 2]
                for h in range(GDN_H):
                    hh = slice(h * P, (h + 1) * P)
                    m = M(aux[:, T + h * P:T + (h + 1) * P], xt[:, c, hh], vb[:, c * T + h * P:c * T + (h + 1) * P],
                          start=h == 0, stop=c == 0, skip_group_check=True)
                if c:
                    own["nwt_ready"].next()
                    own["s_ready"].next()
                    for h in range(GDN_H):
                        hh = slice(h * P, (h + 1) * P)
                        m = M(aux[:, T + h * P:T + (h + 1) * P], solve[:, c % 2, hh], before[:, hh], start=False, stop=True,
                              skip_group_check=True)
                m.then_inc(S["vnew_done"], 1)
                if c + 1 < NB:
                    w_turned(c + 1)
                own["vnew_ready"].next()
                if c + 1 < NB:
                    each(4, kdec[:, c * T:(c + 1) * T], vn).then_inc(S["s_done"], 1)
                pe.wait_ge(S["at_ready"], c + 1)
                if c:
                    pe.wait_ge(S["o_ready"], c)
                for h in range(GDN_H):
                    hh, out = slice(h * P, (h + 1) * P), aux[:, 3 * T + h * P:3 * T + (h + 1) * P]
                    m = M(out, vn[:, hh], att[c % 2][:, hh], start=True, stop=c == 0)
                    if c:
                        m = M(out, before[:, hh], egr[:, h, c * P:(c + 1) * P], start=False, stop=True)
                m.then_inc(S["o_done"], 1)
                if c + 1 < NB:
                    within(c + 1)

            own["osq_ready"].next()
            head_sums(4 * T, kdec).then_inc(S["ostat_done"], 1)
            own["cf_dve"].next()
            own["cf_pool"].next()
            for k in range(CFM_T):
                m = M(rs, ones, cfy[:, k, :], start=k == 0, stop=k == CFM_T - 1)
            m.then_inc(S["cfsum_done"], 1)
            own["hrecip_ready"].next()
            head_spread(0)
            own["cfsq_ready"].next()
            stat([kb[:, k * T:(k + 1) * T] for k in range(CFM_T)])
            spread_rs()
            u, t = At(U0["mix_out"]), At(T0["mix_out"])
            pair_tiles(u, t, x_hi, x_lo, own["x_ready"])
            tile(u + 2, t + 2, x_hi, x_lo)
            own["memsq_ready"].next()
            column_sums(4 * T, [msq[:, k * MEM:(k + 1) * MEM] for k in range(KT)], 2).then_inc(S["memstat_done"], 1)
            tile(u + 3, t + 3, x_hi, x_lo)
            own["hrecip_ready"].next()
            spread(4 * T, 0, 2).then_inc(S["hs_ready"], 1)
            for n in range(4, 8):
                tile(u + n, t + n, x_hi, x_lo)
            stat()
            own["mem_ready"].next()
            for n in range(KT):
                tile(At(U0["kv"] + n), At(T0["kv"] + n), mem_hi, mem_lo, width=MEM)
                if n == 0:
                    spread_rs()
            token_tiles(At(U0["kv"] + 8), (0, 1), mem_hi, mem_lo)
            stat()
            token_tiles(At(U0["kv"] + 12), (2, 3), mem_hi, mem_lo)
            spread_rs()
            own["x_ready"].next(KT)
            tiles("xq", KT, T0["xq"], x_hi, x_lo)

            own["km_ready"].next(KT)
            own["vm_ready"].next(4)
            own["qx_ready"].next(KT)

            def scores(h):
                if h >= 2:
                    own["px_ready"].next()
                b = (h % 2) * 2 * T
                for t in range(NB):
                    for k in range(2):
                        m = M(aux[:, b + t * MEM:b + (t + 1) * MEM], qx[:, 2 * h + k, t * P:(t + 1) * P],
                              kmt[:, 2 * h + k, :], start=k == 0, stop=k == 1)
                m.then_inc(S["xs_done"], 1)

            def attend(h):
                own["pxn_ready"].next()
                if h:
                    pe.wait_ge(S["pxt_ready"], h)
                for mt_ in range(2):
                    for t in range(NB):
                        m = nc.tensor.transpose(aux[:, (4 + mt_) * T + t * P:(4 + mt_) * T + (t + 1) * P],
                                                px[:, h % 2, t, mt_ * P:(mt_ + 1) * P], ident)
                m.then_inc(S["px_turned"], 1)
                own["pxt_ready"].next()
                for d in range(2):
                    t, k = At(T0["x_val"] + 2 * h + d), 2 * h + d
                    wait_bank(t)
                    for mt_ in range(2):
                        m = M(bank(t), vm[:, mt_, k * P:(k + 1) * P], pxt[:, h % 2, mt_ * T:(mt_ + 1) * T],
                              start=mt_ == 0, stop=mt_ == 1)
                    m.then_inc(S["tile_done"], 1)

            scores(0)
            scores(1)
            for h in range(XH):
                attend(h)
                if h + 2 < XH:
                    scores(h + 2)
            lead("xo", T0["xo"], xo_hi, xo_lo, own["xo_ready"])
            tiles("xo", KT, T0["xo"], xo_hi, xo_lo, first=4)
            stat_spread()
            lead("up", T0["up"], x_hi, x_lo, own["x_ready"], stat_spread)
            tiles("up", 2 * FT, T0["up"], x_hi, x_lo, first=4)
            down("down", T0["down"], g_hi, g_lo)
            stat_spread()



def feature_units(w):
    k, n = w.shape
    return w.reshape(k // P, P, n // P, P).transpose(2, 1, 0, 3).reshape(n // P, P, k)


def token_units(w):
    k, n = w.shape
    return w.reshape(k // (2 * P), 2, P, n // T, T).transpose(3, 0, 2, 1, 4).reshape(-1, P, UNIT)


def zeros(n):
    return np.zeros((n, P, UNIT), np.float32)


def interleave(*parts):
    return np.stack(parts, 1).reshape(-1, P, UNIT)


def two_by_two(a, b):
    return np.stack([a.reshape(-1, 2, P, UNIT), b.reshape(-1, 2, P, UNIT)], 1).reshape(-1, P, UNIT)


def down_units(w):
    f = w.reshape(FT, P, KT, P).transpose(2, 0, 1, 3).reshape(2, 4 * FT // KT, KT, P, P).transpose(0, 1, 3, 2, 4)
    f = f.reshape(2, 4 * FT // KT, P, UNIT)
    return np.concatenate([f, np.zeros((2, 1, P, UNIT), np.float32)], 1).reshape(-1, P, UNIT)


def gdn_units(w):
    g = GDN_H * P
    q, k, v, gate = [w[:, n * g:(n + 1) * g] for n in range(4)]
    a, b, cfm = w[:, 4 * g:4 * g + 4], w[:, 4 * g + 4:4 * g + 8], w[:, 4 * g + 8:]
    ab = np.concatenate([a, np.zeros((D, 28), w.dtype), b, np.zeros((D, P - 36), w.dtype)], axis=1)
    half = CFM_T * P
    return np.concatenate([
        feature_units(ab), feature_units(k), feature_units(v), feature_units(q), feature_units(gate),
        interleave(feature_units(cfm[:, half:]), feature_units(cfm[:, :half])), zeros(3),
    ])


def tap_columns(w):
    return w.reshape(w.shape[0], -1, P).transpose(2, 1, 0).reshape(P, -1)


def few(v):
    return np.concatenate([v, np.zeros(P - len(v), v.dtype)])[:, None]


def halves_in_turn(v):
    return np.moveaxis(v.reshape(v.shape[:-1] + (2, FT, P)), -3, -2).reshape(v.shape)


def columns(v):
    return v.reshape(-1, P).T


def weight_stream(i):
    w_in = i["w_in"][0]
    sw, qw, vw = D, RET_H * RET_QT * P, RET_H * RET_VT * P
    cut = np.cumsum([0, sw, sw, sw, qw, qw, vw, vw, D, D])
    sq, sk, sv, rq, rk, rv, rg, b_sb, b_ret = [w_in[:, a:b] for a, b in zip(cut[:-1], cut[1:])]
    heads = []
    proj = i["w_proj_ret"][0].reshape(RET_H, RET_VT, P, KT // 2, 2, P).transpose(0, 3, 2, 4, 1, 5)
    for h in range(RET_H):
        q = slice(h * RET_QT * P, (h + 1) * RET_QT * P)
        v = slice(h * RET_VT * P, (h + 1) * RET_VT * P)
        heads += [feature_units(rq[:, q]), feature_units(rk[:, q]), token_units(rv[:, v]), feature_units(rg[:, v]),
                  proj[h].reshape(KT // 2, P, UNIT)]
    ff = i["w_ffn_in"][0]
    return {
        "sb_v": token_units(sv),
        "sb_qk": interleave(feature_units(sq), feature_units(sk)),
        "sb_out": two_by_two(feature_units(b_sb), feature_units(i["w_proj_sb"][0])),
        "ret": np.concatenate(heads),
        "merge": feature_units(b_ret),
        "out": feature_units(i["w_out"][0]),
        "ff_in": interleave(feature_units(ff[:, :D_FF]), feature_units(ff[:, D_FF:])),
        "ff_out": down_units(i["w_ffn_out"][0]),
        "gdn_in": gdn_units(i["w_in_2"][0]),
        "mix_out": feature_units(i["w_out_2"][0]),
        "kv": np.concatenate([feature_units(i["xa_w_kv_2"][0][:, :D]), token_units(i["xa_w_kv_2"][0][:, D:])]),
        "xq": feature_units(i["xa_w_q_2"][0]),
        "xo": feature_units(i["xa_w_o_2"][0]),
        "up": interleave(feature_units(i["ffn_w_up_2"][0][:, :D_FF]), feature_units(i["ffn_w_up_2"][0][:, D_FF:])),
        "down": down_units(i["ffn_w_down_2"][0]),
    }


def parameter_columns(i):
    return {
        "c": columns(i["c"][0]), "b_ada": columns(i["b_ada"][0]), "g_norm1": columns(i["g_norm1"][0]),
        "b_branch": columns(i["b_branch"][0]), "g_norm2": columns(i["g_norm2"][0]), "g_final": columns(i["g_final"]),
        "norm_g": columns(i["norm_g_2"][0].reshape(-1)), "mem_g": columns(i["mem_norm_g_2"][0]),
        "gdn_conv": tap_columns(np.concatenate(
            [i["gdn_conv_w_2"][0][:, n * GDN_H * P:(n + 1) * GDN_H * P] for n in (1, 2, 0)], axis=1)),
        "cfm_conv": tap_columns(i["cfm_dw_w_2"][0]), "cfm_b": columns(i["cfm_dw_b_2"][0]),
        "ln_g": columns(i["cfm_ln_g_2"][0]), "ln_b": columns(i["cfm_ln_b_2"][0]), "gdn_g": columns(i["gdn_norm_g_2"][0]),
        "a_log": few(i["gdn_a_log_2"][0]), "dt_bias": few(i["gdn_dt_bias_2"][0]),
        "ff_conv": tap_columns(halves_in_turn(i["ffn_conv_w_2"][0])),
        "ff_conv_b": columns(halves_in_turn(i["ffn_conv_b_2"][0])),
    }


def laid_out(i):
    stream, params = weight_stream(i), parameter_columns(i)
    assert [(n, len(stream[n])) for n, _ in PHASES] == PHASES
    assert [(n, params[n].shape[1]) for n, _ in COLS] == COLS
    tables, small, halves = shape_tables()
    ada = i["w_ada"][0].reshape(KT, P, N_MOD, D).transpose(2, 0, 1, 3).reshape(-1, P, UNIT)
    x = i["x"][0].T.reshape(KT, P, T).transpose(1, 0, 2)
    arrays = {
        "weights": np.concatenate([stream[n] for n, _ in PHASES]), "ada": ada,
        "cols": np.concatenate([params[n] for n, _ in COLS], 1), "small": small, "tables": tables, "x": x,
        "halves": halves.reshape(P, LEVELS, P), "mem": i["mem_2"][0].T.reshape(KT, P, MEM).transpose(1, 0, 2),
    }
    return {n: np.ascontiguousarray(a) for n, a in arrays.items()}


def kernel(**inputs):
    import concourse.bacc as bacc
    from concourse.bass_utils import run_bass_kernel_spmd as run

    nc = bacc.Bacc("TRN2", target_bir_lowering=False, num_devices=1)
    arrays = laid_out({n: np.asarray(a) for n, a in inputs.items()})
    dram = {n: nc.dram_tensor(f"in_{n}", a.shape, mybir.dt.from_np(a.dtype), kind="ExternalInput").ap()
            for n, a in arrays.items()}
    dram["out"] = nc.dram_tensor("out", (P, KT, T), F32, kind="ExternalOutput").ap()
    build_program(nc, dram)
    r = run(nc, [{f"in_{n}": a for n, a in arrays.items()}], core_ids=[0])
    out = r.results[0]["out"]
    return out.transpose(2, 1, 0).reshape(1, T, D)
```
